# Optimizing a Trainium2 kernel written in Bass

```python
import jax, jax.numpy as jnp
from jax import lax
import numpy as np

D_MODEL = 1024
BATCH = 1
SEQ = 256
DEPTH = 2

MEM_LEN = 256
HEAD_DIM = 64
N_SB_HEADS = 8
N_FOX_HEADS = 8
N_MEM_HEADS = 4
MEM_HEAD_DIM = 128
SB_W = N_SB_HEADS * HEAD_DIM
FOX_W = N_FOX_HEADS * HEAD_DIM
MEM_W = N_MEM_HEADS * MEM_HEAD_DIM
N_BRANCH = 3
IN_W = 3 * SB_W + 3 * FOX_W + N_FOX_HEADS + MEM_W
D_FF = ((8 * D_MODEL // 3 + 127) // 128) * 128
Q_BLOCK = 128
RMS_EPS = 1e-6


def _rmsnorm(t, g):
    t32 = t.astype(jnp.float32)
    t32 = t32 * lax.rsqrt(jnp.mean(t32 * t32, axis=-1, keepdims=True) + RMS_EPS)
    return t32.astype(t.dtype) * g

def _swiglu(t, w_gate, w_up, w_down):
    return (jax.nn.silu(t @ w_gate) * (t @ w_up)) @ w_down

def _split_heads(t, n_heads):
    b, s, _ = t.shape
    return t.reshape(b, s, n_heads, -1).transpose(0, 2, 1, 3)

def _merge_heads(t):
    b, h, s, d = t.shape
    return t.transpose(0, 2, 1, 3).reshape(b, s, h * d)

def _query_blocks(t):
    b, h, s = t.shape[:3]
    t = t.reshape((b, h, s // Q_BLOCK, Q_BLOCK) + t.shape[3:])
    return jnp.moveaxis(t, 2, 0)

def _unblock(o):
    nb, b, h, blk, d = o.shape
    return jnp.moveaxis(o, 0, 2).reshape(b, h, nb * blk, d)

def _stick_breaking_attention(q, k, v):
    b, h, s_len, d = q.shape
    scale = d ** -0.5
    key_pos = jnp.arange(s_len)

    def block(args):
        qb, i = args
        z = jnp.einsum('bhqd,bhkd->bhqk', qb, k).astype(jnp.float32) * scale
        q_pos = i * Q_BLOCK + jnp.arange(Q_BLOCK)
        mask = key_pos[None, :] < q_pos[:, None]
        log_beta = jax.nn.log_sigmoid(z)
        log_not = jnp.where(mask, log_beta - z, 0.0)
        log_between = lax.cumsum(log_not, axis=3, reverse=True) - log_not
        w = jnp.where(mask, jnp.exp(log_beta + log_between), 0.0)
        return jnp.einsum('bhqk,bhkd->bhqd', w.astype(v.dtype), v)

    out = lax.map(block, (_query_blocks(q), jnp.arange(s_len // Q_BLOCK)))
    return _unblock(out)

def _forgetting_attention(q, k, v, log_f):
    b, h, s_len, d = q.shape
    scale = d ** -0.5
    key_pos = jnp.arange(s_len)
    c = lax.cumsum(log_f.astype(jnp.float32), axis=2)
    neg = jnp.finfo(jnp.float32).min

    def block(args):
        qb, cb, i = args
        z = jnp.einsum('bhqd,bhkd->bhqk', qb, k).astype(jnp.float32) * scale
        z = z + cb[..., :, None] - c[..., None, :]
        q_pos = i * Q_BLOCK + jnp.arange(Q_BLOCK)
        mask = key_pos[None, :] <= q_pos[:, None]
        p = jax.nn.softmax(jnp.where(mask, z, neg), axis=-1)
        return jnp.einsum('bhqk,bhkd->bhqd', p.astype(v.dtype), v)

    out = lax.map(block, (_query_blocks(q), _query_blocks(c), jnp.arange(s_len // Q_BLOCK)))
    return _unblock(out)

def _memory_attention(q, k, v):
    z = jnp.einsum('bhqd,bhkd->bhqk', q, k).astype(jnp.float32) * (q.shape[-1] ** -0.5)
    p = jax.nn.softmax(z, axis=-1)
    return jnp.einsum('bhqk,bhkd->bhqd', p.astype(v.dtype), v)

def first_inputs(seed: int = 0) -> dict:
    key = jax.random.key(seed)
    ks = jax.random.split(key, 32)
    L = DEPTH

    def w(k, shape, fan_in):
        return jax.random.normal(k, shape, jnp.float32) * (fan_in ** -0.5)

    def gain(k, shape):
        return 1.0 + 0.05 * jax.random.normal(k, shape, jnp.float32)

    return {
        'x': jax.random.normal(ks[0], (BATCH, SEQ, D_MODEL), jnp.float32),
        'mem': jax.random.normal(ks[1], (BATCH, MEM_LEN, D_MODEL), jnp.float32),
        'ffn1_pre_g': gain(ks[2], (L, D_MODEL)),
        'ffn1_post_g': gain(ks[3], (L, D_MODEL)),
        'ffn1_w_gate': w(ks[4], (L, D_MODEL, D_FF), D_MODEL),
        'ffn1_w_up': w(ks[5], (L, D_MODEL, D_FF), D_MODEL),
        'ffn1_w_down': w(ks[6], (L, D_FF, D_MODEL), D_FF),
        'mix_pre_g': gain(ks[7], (L, D_MODEL)),
        'mix_post_g': gain(ks[8], (L, D_MODEL)),
        'w_in': w(ks[9], (L, D_MODEL, IN_W), D_MODEL),
        'b_forget': 2.0 + 0.5 * jax.random.normal(ks[10], (L, N_FOX_HEADS), jnp.float32),
        'mem_norm_g': gain(ks[11], (D_MODEL,)),
        'w_mem_kv': w(ks[12], (L, D_MODEL, 2 * MEM_W), D_MODEL),
        'w_gate': w(ks[13], (L, D_MODEL, N_BRANCH * D_MODEL), D_MODEL),
        'b_gate': 0.02 * jax.random.normal(ks[14], (L, N_BRANCH * D_MODEL), jnp.float32),
        'w_br_sb': w(ks[15], (L, SB_W, D_MODEL), SB_W),
        'w_br_fox': w(ks[16], (L, FOX_W, D_MODEL), FOX_W),
        'w_br_mem': w(ks[17], (L, MEM_W, D_MODEL), MEM_W),
        'w_out': w(ks[18], (L, D_MODEL, D_MODEL), D_MODEL),
        'ffn2_pre_g': gain(ks[19], (L, D_MODEL)),
        'ffn2_post_g': gain(ks[20], (L, D_MODEL)),
        'ffn2_w_gate': w(ks[21], (L, D_MODEL, D_FF), D_MODEL),
        'ffn2_w_up': w(ks[22], (L, D_MODEL, D_FF), D_MODEL),
        'ffn2_w_down': w(ks[23], (L, D_FF, D_MODEL), D_FF),
    }

def first_block(x, mem, ffn1_pre_g, ffn1_post_g, ffn1_w_gate, ffn1_w_up, ffn1_w_down,
              mix_pre_g, mix_post_g, w_in, b_forget, mem_norm_g, w_mem_kv, w_gate, b_gate,
              w_br_sb, w_br_fox, w_br_mem, w_out,
              ffn2_pre_g, ffn2_post_g, ffn2_w_gate, ffn2_w_up, ffn2_w_down):
    mem_n = _rmsnorm(mem, mem_norm_g)
    split_at = np.cumsum([SB_W, SB_W, SB_W, FOX_W, FOX_W, FOX_W, N_FOX_HEADS])
    h = x
    for l in range(DEPTH):
        f = _swiglu(_rmsnorm(h, ffn1_pre_g[l]), ffn1_w_gate[l], ffn1_w_up[l], ffn1_w_down[l])
        h = h + 0.5 * _rmsnorm(f, ffn1_post_g[l])

        u = _rmsnorm(h, mix_pre_g[l])
        proj = u @ w_in[l]
        q_sb, k_sb, v_sb, q_fx, k_fx, v_fx, f_logit, q_mem = jnp.split(proj, split_at, axis=-1)

        o_sb = _stick_breaking_attention(_split_heads(q_sb, N_SB_HEADS), _split_heads(k_sb, N_SB_HEADS),
                                         _split_heads(v_sb, N_SB_HEADS))
        log_f = jax.nn.log_sigmoid((f_logit + b_forget[l]).astype(jnp.float32)).transpose(0, 2, 1)
        o_fx = _forgetting_attention(_split_heads(q_fx, N_FOX_HEADS), _split_heads(k_fx, N_FOX_HEADS),
                                     _split_heads(v_fx, N_FOX_HEADS), log_f)
        k_mem, v_mem = jnp.split(mem_n @ w_mem_kv[l], 2, axis=-1)
        o_mem = _memory_attention(_split_heads(q_mem, N_MEM_HEADS), _split_heads(k_mem, N_MEM_HEADS),
                                  _split_heads(v_mem, N_MEM_HEADS))

        g_sb, g_fx, g_mem = jnp.split(jax.nn.sigmoid(u @ w_gate[l] + b_gate[l]), N_BRANCH, axis=-1)
        merged = (g_sb * (_merge_heads(o_sb) @ w_br_sb[l])
                  + g_fx * (_merge_heads(o_fx) @ w_br_fox[l])
                  + g_mem * (_merge_heads(o_mem) @ w_br_mem[l]))
        h = h + _rmsnorm(merged @ w_out[l], mix_post_g[l])

        f = _swiglu(_rmsnorm(h, ffn2_pre_g[l]), ffn2_w_gate[l], ffn2_w_up[l], ffn2_w_down[l])
        h = h + 0.5 * _rmsnorm(f, ffn2_post_g[l])
    return h


N_A_LAYERS = DEPTH // 2
N_B_LAYERS = DEPTH - N_A_LAYERS
CONV_WIDTH = 3
D_FF_2 = 2816
N_HEADS = 8
QK_NOPE_DIM = 128
QK_ROPE_DIM = 64
V_HEAD_DIM = 128
Q_LORA_RANK = 512
KV_LORA_RANK = 256
ROPE_THETA = 10000.0


def rms_norm(x, g):
    xf = x.astype(jnp.float32)
    y = xf * lax.rsqrt(jnp.mean(xf * xf, axis=-1, keepdims=True) + RMS_EPS)
    return (y * g.astype(jnp.float32)).astype(x.dtype)

def causal_dwconv(x, w):
    c = x.shape[-1]
    return lax.conv_general_dilated(
        x, w[:, None, :].astype(x.dtype), window_strides=(1,),
        padding=((CONV_WIDTH - 1, 0),), dimension_numbers=("NWC", "WIO", "NWC"),
        feature_group_count=c)

def rope_tables(seq, dtype):
    inv = 1.0 / (ROPE_THETA ** (jnp.arange(0, QK_ROPE_DIM, 2, dtype=jnp.float32) / QK_ROPE_DIM))
    ang = jnp.arange(seq, dtype=jnp.float32)[:, None] * inv[None, :]
    return jnp.cos(ang).astype(dtype), jnp.sin(ang).astype(dtype)

def apply_rope(x, cos, sin):
    x1, x2 = jnp.split(x, 2, axis=-1)
    return jnp.concatenate([x1 * cos - x2 * sin, x1 * sin + x2 * cos], axis=-1)

def short_conv_mixer(x_n, w_in, conv_w, w_out):
    b, c, h = jnp.split(x_n @ w_in, 3, axis=-1)
    return (b * causal_dwconv(c * h, conv_w)) @ w_out

def conv_ffn(x_n, w_up, conv_w, w_down):
    g, u = jnp.split(causal_dwconv(x_n @ w_up, conv_w), 2, axis=-1)
    return (jax.nn.silu(g) * u) @ w_down

def shared_latent_kv(h, kv_in_norm, w_dkv, kv_norm, w_ukv, cos, sin):
    bsz, seq, _ = h.shape
    ckv = rms_norm(h, kv_in_norm) @ w_dkv
    c_kv, k_rope = ckv[..., :KV_LORA_RANK], ckv[..., KV_LORA_RANK:]
    k_rope = apply_rope(k_rope, cos, sin)
    kv = (rms_norm(c_kv, kv_norm) @ w_ukv).reshape(bsz, seq, N_HEADS, QK_NOPE_DIM + V_HEAD_DIM)
    return kv[..., :QK_NOPE_DIM], kv[..., QK_NOPE_DIM:], k_rope

def mla_attention(x_n, w_dq, q_norm, w_uq, w_o, k_nope, v, k_rope, cos, sin):
    bsz, seq, _ = x_n.shape
    q = (rms_norm(x_n @ w_dq, q_norm) @ w_uq).reshape(bsz, seq, N_HEADS, QK_NOPE_DIM + QK_ROPE_DIM)
    q_nope = q[..., :QK_NOPE_DIM]
    q_rope = apply_rope(q[..., QK_NOPE_DIM:], cos[:, None, :], sin[:, None, :])
    n_blk = seq // Q_BLOCK

    def to_blocks(t):
        return jnp.moveaxis(t.reshape(bsz, n_blk, Q_BLOCK, *t.shape[2:]), 1, 0)

    k_pos = jnp.arange(seq)
    scale = (QK_NOPE_DIM + QK_ROPE_DIM) ** -0.5

    def attend_block(args):
        qn, qr, blk = args
        s = (jnp.einsum('bqhd,bkhd->bhqk', qn, k_nope)
             + jnp.einsum('bqhr,bkr->bhqk', qr, k_rope)).astype(jnp.float32) * scale
        q_pos = blk * Q_BLOCK + jnp.arange(Q_BLOCK)
        s = jnp.where(k_pos[None, :] <= q_pos[:, None], s, -jnp.inf)
        p = jax.nn.softmax(s, axis=-1).astype(v.dtype)
        return jnp.einsum('bhqk,bkhd->bqhd', p, v)

    o = lax.map(attend_block, (to_blocks(q_nope), to_blocks(q_rope), jnp.arange(n_blk)))
    o = jnp.moveaxis(o, 0, 1).reshape(bsz, seq, N_HEADS * V_HEAD_DIM)
    return o @ w_o

def second_inputs(seed: int = 0) -> dict:
    key = jax.random.key(seed)
    ks = jax.random.split(key, 24)
    f32 = jnp.float32

    def w(k, shape, fan_in):
        return jax.random.normal(k, shape, f32) * (fan_in ** -0.5)

    def gain(k, shape):
        return 1.0 + 0.02 * jax.random.normal(k, shape, f32)

    return {
        "x": jax.random.normal(ks[0], (BATCH, SEQ, D_MODEL), f32),
        "a_mix_norm": gain(ks[1], (N_A_LAYERS, D_MODEL)),
        "a_w_in": w(ks[2], (N_A_LAYERS, D_MODEL, 3 * D_MODEL), D_MODEL),
        "a_conv": w(ks[3], (N_A_LAYERS, CONV_WIDTH, D_MODEL), CONV_WIDTH),
        "a_w_out": w(ks[4], (N_A_LAYERS, D_MODEL, D_MODEL), D_MODEL),
        "b_mix_norm": gain(ks[5], (N_B_LAYERS, D_MODEL)),
        "b_w_dq": w(ks[6], (N_B_LAYERS, D_MODEL, Q_LORA_RANK), D_MODEL),
        "b_q_norm": gain(ks[7], (N_B_LAYERS, Q_LORA_RANK)),
        "b_w_uq": w(ks[8], (N_B_LAYERS, Q_LORA_RANK, N_HEADS * (QK_NOPE_DIM + QK_ROPE_DIM)), Q_LORA_RANK),
        "b_w_o": w(ks[9], (N_B_LAYERS, N_HEADS * V_HEAD_DIM, D_MODEL), N_HEADS * V_HEAD_DIM),
        "kv_in_norm": gain(ks[10], (D_MODEL,)),
        "w_dkv": w(ks[11], (D_MODEL, KV_LORA_RANK + QK_ROPE_DIM), D_MODEL),
        "kv_norm": gain(ks[12], (KV_LORA_RANK,)),
        "w_ukv": w(ks[13], (KV_LORA_RANK, N_HEADS * (QK_NOPE_DIM + V_HEAD_DIM)), KV_LORA_RANK),
        "ffn_norm": gain(ks[14], (DEPTH, D_MODEL)),
        "ffn_w_up": w(ks[15], (DEPTH, D_MODEL, 2 * D_FF_2), D_MODEL),
        "ffn_conv": w(ks[16], (DEPTH, CONV_WIDTH, 2 * D_FF_2), CONV_WIDTH),
        "ffn_w_down": w(ks[17], (DEPTH, D_FF_2, D_MODEL), D_FF_2),
        "final_norm": gain(ks[18], (D_MODEL,)),
    }

def second_block(x, a_mix_norm, a_w_in, a_conv, a_w_out, b_mix_norm, b_w_dq, b_q_norm, b_w_uq, b_w_o,
              kv_in_norm, w_dkv, kv_norm, w_ukv, ffn_norm, ffn_w_up, ffn_conv, ffn_w_down, final_norm):
    cos, sin = rope_tables(x.shape[1], x.dtype)
    h = x
    shared = None
    for layer in range(DEPTH):
        if layer < N_A_LAYERS:
            h = h + short_conv_mixer(rms_norm(h, a_mix_norm[layer]), a_w_in[layer],
                                     a_conv[layer], a_w_out[layer])
        else:
            j = layer - N_A_LAYERS
            k_nope, v, k_rope = shared
            h = h + mla_attention(rms_norm(h, b_mix_norm[j]), b_w_dq[j], b_q_norm[j], b_w_uq[j],
                                  b_w_o[j], k_nope, v, k_rope, cos, sin)
        h = h + conv_ffn(rms_norm(h, ffn_norm[layer]), ffn_w_up[layer], ffn_conv[layer], ffn_w_down[layer])
        if layer == N_A_LAYERS - 1:
            shared = shared_latent_kv(h, kv_in_norm, w_dkv, kv_norm, w_ukv, cos, sin)
    return rms_norm(h, final_norm)


def setup_inputs(seed=0):
    out = dict(first_inputs(seed))
    for name, value in second_inputs(seed + 1).items():
        if name != "x":
            out[name + "_2"] = value
    return out


def reference(
    x, mem, ffn1_pre_g, ffn1_post_g, ffn1_w_gate, ffn1_w_up, ffn1_w_down, mix_pre_g, mix_post_g,
    w_in, b_forget, mem_norm_g, w_mem_kv, w_gate, b_gate, w_br_sb, w_br_fox, w_br_mem, w_out,
    ffn2_pre_g, ffn2_post_g, ffn2_w_gate, ffn2_w_up, ffn2_w_down, a_mix_norm_2, a_w_in_2,
    a_conv_2, a_w_out_2, b_mix_norm_2, b_w_dq_2, b_q_norm_2, b_w_uq_2, b_w_o_2, kv_in_norm_2,
    w_dkv_2, kv_norm_2, w_ukv_2, ffn_norm_2, ffn_w_up_2, ffn_conv_2, ffn_w_down_2, final_norm_2,
):
    x = first_block(
        x, mem, ffn1_pre_g, ffn1_post_g, ffn1_w_gate, ffn1_w_up, ffn1_w_down, mix_pre_g,
        mix_post_g, w_in, b_forget, mem_norm_g, w_mem_kv, w_gate, b_gate, w_br_sb, w_br_fox,
        w_br_mem, w_out, ffn2_pre_g, ffn2_post_g, ffn2_w_gate, ffn2_w_up, ffn2_w_down,
    )
    return second_block(
        x, a_mix_norm_2, a_w_in_2, a_conv_2, a_w_out_2, b_mix_norm_2, b_w_dq_2, b_q_norm_2,
        b_w_uq_2, b_w_o_2, kv_in_norm_2, w_dkv_2, kv_norm_2, w_ukv_2, ffn_norm_2, ffn_w_up_2,
        ffn_conv_2, ffn_w_down_2, final_norm_2,
    )


_drawn_inputs = setup_inputs


def setup_inputs(seed=0):
    import zlib

    import numpy as np

    out = dict(_drawn_inputs(seed))
    spreads = {}
    factors = {'mem_norm_g': 4.584,
     'b_gate': 5.597,
     'a_mix_norm_2': 3.342,
     'b_mix_norm_2': 8.0,
     'b_q_norm_2': 8.0,
     'kv_in_norm_2': 8.0,
     'kv_norm_2': 8.0,
     'ffn_norm_2': 5.321,
     'final_norm_2': 2.793}
    for name, (base, spread) in spreads.items():
        noise = np.random.default_rng([zlib.crc32(name.encode()), seed]).standard_normal(out[name].shape)
        drawn = base * np.exp(spread * noise) if base else spread * noise
        out[name] = __import__('jax').numpy.asarray(drawn.astype(out[name].dtype))
    for name, factor in factors.items():
        out[name] = (out[name] * factor).astype(out[name].dtype)
    return out
```

```python
from contextlib import ExitStack

import numpy as np

import concourse.bass as bass
from concourse import mybir

F32 = mybir.dt.float32
F32R = mybir.dt.float32r
ACT = mybir.ActivationFunctionType
ALU = mybir.AluOpType
AX_X = mybir.AxisListType.X

P = 128
DM = 1024
KT = DM // P
TOK = 256
TT = TOK // P
LAYERS = 2
FF = 2816
FT = FF // P
HD = 64
NPAIR = 4
MH = 4
EPS = 1e-6
NOPE, ROPE, VD, NH = 128, 64, 128, 8
QL, KVL = 512, 256
MLA_SCALE = float((NOPE + ROPE) ** -0.5)
MEM_SCALE = float(P ** -0.5)
SB_SCALE = float(HD ** -0.5)

SLOTS = 4
AHEAD = 2
CW = 1024
CAUSAL = 3 * P

FFN_C, FFN_G = 3 * FT, FT
MIX_C = 12 + 12 * NPAIR + 12 + 8
LAYER_C = 2 * FFN_C + MIX_C
LAYER_G = 2 * FFN_G + 12 + 12 * NPAIR + 12
assert LAYER_C % SLOTS == 0 and LAYER_G % 2 == 0

LP = 72
LP_NAMES = [("ffn1_pre_g", 8), ("ffn1_post_g", 8), ("mix_pre_g", 8), ("mix_post_g", 8),
            ("ffn2_pre_g", 8), ("ffn2_post_g", 8), ("b_gate", 24)]
PRE1, POST1, PREM, POSTM, PRE2, POST2, BGATE = 0, 8, 16, 24, 32, 40, 48
MEMG = LAYERS * LP
AMIX, ACONV, BMIX, BQ, KVIN, KVN = MEMG + 8, MEMG + 16, MEMG + 40, MEMG + 48, MEMG + 52, MEMG + 60
FFNN, FINAL, FCONV = MEMG + 62, MEMG + 78, MEMG + 86
PCOLS = FCONV + 2 * 3 * 2 * FT
assert PCOLS <= 512

C_ID, C_ONE, C_GT, C_LE, C_M01, C_MADD, C_PERM, C_COS, C_SIN, C_NEG8 = (
    0, 128, 256, 384, 512, 640, 1024, 1152, 1408, 1664)
C_COLS = C_NEG8 + 8
MASKED = -1e30
PARAM_LOADS = 7 * LAYERS + 10 + PCOLS // P


def constants():
    c = np.zeros((P, C_COLS), np.float32)
    row, col = np.arange(P)[:, None], np.arange(P)[None, :]
    c[:, C_ID:C_ID + P] = row == col
    c[:, C_ONE:C_ONE + P] = 1.0
    c[:, C_GT:C_GT + P] = row > col
    c[:, C_LE:C_LE + P] = row <= col
    c[:, C_M01:C_M01 + P] = row < col
    diagonal = np.where(col <= row, 0.0, MASKED)
    c[:, C_MADD:C_MADD + P] = diagonal
    c[:, C_MADD + 2 * P:C_MADD + 3 * P] = diagonal
    half = ROPE // 2
    c[:, C_PERM:C_PERM + P] = (row // ROPE == col // ROPE) & ((row + half) % ROPE == col % ROPE)
    inv = (1.0 / (10000.0 ** (np.arange(0, ROPE, 2, dtype=np.float32) / ROPE))).astype(np.float32)
    angle = np.arange(TOK, dtype=np.float32)[None, :] * inv[:, None]
    cos, sin = np.cos(angle), np.sin(angle)
    for p in range(0, P, ROPE):
        c[p:p + half, C_COS:C_COS + TOK] = cos
        c[p + half:p + ROPE, C_COS:C_COS + TOK] = cos
        c[p:p + half, C_SIN:C_SIN + TOK] = -sin
        c[p + half:p + ROPE, C_SIN:C_SIN + TOK] = sin
    c[:8, C_NEG8:C_NEG8 + 8] = -np.eye(8)
    return c


class Chunk:

    def __init__(self, rounds, k):
        self.rounds, self.k = rounds, k

    def __add__(self, n):
        return Chunk(self.rounds, self.k + n)

    def later(self, rounds):
        return Chunk(self.rounds + rounds, self.k)

    def count(self, more=0):
        return self.rounds * SLOTS + (self.k + more)

    @property
    def slot(self):
        return self.k % SLOTS

    @property
    def uses(self):
        return self.rounds + (self.k // SLOTS + 1)


class Group:

    def __init__(self, base, k):
        self.base, self.k = base, k

    def __add__(self, n):
        return Group(self.base, self.k + n)

    def later(self, n):
        return Group(self.base + n, self.k)

    def count(self, more=0):
        return self.base + (self.k + more)


def program(nc, A, consts, out):
    ctx = ExitStack()
    with ctx:
        def sb(name, shape, dt=F32):
            return ctx.enter_context(nc.sbuf_tensor(name, shape, dt))

        def sem(name):
            return ctx.enter_context(nc.semaphore(name))

        raw = [sb(f"raw{s}", [P, CW]) for s in range(SLOTS)]
        whi = [sb(f"whi{s}", [P, CW], F32R) for s in range(SLOTS)]
        wlo = [sb(f"wlo{s}", [P, CW], F32R) for s in range(SLOTS)]
        H = sb("H", [P, KT, TOK])
        work = sb("work", [P, KT, TOK])
        sq = sb("sq", [P, KT, TOK])
        uhi, ulo = sb("uhi", [P, KT, TOK], F32R), sb("ulo", [P, KT, TOK], F32R)
        hhi, hlo = sb("hhi", [P, FT, TOK], F32R), sb("hlo", [P, FT, TOK], F32R)
        mhi, mlo = sb("mhi", [P, KT, TOK], F32R), sb("mlo", [P, KT, TOK], F32R)
        gates = sb("gates", [P, 3 * KT, TOK])
        kmem = sb("kmem", [P, MH, TOK])
        vmem = sb("vmem", [P, TT, MH, P])
        qmem = sb("qmem", [P, MH, TOK])
        small = sb("small", [P, 6 * TOK])
        par = sb("par", [P, 512])
        lp = sb("lp", [P, LP])
        cst = sb("cst", [P, C_COLS])
        bfor = sb("bfor", [P, LAYERS, 8])
        wfor = sb("wfor", [P, KT, 8])
        wfhi, wflo = sb("wfhi", [P, KT, 8], F32R), sb("wflo", [P, KT, 8], F32R)
        flog, fabs = sb("flog", [P, TT, 8]), sb("fabs", [P, TT, 8])
        ctok = sb("ctok", [P, TT, 8])
        crow = sb("crow", [8, TOK])
        cpair = sb("cpair", [8, 2, TOK])
        qm1, vm1 = sb("qm1", [P, TOK]), sb("vm1", [P, TT, P])
        root, rstd = sb("root", [P, TOK]), sb("rstd", [P, TOK])
        fmax, fsum, frec = sb("fmax", [P, 4]), sb("fsum", [P, 4]), sb("frec", [P, 4])
        mmax, msum, mrec = sb("mmax", [P, 2]), sb("msum", [P, 2]), sb("mrec", [P, 2])

        param_rows = gates[:, 0:2, :].rearrange("p a (b n) -> p (a b) n", n=P)
        mtok = gates[:, 8:16, :].rearrange("p (t a) n -> p t (a n)", t=TT)
        flat = lambda t: t[:, :, :].rearrange("p a b -> p (a b)")
        ident, ones = cst[:, C_ID:C_ID + P], cst[:, C_ONE:C_ONE + P]
        later_keys, up_to = cst[:, C_GT:C_GT + P], cst[:, C_LE:C_LE + P]
        before = cst[:, C_M01:C_M01 + P]
        hide = cst[:, C_MADD:C_MADD + CAUSAL]
        swap = cst[:, C_PERM:C_PERM + P]
        cosine, sine = cst[:, C_COS:C_COS + TOK], cst[:, C_SIN:C_SIN + TOK]

        def two(t, a):
            return flat(t)[:, a:a + 2 * CAUSAL].rearrange("p (h c) -> p h c", h=2)

        sb_e, sb_sp = two(sq, 0), two(sq, 2 * CAUSAL)
        fx_pT = sb_e
        mem_p = flat(sq)[:, 4 * CAUSAL:4 * CAUSAL + 512]
        sb_w, fx_s = two(work, 0), two(work, 2 * CAUSAL)
        mem_pT = flat(work)[:, 4 * CAUSAL:4 * CAUSAL + 512]
        part = lambda n: small[:, n * TOK:(n + 1) * TOK]
        qs, ks, vs, qf, kf, vf = (part(n) for n in range(6))
        sg = [part(0), part(1)]
        hf = [part(2), part(3)]
        conv_y = [flat(gates)[:, n * 512:(n + 1) * 512] for n in range(2)]
        kn = gates[:, 0:8, :]
        vn = flat(gates)[:, 2048:4096].rearrange("p (t h d) -> p t h d", t=TT, h=NH)
        qn = gates[:, 16:24, :]
        ckv, kr_raw, kr = kmem[:, 0:2, :], kmem[:, 2, :], kmem[:, 3, :]
        qlat = vmem[:, :, :, :].rearrange("p t h d -> p (t h) d").rearrange("p (k a) d -> p k (a d)", a=2)
        qr = qmem

        def half(t, h, n=CAUSAL, at=0):
            a = at + (h % 2) * n
            return t[:, a:a + n]

        ls = lambda h: half(flat(sq), h)
        lpT = lambda h: half(flat(sq), h, at=2 * CAUSAL)
        lmax, lsum, lrec = (lambda h, t=t: half(t, h, 2) for t in (fmax, fsum, frec))

        bank = [ctx.enter_context(nc.psum_tensor(f"bank{n}", [P, 512], F32)) for n in range(8)]
        pair_bank = lambda n: bank[n][:, :].rearrange("p (t n) -> p t n", t=2)

        w_loaded = [sem(f"w_loaded{s}") for s in range(SLOTS)]
        hi_ready = sem("hi_ready")
        lo_ready = sem("lo_ready")
        w_used = sem("w_used")
        group_done = sem("group_done")
        sq_done = sem("sq_done")
        ss_full = sem("ss_full")
        root_done = sem("root_done")
        rstd_done = sem("rstd_done")
        acc_copied = sem("acc_copied")
        scaled = sem("scaled")
        h_ready = sem("h_ready")
        un_done = sem("un_done")
        uhi_done = sem("uhi_done")
        ulo_done = sem("ulo_done")
        silu_done, hid_done, hhi_done, hlo_done = sem("silu_done"), sem("hid_done"), sem("hhi_done"), sem("hlo_done")
        tap_done, conv_done, y_done = sem("tap_done"), sem("conv_done"), sem("y_done")
        zeroed = sem("zeroed")
        f_full, f_biased, f_log, f_ready = sem("f_full"), sem("f_biased"), sem("f_log"), sem("f_ready")
        f_split = sem("f_split")
        wf_loaded = sem("wf_loaded")
        c_full, c_ready = sem("c_full"), sem("c_ready")
        mem_full, mem_max, mem_exp, mem_rec, mem_norm = (sem(n) for n in ("mem_full", "mem_max", "mem_exp", "mem_rec", "mem_norm"))
        mem_staged, mem_tp, mem_pt = sem("mem_staged"), sem("mem_tp"), sem("mem_pt")
        sbz_full, sb_act, sb_dve, sb_masked = sem("sbz_full"), sem("sb_act"), sem("sb_dve"), sem("sb_masked")
        sb_cum, sb_lw, sb_exp, sb_ready = sem("sb_cum"), sem("sb_lw"), sem("sb_exp"), sem("sb_ready")
        fxz_full, fx_add, fx_max, fx_exp, fx_rec, fx_norm = (sem(n) for n in ("fxz_full", "fx_add", "fx_max", "fx_exp", "fx_rec", "fx_norm"))
        fx_tp, fx_pt = sem("fx_tp"), sem("fx_pt")
        c_pair = sem("c_pair")
        o_full, ohi_done, olo_done = sem("o_full"), sem("ohi_done"), sem("olo_done")
        sig_done, gated, merged, mgh_done, mgl_done = (sem(n) for n in ("sig_done", "gated", "merged", "mgh_done", "mgl_done"))
        cst_loaded, x_loaded, m_loaded, p_loaded, bf_loaded = (sem(n) for n in ("cst_loaded", "x_loaded", "m_loaded", "p_loaded", "bf_loaded"))
        par_tp, par_ready, x_tp, lp_ready = sem("par_tp"), sem("par_ready"), sem("x_tp"), sem("lp_ready")
        m_sq, m_root, m_rstd, m_scaled, m_tp, m_gain, m_hi, m_lo = (
            sem(n) for n in ("m_sq", "m_root", "m_rstd", "m_scaled", "m_tp", "m_gain", "m_hi", "m_lo"))
        rp_swap, rp_cos, rp_sin, rp_done = (sem(n) for n in ("rp_swap", "rp_cos", "rp_sin", "rp_done"))
        lat_done, lat_hi, lat_lo = sem("lat_done"), sem("lat_hi"), sem("lat_lo")
        ls_full, ls_add, ls_max, ls_exp, ls_rec, ls_norm, ls_tp, ls_pt = (
            sem(n) for n in ("ls_full", "ls_add", "ls_max", "ls_exp", "ls_rec", "ls_norm", "ls_tp", "ls_pt"))
        la_full, la_hi, la_lo = sem("la_full"), sem("la_hi"), sem("la_lo")
        y_tp, y_copied, y_stored = sem("y_tp"), sem("y_copied"), sem("y_stored")

        C2, G2 = LAYERS * LAYER_C, LAYERS * LAYER_G
        rounds2 = C2 // SLOTS
        c_conv = Chunk(rounds2, 0)
        c_aout = c_conv + 3 * KT
        c_ffa = c_aout + KT
        c_kv = c_ffa + FFN_C
        c_dq = c_kv + 3
        c_uqr = c_dq + 4
        c_pairs = c_uqr + 4
        c_o = c_pairs + 8
        c_ffb = c_o + KT
        CHUNKS = C2 + c_ffb.k + FFN_C
        g_conv = G2
        g_ffa = g_conv + 3 * KT
        g_kv = g_ffa + FFN_G
        g_dq = g_kv + 3
        g_uqr = g_dq + 4
        g_pairs = g_uqr + 4
        g_ffb = g_pairs + 12
        N2, S2 = 6 * LAYERS, 24 * LAYERS
        n_conv, n_ffa, n_h2, n_kv, n_q, n_ffb, n_fin = (
            (N2, S2), (N2 + 1, S2 + 4), (N2 + 2, S2 + 8), (N2 + 3, S2 + 12), (N2 + 4, S2 + 13),
            (N2 + 5, S2 + 15), (N2 + 6, S2 + 19))

        block = ctx.enter_context(nc.Block())

        @block.sync
        def _(sp):
            def load(c, halves):
                pieces = halves(raw[c.slot])
                sp.wait_ge(lo_ready, c.count(1))
                for dst, src in pieces:
                    sp.dma_start(dst, src).then_inc(w_loaded[c.slot], 16)

            def place(at):
                return at if isinstance(at, int) else sp.snap(at)

            def cols(w, kt, at, n, rows=0, into=0, width=None):
                def halves(slot):
                    width_ = width or n
                    d = slot[:, 0:kt * width_].rearrange("p (k n) -> p k n", k=kt)[:, :, into:into + n]
                    s = w.rearrange("(k p) n -> p k n", p=P)[:, rows:rows + kt, bass.ds(place(at), n)]
                    m = kt // 2
                    return [(d[:, m:kt, :], s[:, m:kt, :]), (d[:, 0:m, :], s[:, 0:m, :])]
                return halves

            def sides(w, kt, n, ats):
                def halves(slot):
                    d = slot[:, 0:kt * 2 * n].rearrange("p (k s n) -> p k s n", k=kt, s=2)
                    s = w.rearrange("(k p) n -> p k n", p=P)
                    return [(d[:, :, j, :], s[:, 0:kt, bass.ds(a, n)]) for j, a in enumerate(ats)]
                return halves

            def rows_of(w, k):
                def halves(slot):
                    s = w[bass.ds(place(k * P), P), :]
                    return [(slot[:, CW // 2:CW], s[:, CW // 2:CW]), (slot[:, 0:CW // 2], s[:, 0:CW // 2])]
                return halves

            def ffn(c, w_gate, g_at, w_up, u_at, w_down):
                with sp.Fori(0, FT // 2) as i:
                    for j in range(2):
                        load(c.later(i) + 2 * j, cols(w_gate, KT, i * (2 * P) + (g_at + j * P), P))
                        load(c.later(i) + (2 * j + 1), cols(w_up, KT, i * (2 * P) + (u_at + j * P), P))
                down = c + 2 * FT
                for k in range(2):
                    load(down + k, rows_of(w_down, k))
                with sp.Fori(0, (FT - 2) // 4) as i:
                    for j in range(4):
                        load((down + (2 + j)).later(i), rows_of(w_down, i * 4 + (2 + j)))

            sp.dma_start(cst[:, :], consts).then_inc(cst_loaded, 16)
            sp.dma_start(work[:, :, :].rearrange("p (t a) n -> p t (a n)", t=TT),
                         A["x"].rearrange("a (t p) d -> p (a t) d", p=P)).then_inc(x_loaded, 16)
            with sp.Fori(0, LAYERS) as l:
                of = lambda name: A[name][bass.ds(l, 1), :, :].rearrange("a k n -> (a k) n")
                c = Chunk(l * (LAYER_C // SLOTS), 0)
                ffn(c, of("ffn1_w_gate"), 0, of("ffn1_w_up"), 0, of("ffn1_w_down"))
                c = c + FFN_C
                w_in, w_mem, w_gate = of("w_in"), of("w_mem_kv"), of("w_gate")
                sp.wait_ge(f_split, l * 2 + 2)
                sp.dma_start(wfor[:, :, :], w_in.rearrange("(k p) n -> p k n", p=P)[:, :, 3072:3080])\
                  .then_inc(wf_loaded, 16)
                for n in range(8):
                    load(c + n, cols(w_mem, KT, n * P, P))
                for h in range(MH):
                    load(c + (8 + h), cols(w_in, KT, 3080 + h * P, P))
                with sp.Fori(0, NPAIR) as p:
                    cp = (c + 12).later(p * 3)
                    for n in range(6):
                        load(cp + n, cols(w_in, KT, p * P + n * 512, P))
                    for n in range(6):
                        load(cp + (6 + n), cols(w_gate, KT, p * (6 * P) + n * P, P))
                c = c + (12 + 12 * NPAIR)
                branches = [of(n) for n in ("w_br_sb", "w_br_fox", "w_br_mem")]
                for j in range(4):
                    for b in range(3):
                        load(c + (3 * j + b), cols(branches[b], 4, j * 2 * P, 2 * P))
                c = c + 12
                w_out = of("w_out")
                for n in range(KT):
                    load(c + n, cols(w_out, KT, n * P, P))
                c = c + KT
                ffn(c, of("ffn2_w_gate"), 0, of("ffn2_w_up"), 0, of("ffn2_w_down"))
            a_in = A["a_w_in_2"][0]
            with sp.Fori(0, 2) as i:
                for f in range(4):
                    for n, part_at in enumerate((DM, 2 * DM, 0)):
                        load(c_conv.later(i * 3) + (3 * f + n), cols(a_in, KT, i * (4 * P) + (part_at + f * P), P))
            for n in range(KT):
                load(c_aout + n, cols(A["a_w_out_2"][0], KT, n * P, P))
            ffn(c_ffa, A["ffn_w_up_2"][0], 0, A["ffn_w_up_2"][0], FF, A["ffn_w_down_2"][0])
            for n in range(2):
                load(c_kv + n, cols(A["w_dkv_2"], KT, n * P, P))
            load(c_kv + 2, sides(A["w_dkv_2"], KT, ROPE, (KVL, KVL)))
            for n in range(4):
                load(c_dq + n, cols(A["b_w_dq_2"][0], KT, n * P, P))
            w_uq, w_ukv = A["b_w_uq_2"][0], A["w_ukv_2"]
            HQ = NOPE + ROPE
            for p in range(4):
                load(c_uqr + p, sides(w_uq, 4, ROPE, (2 * p * HQ + NOPE, (2 * p + 1) * HQ + NOPE)))
            for p in range(4):
                load(c_pairs + 2 * p, cols(w_ukv, 2, p * 512, 512))
                load(c_pairs + (2 * p + 1), sides(w_uq, 4, NOPE, (2 * p * HQ, (2 * p + 1) * HQ)))
            for n in range(KT):
                load(c_o + n, cols(A["b_w_o_2"][0], KT, n * P, P))
            ffn(c_ffb, A["ffn_w_up_2"][1], 0, A["ffn_w_up_2"][1], FF, A["ffn_w_down_2"][1])
            for t in range(TT):
                sp.wait_ge(y_copied, 4 * t + 4)
                sp.dma_start(out[0, t * P:(t + 1) * P, :], gates[:, 4 * t:4 * t + 4, :].rearrange("p a n -> p (a n)"))\
                  .then_inc(y_stored, 16)
            sp.wait_ge(y_stored, 16 * TT)

        @block.gpsimd
        def _(pool):
            pool.memset(param_rows[:, 3, :], 0.0).then_inc(zeroed, 1)

            def ulow(m, dst=ulo, src=uhi):
                for b in range(4):
                    pool.wait_ge(uhi_done, m * 4 + (b + 1))
                    s = slice(2 * b, 2 * b + 2)
                    pool.tensor_tensor(dst[:, s, :], work[:, s, :], src[:, s, :].bitcast(F32), ALU.subtract)\
                        .then_inc(ulo_done, 1)

            diag = lambda t: t.rearrange("p h (a n) -> p h a n", n=P)[:, :, 0:3:2, :]
            mask = before.unsqueeze(1).unsqueeze(1).to_broadcast([P, 2, 2, P])
            with pool.Fori(0, LAYERS) as l:
                ulow(l * 3)
                ulow(l * 3 + 1)
                with pool.Fori(0, NPAIR) as p:
                    I = l * NPAIR + p
                    pool.wait_ge(sb_dve, I * 2 + 2)
                    pool.tensor_tensor(diag(sb_sp), diag(sb_sp), mask, ALU.mult).then_inc(sb_masked, 1)
                    pool.wait_ge(sb_exp, I + 1)
                    pool.tensor_tensor(diag(sb_w), diag(sb_w), mask, ALU.mult).then_inc(sb_ready, 1)
                ulow(l * 3 + 2)
            M2 = 3 * LAYERS
            ulow(M2)
            ulow(M2 + 1)
            ulow(M2 + 2)
            ulow(M2 + 3, hlo, hhi)
            ulow(M2 + 4)

        @block.scalar
        def _(act):
            def hi(c):
                if isinstance(c.rounds, int) and c.count() >= CHUNKS:
                    return
                act.wait_ge(w_loaded[c.slot], c.uses * 32)
                act.wait_ge(w_used, c.count(1))
                act.activation(whi[c.slot][:, :], raw[c.slot][:, :], ACT.Copy).then_inc(hi_ready, 1)

            def prime():
                for n in range(AHEAD):
                    act.wait_ge(w_loaded[n], 32)
                    act.wait_ge(w_used, n + 1)
                    act.activation(whi[n][:, :], raw[n][:, :], ACT.Copy).then_inc(hi_ready, 1)

            def chunks(c, n):
                for j in range(n):
                    hi(c + (AHEAD + j))

            def take_root(n, width):
                act.wait_ge(ss_full, n + 1)
                act.activation(root[:, :], bank[2][:, 0:TOK], ACT.Sqrt, scale=1.0 / width, bias=EPS)\
                   .then_inc(root_done, 1)

            def squares_of_stream(n, version):
                for b in range(4):
                    act.wait_ge(h_ready, version * 4 + (b + 1))
                    s = slice(2 * b, 2 * b + 2)
                    act.activation(sq[:, s, :], H[:, s, :], ACT.Square).then_inc(sq_done, 1)
                take_root(n, DM)

            def squares_of_result(n, last):
                act.wait_ge(w_used, last.count(1 + SLOTS))
                for b in range(4):
                    act.activation(sq[:, 2 * b:2 * b + 2, :], pair_bank(4 + b), ACT.Square).then_inc(sq_done, 1)
                take_root(n, DM)

            def uhigh(m, dst=uhi):
                for b in range(4):
                    act.wait_ge(un_done, m * 4 + (b + 1))
                    s = slice(2 * b, 2 * b + 2)
                    act.activation(dst[:, s, :], work[:, s, :], ACT.Copy).then_inc(uhi_done, 1)

            def ffn(c, g, use):
                with act.Fori(0, FT // 2) as i:
                    for j in range(2):
                        ci = c.later(i) + 2 * j
                        chunks(ci, 2)
                        act.wait_ge(w_used, ci.count(2 + SLOTS))
                        act.activation(sg[j], bank[(g.k + j) % 2][:, 0:TOK], ACT.Silu).then_inc(silu_done, 1)
                        act.wait_ge(group_done, g.base + i * 2 + (g.k + j + 3))
                        act.activation(hhi[:, bass.ds(i * 2 + j, 1), :].rearrange("p a n -> p (a n)"), hf[j], ACT.Copy)\
                           .then_inc(hhi_done, 1)
                down(c + 2 * FT)

            def down(c):
                chunks(c, 2)
                turns = (FT - 2) // 4
                last = isinstance(c.rounds, int) and c.count(FT) == CHUNKS
                with act.Fori(0, turns - last) as i:
                    chunks((c + 2).later(i), 4)
                if last:
                    chunks((c + 2).later(turns - 1), 4)

            def conv_ffn(c, g, use, layer):
                taps = FCONV + layer * 6 * FT
                with act.Fori(0, FT // 2) as i:
                    for j in range(2):
                        ci = c.later(i) + 2 * j
                        chunks(ci, 2)
                        act.wait_ge(w_used, ci.count(2 + SLOTS))
                        for s in range(2):
                            act.activation(conv_y[j][:, s * TOK:(s + 1) * TOK],
                                           bank[(g.k + j) % 2][:, s * TOK:(s + 1) * TOK], ACT.Copy,
                                           scale=par[:, bass.ds(i * 2 + (taps + 4 * FT + s * FT + j), 1)]).then_inc(tap_done, 1)
                        f = i * 2 + (j + (use * FT))
                        act.wait_ge(conv_done, f * 3 + 3)
                        act.activation(sg[j], conv_y[j][:, 0:TOK], ACT.Silu).then_inc(silu_done, 1)
                        act.wait_ge(hid_done, f + 1)
                        act.activation(hhi[:, bass.ds(i * 2 + j, 1), :].rearrange("p a n -> p (a n)"), hf[j], ACT.Copy)\
                           .then_inc(hhi_done, 1)
                down(c + 2 * FT)

            def head_high(count, src, dst):
                act.wait_ge(o_full, count)
                act.activation(dst, src, ACT.Copy).then_inc(ohi_done, 1)

            at = 0
            pieces = [(A[n][l], k) for l in range(LAYERS) for n, k in LP_NAMES]
            pieces += [(A["mem_norm_g"], 8), (A["a_mix_norm_2"][0], 8), (A["a_conv_2"][0], 24),
                       (A["b_mix_norm_2"][0], 8), (A["b_q_norm_2"][0], 4), (A["kv_in_norm_2"], 8),
                       (A["kv_norm_2"], 2), (A["ffn_norm_2"], 16), (A["final_norm_2"], 8),
                       (A["ffn_conv_2"], 264)]
            loads = 0
            act.wait_ge(zeroed, 1)
            for src, k in pieces:
                if len(src.shape) == 3:
                    src = src.rearrange("a b (k p) -> (a b k) p", p=P)
                elif len(src.shape) == 2:
                    src = src.rearrange("a (k p) -> (a k) p", p=P)
                else:
                    src = src.rearrange("(k p) -> k p", p=P)
                done = 0
                while done < k:
                    r, g = at % P, at // P
                    m = min(k - done, P - r)
                    act.dma_start(param_rows[r:r + m, g, :], src[done:done + m, :]).then_inc(p_loaded, 16)
                    loads += 1
                    at += m
                    done += m
            assert at == PCOLS
            assert loads == PARAM_LOADS
            act.dma_start(gates[:, 8:16, :].rearrange("p (t a) n -> p t (a n)", t=TT),
                           A["mem"].rearrange("a (t p) d -> p (a t) d", p=P)).then_inc(m_loaded, 16)
            act.dma_start(bfor[:, :, :].rearrange("p l h -> p (l h)"),
                           A["b_forget"].rearrange("l h -> (l h)").partition_broadcast(P)).then_inc(bf_loaded, 16)

            act.wait_ge(m_loaded, 16)
            for t in range(TT):
                act.activation(flat(sq)[:, t * DM:(t + 1) * DM], mtok[:, t, :], ACT.Square,
                               accum_out=msum[:, t:t + 1]).then_inc(m_sq, 1)
            act.wait_ge(m_sq, TT)
            act.activation(mmax[:, :], msum[:, :], ACT.Sqrt, scale=1.0 / DM, bias=EPS).then_inc(m_root, 1)
            for b in range(4):
                act.wait_ge(m_gain, 2 * b + 2)
                act.activation(mhi[:, 2 * b:2 * b + 2, :], gates[:, 16 + 2 * b:18 + 2 * b, :], ACT.Copy).then_inc(m_hi, 1)
            prime()

            with act.Fori(0, LAYERS) as l:
                c = Chunk(l * (LAYER_C // SLOTS), 0)
                g = Group(l * LAYER_G, 0)
                squares_of_stream(l * 6, l * 3)
                uhigh(l * 3)
                ffn(c, g, l * 2)
                c, g = c + FFN_C, g + FFN_G
                chunks(c, 1)
                squares_of_result(l * 6 + 1, c + (-1))
                chunks(c + 1, 3)
                squares_of_stream(l * 6 + 2, l * 3 + 1)
                uhigh(l * 3 + 1)
                chunks(c + 4, 5)
                act.wait_ge(wf_loaded, l * 16 + 16)
                act.activation(wfhi[:, :, :], wfor[:, :, :], ACT.Copy).then_inc(f_split, 1)
                act.wait_ge(f_biased, l + 1)
                act.activation(fabs[:, :, :], flog[:, :, :], ACT.Abs).then_inc(f_log, 1)
                act.wait_ge(f_log, l * 3 + 1)
                act.activation(fabs[:, :, :], fabs[:, :, :], ACT.Exp, scale=-1.0).then_inc(f_log, 1)
                act.wait_ge(f_log, l * 3 + 2)
                act.activation(fabs[:, :, :], fabs[:, :, :], ACT.Ln, bias=1.0).then_inc(f_log, 1)
                chunks(c + 9, 3)
                with act.Fori(0, NPAIR) as p:
                    I = l * NPAIR + p
                    cp = (c + 12).later(p * 3)
                    o = lambda branch: hhi[:, bass.ds(p + 4 * branch, 1), :].rearrange("p a n -> p (a n)")
                    chunks(cp, 2)
                    act.wait_ge(mem_max, I + 1)
                    for q in range(TT):
                        act.activation(mem_p[:, q * TOK:(q + 1) * TOK], bank[6][:, q * TOK:(q + 1) * TOK], ACT.Exp,
                                       bias=mmax[:, q:q + 1], accum_out=msum[:, q:q + 1]).then_inc(mem_exp, 1)
                    chunks(cp + 2, 2)
                    act.wait_ge(mem_tp, I + 1)
                    act.activation(mem_pT, bank[7][:, :], ACT.Copy).then_inc(mem_pt, 1)
                    chunks(cp + 4, 2)
                    head_high(I * 3 + 1, bank[6][:, 0:TOK], o(2))
                    chunks(cp + 6, 1)
                    act.wait_ge(sbz_full, I + 1)
                    act.activation(sb_e[:, 0, :], bank[2][:, 0:CAUSAL], ACT.Abs).then_inc(sb_act, 1)
                    act.activation(sb_e[:, 1, :], bank[3][:, 0:CAUSAL], ACT.Abs).then_inc(sb_act, 1)
                    act.wait_ge(sb_act, I * 4 + 2)
                    act.activation(sb_e, sb_e, ACT.Exp, scale=-1.0).then_inc(sb_act, 1)
                    act.wait_ge(sb_act, I * 4 + 3)
                    act.activation(sb_e, sb_e, ACT.Ln, bias=1.0).then_inc(sb_act, 1)
                    chunks(cp + 7, 1)
                    act.wait_ge(fx_max, I * 2 + 2)
                    for h in range(2):
                        for q, (a, b) in enumerate(((0, P), (P, CAUSAL))):
                            n = 2 * q + h
                            act.activation(fx_s[:, h, a:b], fx_s[:, h, a:b], ACT.Exp, bias=fmax[:, n:n + 1],
                                           accum_out=fsum[:, n:n + 1]).then_inc(fx_exp, 1)
                    chunks(cp + 8, 1)
                    act.wait_ge(sb_lw, I * 2 + 2)
                    act.activation(sb_w, sb_w, ACT.Exp).then_inc(sb_exp, 1)
                    chunks(cp + 9, 1)
                    act.wait_ge(fx_tp, I + 1)
                    for h in range(2):
                        act.activation(fx_pT[:, h, :], bank[2 + h][:, 0:CAUSAL], ACT.Copy).then_inc(fx_pt, 1)
                    chunks(cp + 10, 1)
                    head_high(I * 3 + 2, bank[4][:, 0:TOK], o(0))
                    chunks(cp + 11, 1)
                    head_high(I * 3 + 3, bank[5][:, 0:TOK], o(1))
                c, g = c + (12 + 12 * NPAIR), g + (12 + 12 * NPAIR)
                act.wait_ge(group_done, g.count(2))
                for n in range(4):
                    for b in range(3):
                        s = slice(8 * b + 2 * n, 8 * b + 2 * n + 2)
                        act.activation(gates[:, s, :], gates[:, s, :], ACT.Sigmoid).then_inc(sig_done, 1)
                    chunks(c + 3 * n, 3)
                    act.wait_ge(merged, l * 8 + (2 * n + 2))
                    s = slice(2 * n, 2 * n + 2)
                    act.activation(uhi[:, s, :], work[:, s, :], ACT.Copy).then_inc(mgh_done, 1)
                c, g = c + 12, g + 12
                chunks(c, KT)
                c = c + KT
                squares_of_result(l * 6 + 3, c + (-1))
                squares_of_stream(l * 6 + 4, l * 3 + 2)
                uhigh(l * 3 + 2)
                ffn(c, g, l * 2 + 1)
                squares_of_result(l * 6 + 5, c + (FFN_C - 1))

            V2, M2 = 3 * LAYERS, 3 * LAYERS
            squares_of_stream(n_conv[0], V2)
            uhigh(M2)
            with act.Fori(0, 2) as i:
                for f in range(4):
                    ci = c_conv.later(i * 3) + 3 * f
                    chunks(ci, 2)
                    tile = i * 4 + f
                    act.wait_ge(group_done, i * 12 + (g_conv + 3 * f + 2 + 2))
                    act.activation(sg[f % 2], hf[f % 2], ACT.Copy,
                                   scale=par[:, bass.ds(tile + (ACONV + 2 * KT), 1)]).then_inc(tap_done, 1)
                    chunks(ci + 2, 1)
                    act.wait_ge(group_done, i * 12 + (g_conv + 3 * f + 3 + 2))
                    act.activation(hhi[:, bass.ds(tile, 1), :].rearrange("p a n -> p (a n)"), hf[f % 2], ACT.Copy)\
                       .then_inc(hhi_done, 1)
            chunks(c_aout, KT)
            squares_of_stream(n_ffa[0], V2 + 1)
            uhigh(M2 + 1)
            conv_ffn(c_ffa, Group(0, g_ffa), 0, 0)
            squares_of_stream(n_h2[0], V2 + 2)
            uhigh(M2 + 2)
            uhigh(M2 + 3, hhi)
            chunks(c_kv, 2)
            act.wait_ge(group_done, g_kv + 2 + 2)
            act.activation(sq[:, 0:2, :], ckv, ACT.Square).then_inc(sq_done, 1)
            chunks(c_kv + 2, 1)
            take_root(n_kv[0], KVL)
            act.wait_ge(lat_done, 1)
            act.wait_ge(w_used, c_kv.count(3 + SLOTS))
            act.activation(uhi[:, 0:2, :], work[:, 0:2, :], ACT.Copy).then_inc(lat_hi, 1)
            chunks(c_dq, 4)
            act.wait_ge(group_done, g_dq + 4 + 2)
            for b in range(2):
                act.activation(sq[:, 2 * b:2 * b + 2, :], qlat[:, 2 * b:2 * b + 2, :], ACT.Square).then_inc(sq_done, 1)
            take_root(n_q[0], QL)
            act.wait_ge(lat_done, 2)
            act.activation(uhi[:, 2:6, :], work[:, 2:6, :], ACT.Copy).then_inc(lat_hi, 1)
            chunks(c_uqr, 4)

            def mla_exp(h):
                act.wait_ge(ls_max, 2 * h + 2)
                for q, (a, b) in enumerate(((0, P), (P, CAUSAL))):
                    act.activation(ls(h)[:, a:b], ls(h)[:, a:b], ACT.Exp, bias=lmax(h)[:, q:q + 1],
                                   accum_out=lsum(h)[:, q:q + 1]).then_inc(ls_exp, 1)

            def mla_pT(h):
                act.wait_ge(ls_tp, h + 1)
                act.activation(lpT(h), bank[4 + h % 2][:, 0:CAUSAL], ACT.Copy).then_inc(ls_pt, 1)

            def mla_high(h):
                act.wait_ge(la_full, h + 1)
                act.activation(hhi[:, h, :], bank[6 + h % 2][:, 0:TOK], ACT.Copy).then_inc(la_hi, 1)

            for p in range(5):
                if p < 4:
                    chunks(c_pairs + 2 * p, 1)
                if p > 0:
                    mla_exp(2 * p - 2)
                    mla_exp(2 * p - 1)
                    mla_pT(2 * p - 2)
                    mla_pT(2 * p - 1)
                if p < 4:
                    chunks(c_pairs + (2 * p + 1), 1)
                if p > 0:
                    mla_high(2 * p - 2)
                    mla_high(2 * p - 1)
            chunks(c_o, KT)
            squares_of_stream(n_ffb[0], V2 + 3)
            uhigh(M2 + 4)
            conv_ffn(c_ffb, Group(0, g_ffb), 1, 1)
            squares_of_stream(n_fin[0], V2 + 4)

        @block.vector
        def _(dve):
            def lo(c):
                if isinstance(c.rounds, int) and c.count() >= CHUNKS:
                    return
                dve.wait_ge(hi_ready, c.count(1))
                dve.tensor_tensor(wlo[c.slot][:, :], raw[c.slot][:, :], whi[c.slot][:, :].bitcast(F32), ALU.subtract)\
                   .then_inc(lo_ready, 1)

            def chunks(c, n):
                for j in range(n):
                    lo(c + (AHEAD + j))

            def done(c):
                dve.wait_ge(w_used, c.count(1 + SLOTS))

            def take_rstd(n):
                dve.wait_ge(root_done, n + 1)
                dve.reciprocal(rstd[:, :], root[:, :]).then_inc(rstd_done, 1)
                dve.wait_ge(rstd_done, n + 1)

            def add_normed(n, s_at, version, gain, a_at):
                for b in range(4):
                    dve.wait_ge(sq_done, s_at + (b + 1))
                    dve.tensor_copy(work[:, 2 * b:2 * b + 2, :], pair_bank(4 + b)).then_inc(acc_copied, 1)
                take_rstd(n)
                for b in range(5):
                    if b < 4:
                        dve.wait_ge(acc_copied, a_at + (b + 1))
                        for k in (2 * b, 2 * b + 1):
                            ins = dve.scalar_tensor_tensor(work[:, k, :], work[:, k, :], gain[:, k:k + 1], rstd[:, :],
                                                           ALU.mult, ALU.mult)
                        ins.then_inc(scaled, 1)
                    if b > 0:
                        s = slice(2 * b - 2, 2 * b)
                        dve.wait_ge(scaled, a_at + b)
                        dve.tensor_tensor(H[:, s, :], H[:, s, :], work[:, s, :], ALU.add).then_inc(h_ready, 1)

            def add_result(last):
                done(last)
                for b in range(4):
                    s = slice(2 * b, 2 * b + 2)
                    dve.tensor_tensor(H[:, s, :], pair_bank(4 + b), H[:, s, :], ALU.add).then_inc(h_ready, 1)

            def normed(gain):
                for b in range(4):
                    for k in (2 * b, 2 * b + 1):
                        ins = dve.scalar_tensor_tensor(work[:, k, :], H[:, k, :], gain[:, k:k + 1], rstd[:, :],
                                                       ALU.mult, ALU.mult)
                    ins.then_inc(un_done, 1)

            def down(c):
                chunks(c, 2)
                turns = (FT - 2) // 4
                last = isinstance(c.rounds, int) and c.count(FT) == CHUNKS
                with dve.Fori(0, turns - last) as i:
                    chunks((c + 2).later(i), 4)
                if last:
                    chunks((c + 2).later(turns - 1), 4)

            def ffn(c, g, use):
                with dve.Fori(0, FT // 2) as i:
                    for j in range(2):
                        chunks(c.later(i) + 2 * j, 2)
                        f = use * FT + (i * 2 + j)
                        dve.wait_ge(silu_done, f + 1)
                        dve.tensor_tensor(hf[j], bank[(g.k + j) % 2][:, TOK:2 * TOK], sg[j], ALU.mult).then_inc(group_done, 1)
                        dve.wait_ge(hhi_done, f + 1)
                        at = lambda t: t[:, bass.ds(i * 2 + j, 1), :].rearrange("p a n -> p (a n)")
                        dve.tensor_tensor(at(hlo), hf[j], at(hhi).bitcast(F32), ALU.subtract).then_inc(hlo_done, 1)
                down(c + 2 * FT)

            def conv_ffn(c, g, use, layer):
                taps = FCONV + layer * 6 * FT
                before_it = LAYERS * 2 * FT
                with dve.Fori(0, FT // 2) as i:
                    for j in range(2):
                        chunks(c.later(i) + 2 * j, 2)
                        f = i * 2 + (j + use * FT)
                        y = conv_y[j]
                        b = bank[(g.k + j) % 2]
                        dve.wait_ge(tap_done, f * 2 + (2 + KT))
                        for back in (1, 2):
                            for s in range(2):
                                a = s * TOK
                                if back == 2:
                                    dve.wait_ge(conv_done, f * 3 + (s + 1))
                                ins = dve.scalar_tensor_tensor(
                                    y[:, a + back:a + TOK], b[:, a:a + TOK - back],
                                    par[:, bass.ds(i * 2 + (taps + (2 - back) * 2 * FT + s * FT + j), 1)],
                                    y[:, a + back:a + TOK], ALU.mult, ALU.add)
                                ins.then_inc(group_done if (back, s) == (2, 1) else conv_done, 1)
                        dve.wait_ge(silu_done, f + (before_it + 1))
                        dve.wait_ge(group_done, i * 2 + (g.k + j + 3))
                        dve.tensor_tensor(hf[j], y[:, TOK:2 * TOK], sg[j], ALU.mult).then_inc(hid_done, 1)
                        dve.wait_ge(hhi_done, f + (before_it + KT + 1))
                        at = lambda t: t[:, bass.ds(i * 2 + j, 1), :].rearrange("p a n -> p (a n)")
                        dve.tensor_tensor(at(hlo), hf[j], at(hhi).bitcast(F32), ALU.subtract).then_inc(hlo_done, 1)
                down(c + 2 * FT)

            def head_low(count, src, hi_part, lo_part):
                dve.wait_ge(ohi_done, count)
                dve.tensor_tensor(lo_part, src, hi_part.bitcast(F32), ALU.subtract).then_inc(olo_done, 1)

            dve.sem_inc(lo_ready, SLOTS)
            dve.sem_inc(group_done, 2)
            dve.sem_inc(f_split, 2)
            dve.wait_ge(par_tp, 1)
            dve.tensor_copy(par[:, :], bank[3][:, :]).then_inc(par_ready, 1)
            dve.wait_ge(par_ready, 1)
            for at in (POST1, POST2):
                v = par[:, 0:LAYERS * LP].rearrange("p (l n) -> p l n", l=LAYERS)[:, :, at:at + KT]
                dve.tensor_scalar(v, v, 0.5, None, ALU.mult).then_inc(par_ready, 1)
            for b in range(4):
                dve.wait_ge(x_tp, b + 1)
                dve.tensor_copy(H[:, 2 * b:2 * b + 2, :], pair_bank(4 + b)).then_inc(h_ready, 1)
            dve.wait_ge(m_root, 1)
            dve.reciprocal(mrec[:, :], mmax[:, :]).then_inc(m_rstd, 1)
            dve.wait_ge(m_rstd, 1)
            for t in range(TT):
                dve.tensor_scalar(mtok[:, t, :], mtok[:, t, :], mrec[:, t:t + 1], None, ALU.mult).then_inc(m_scaled, 1)
            for k in range(KT):
                dve.wait_ge(m_tp, k // 2 + 1)
                dve.tensor_scalar(gates[:, 16 + k, :], bank[4 + k // 2][:, (k % 2) * TOK:(k % 2 + 1) * TOK],
                                  par[:, MEMG + k:MEMG + k + 1], None, ALU.mult).then_inc(m_gain, 1)
            for b in range(4):
                dve.wait_ge(m_hi, b + 1)
                s = slice(2 * b, 2 * b + 2)
                dve.tensor_tensor(mlo[:, s, :], gates[:, 16 + 2 * b:18 + 2 * b, :], mhi[:, s, :].bitcast(F32), ALU.subtract)\
                   .then_inc(m_lo, 1)
            for n in range(AHEAD):
                lo(Chunk(0, n))

            with dve.Fori(0, LAYERS) as l:
                c = Chunk(l * (LAYER_C // SLOTS), 0)
                g = Group(l * LAYER_G, 0)
                dve.wait_ge(par_ready, 3)
                dve.tensor_copy(lp[:, :], par[:, bass.ds(l * LP, LP)]).then_inc(lp_ready, 1)
                dve.wait_ge(lp_ready, l + 1)
                gain = lambda at: lp[:, at:at + KT]
                take_rstd(l * 6)
                normed(gain(PRE1))
                ffn(c, g, l * 2)
                c, g = c + FFN_C, g + FFN_G
                chunks(c, 1)

                def take_mem(n):
                    done(c + n)
                    src = bank[n % 2][:, 0:TOK]
                    if n < 4:
                        dve.tensor_copy(kmem[:, n, :], src).then_inc(group_done, 1)
                    elif n < 8:
                        dve.tensor_copy(vmem[:, :, n - 4, :], src.rearrange("p (t d) -> p t d", t=TT)).then_inc(group_done, 1)
                    else:
                        dve.tensor_scalar(qmem[:, n - 8, :], src, MEM_SCALE, None, ALU.mult).then_inc(group_done, 1)

                add_normed(l * 6 + 1, l * 24 + 4, l * 3 + 1, gain(POST1), l * 12)
                take_mem(0)
                for n in range(1, 4):
                    chunks(c + n, 1)
                    take_mem(n)
                take_rstd(l * 6 + 2)
                normed(gain(PREM))
                for n in range(4, 8):
                    chunks(c + n, 1)
                    take_mem(n)
                chunks(c + 8, 1)
                dve.wait_ge(f_split, l * 2 + 3)
                dve.tensor_tensor(wflo[:, :, :], wfor[:, :, :], wfhi[:, :, :].bitcast(F32), ALU.subtract).then_inc(f_split, 1)
                take_mem(8)
                dve.wait_ge(f_full, l + 1)
                dve.wait_ge(bf_loaded, 16)
                dve.tensor_tensor(flog[:, :, :], bank[3][:, 0:16].rearrange("p (t h) -> p t h", t=TT),
                                  bfor[:, bass.ds(l, 1), :].to_broadcast([P, TT, 8]), ALU.add).then_inc(f_biased, 1)
                dve.wait_ge(f_log, l * 3 + 3)
                dve.scalar_tensor_tensor(flog[:, :, :], flog[:, :, :], 0.0, fabs[:, :, :], ALU.min, ALU.subtract)\
                   .then_inc(f_ready, 1)
                for n in range(9, 11):
                    chunks(c + n, 1)
                    take_mem(n)
                dve.wait_ge(c_full, l + 1)
                dve.tensor_copy(ctok[:, :, :], bank[3][:, 32:48].rearrange("p (t h) -> p t h", t=TT)).then_inc(c_ready, 1)
                dve.tensor_copy(crow[:, :], bank[3][0:8, 64:64 + TOK]).then_inc(c_ready, 1)
                chunks(c + 11, 1)
                take_mem(11)
                with dve.Fori(0, NPAIR) as p:
                    I = l * NPAIR + p
                    cp = (c + 12).later(p * 3)
                    o = lambda t, branch: t[:, bass.ds(p + 4 * branch, 1), :].rearrange("p a n -> p (a n)")

                    def gate(n):
                        done(cp + (6 + n))
                        dve.tensor_scalar(gates[:, bass.ds(p * 6 + n, 1), :].rearrange("p a n -> p (a n)"),
                                          bank[n % 2][:, 0:TOK], lp[:, bass.ds(p * 6 + (BGATE + n), 1)], None, ALU.add)\
                           .then_inc(group_done, 1)

                    dve.tensor_copy(qm1[:, :], qmem[:, bass.ds(p, 1), :].rearrange("p a n -> p (a n)")).then_inc(mem_staged, 1)
                    dve.tensor_copy(vm1[:, :, :], vmem[:, :, bass.ds(p, 1), :].rearrange("p t a d -> p t (a d)"))\
                       .then_inc(mem_staged, 1)
                    chunks(cp, 1)
                    dve.wait_ge(c_ready, l * 2 + 2)
                    for h in range(2):
                        dve.tensor_scalar(cpair[:, h, :], crow[:, :], cst[0:8, bass.ds(p * 2 + (C_NEG8 + h), 1)], None,
                                          ALU.mult).then_inc(c_pair, 1)
                    done(cp)
                    dve.tensor_scalar(qs, bank[0][:, 0:TOK], SB_SCALE, None, ALU.mult).then_inc(group_done, 1)
                    chunks(cp + 1, 1)
                    dve.wait_ge(mem_full, I + 1)
                    dve.tensor_reduce(mmax[:, :], pair_bank(6), AX_X, ALU.max, negate=True).then_inc(mem_max, 1)
                    done(cp + 1)
                    dve.tensor_copy(ks, bank[1][:, 0:TOK]).then_inc(group_done, 1)
                    chunks(cp + 2, 1)
                    dve.wait_ge(mem_exp, I * 2 + 2)
                    dve.reciprocal(mrec[:, :], msum[:, :]).then_inc(mem_rec, 1)
                    dve.wait_ge(mem_rec, I + 1)
                    for q in range(TT):
                        ins = dve.tensor_scalar(mem_p[:, q * TOK:(q + 1) * TOK], mem_p[:, q * TOK:(q + 1) * TOK],
                                                mrec[:, q:q + 1], None, ALU.mult)
                    ins.then_inc(mem_norm, 1)
                    done(cp + 2)
                    dve.tensor_copy(vs, bank[0][:, 0:TOK]).then_inc(group_done, 1)
                    chunks(cp + 3, 1)
                    done(cp + 3)
                    dve.tensor_scalar(qf, bank[1][:, 0:TOK], SB_SCALE, None, ALU.mult).then_inc(group_done, 1)
                    chunks(cp + 4, 1)
                    done(cp + 4)
                    dve.tensor_copy(kf, bank[0][:, 0:TOK]).then_inc(group_done, 1)
                    chunks(cp + 5, 1)
                    head_low(I * 3 + 1, bank[6][:, 0:TOK], o(hhi, 2), o(hlo, 2))
                    done(cp + 5)
                    dve.tensor_copy(vf, bank[1][:, 0:TOK]).then_inc(group_done, 1)
                    chunks(cp + 6, 1)
                    dve.wait_ge(sb_act, I * 4 + 4)
                    for h in range(2):
                        ins = dve.scalar_tensor_tensor(sb_sp[:, h, :], bank[2 + h][:, 0:CAUSAL], 0.0, sb_e[:, h, :],
                                                       ALU.max, ALU.add)
                    ins.then_inc(sb_dve, 1)
                    dve.wait_ge(sb_dve, I * 2 + 1)
                    for h in range(2):
                        ins = dve.tensor_tensor(sb_w[:, h, :], bank[2 + h][:, 0:CAUSAL], sb_sp[:, h, :], ALU.subtract)
                    ins.then_inc(sb_dve, 1)
                    gate(0)
                    chunks(cp + 7, 1)
                    dve.wait_ge(fxz_full, I + 1)
                    for h in range(2):
                        for q, (a, b) in enumerate(((0, P), (P, CAUSAL))):
                            dve.scalar_tensor_tensor(fx_s[:, h, a:b], bank[4 + h][:, a:b],
                                                     ctok[:, q, bass.ds(p * 2 + h, 1)], hide[:, a:b],
                                                     ALU.add, ALU.add).then_inc(fx_add, 1)
                    dve.wait_ge(fx_add, I * 4 + 4)
                    for q, (a, b) in enumerate(((0, P), (P, CAUSAL))):
                        dve.tensor_reduce(fmax[:, 2 * q:2 * q + 2], fx_s[:, :, a:b], AX_X, ALU.max, negate=True)\
                           .then_inc(fx_max, 1)
                    gate(1)
                    chunks(cp + 8, 1)
                    dve.wait_ge(sb_cum, I + 1)
                    for h in range(2):
                        dve.tensor_tensor(sb_w[:, h, :], sb_w[:, h, :], bank[6 + h][:, 0:CAUSAL], ALU.subtract)\
                           .then_inc(sb_lw, 1)
                    dve.wait_ge(fx_exp, I * 4 + 4)
                    dve.reciprocal(frec[:, :], fsum[:, :]).then_inc(fx_rec, 1)
                    dve.wait_ge(fx_rec, I + 1)
                    for h in range(2):
                        for q, (a, b) in enumerate(((0, P), (P, CAUSAL))):
                            n = 2 * q + h
                            ins = dve.tensor_scalar(fx_s[:, h, a:b], fx_s[:, h, a:b], frec[:, n:n + 1], None, ALU.mult)
                    ins.then_inc(fx_norm, 1)
                    gate(2)
                    chunks(cp + 9, 1)
                    gate(3)
                    chunks(cp + 10, 1)
                    head_low(I * 3 + 2, bank[4][:, 0:TOK], o(hhi, 0), o(hlo, 0))
                    gate(4)
                    chunks(cp + 11, 1)
                    head_low(I * 3 + 3, bank[5][:, 0:TOK], o(hhi, 1), o(hlo, 1))
                    gate(5)
                c, g = c + (12 + 12 * NPAIR), g + (12 + 12 * NPAIR)
                for n in range(4):
                    s = slice(2 * n, 2 * n + 2)
                    for b in range(3):
                        chunks(c + (3 * n + b), 1)
                        dve.wait_ge(sig_done, l * 12 + (3 * n + b + 1))
                        done(c + (3 * n + b))
                        dst = work[:, s, :] if b == 0 else sq[:, 2 * b:2 * b + 2, :]
                        dve.tensor_tensor(dst, pair_bank((3 * n + b) % 2), gates[:, 8 * b + 2 * n:8 * b + 2 * n + 2, :],
                                          ALU.mult).then_inc(group_done, 1)
                        if b > 0:
                            dve.wait_ge(group_done, g.count(3 * n + b + 3))
                            if b == 2:
                                dve.wait_ge(merged, l * 8 + (2 * n + 1))
                            dve.tensor_tensor(work[:, s, :], work[:, s, :], dst, ALU.add).then_inc(merged, 1)
                    dve.wait_ge(mgh_done, l * 4 + (n + 1))
                    dve.tensor_tensor(ulo[:, s, :], work[:, s, :], uhi[:, s, :].bitcast(F32), ALU.subtract).then_inc(mgl_done, 1)
                c, g = c + 12, g + 12
                chunks(c, KT)
                c = c + KT
                add_normed(l * 6 + 3, l * 24 + 12, l * 3 + 2, gain(POSTM), l * 12 + 4)
                take_rstd(l * 6 + 4)
                normed(gain(PRE2))
                ffn(c, g, l * 2 + 1)
                add_normed(l * 6 + 5, l * 24 + 20, l * 3 + 3, gain(POST2), l * 12 + 8)

            pgain = lambda at: par[:, at:at + KT]
            HID = LAYERS * 2 * FT
            take_rstd(n_conv[0])
            normed(pgain(AMIX))
            with dve.Fori(0, 2) as i:
                for f in range(4):
                    ci = c_conv.later(i * 3) + 3 * f
                    G = i * 12 + (g_conv + 3 * f + 2)
                    tile = i * 4 + f
                    b0 = 3 * f
                    chunks(ci, 1)
                    done(ci)
                    dve.tensor_copy(part(4), bank[b0 % 2][:, 0:TOK]).then_inc(group_done, 1)
                    chunks(ci + 1, 1)
                    done(ci + 1)
                    dve.wait_ge(group_done, G + 1)
                    dve.tensor_tensor(hf[f % 2], bank[(b0 + 1) % 2][:, 0:TOK], part(4), ALU.mult).then_inc(group_done, 1)
                    chunks(ci + 2, 1)
                    dve.wait_ge(tap_done, tile + 1)
                    for back in (1, 2):
                        if back == 2:
                            dve.wait_ge(y_done, tile * 2 + 1)
                        dve.scalar_tensor_tensor(sg[f % 2][:, back:TOK], hf[f % 2][:, 0:TOK - back],
                                                 par[:, bass.ds(tile + (ACONV + (2 - back) * KT), 1)],
                                                 sg[f % 2][:, back:TOK], ALU.mult, ALU.add).then_inc(y_done, 1)
                    done(ci + 2)
                    dve.wait_ge(y_done, tile * 2 + 2)
                    dve.tensor_tensor(hf[f % 2], bank[(b0 + 2) % 2][:, 0:TOK], sg[f % 2], ALU.mult).then_inc(group_done, 1)
                    dve.wait_ge(hhi_done, tile + (HID + 1))
                    at = lambda t: t[:, bass.ds(tile, 1), :].rearrange("p a n -> p (a n)")
                    dve.tensor_tensor(at(hlo), hf[f % 2], at(hhi).bitcast(F32), ALU.subtract).then_inc(hlo_done, 1)
            chunks(c_aout, KT)
            add_result(c_aout + (KT - 1))
            take_rstd(n_ffa[0])
            normed(pgain(FFNN))
            conv_ffn(c_ffa, Group(0, g_ffa), 0, 0)
            add_result(c_ffa + (FFN_C - 1))
            take_rstd(n_h2[0])
            normed(pgain(KVIN))
            dve.wait_ge(ulo_done, 4 * (3 * LAYERS + 3))
            normed(pgain(BMIX))
            RP = 2 * KT

            def rotate(n, raw_tile, dst, scale):
                dve.tensor_tensor(dst, raw_tile, cosine, ALU.mult).then_inc(rp_cos, 1)
                dve.wait_ge(rp_swap, n + 1)
                dve.tensor_tensor(part(4), bank[3][:, 0:TOK], sine, ALU.mult).then_inc(rp_sin, 1)
                dve.wait_ge(rp_cos, n + 1)
                dve.wait_ge(rp_sin, n + 1)
                dve.tensor_tensor(dst, dst, part(4), ALU.add).then_inc(rp_done, 1)

            for n in range(2):
                chunks(c_kv + n, 1)
                done(c_kv + n)
                dve.tensor_copy(ckv[:, n, :], bank[(g_kv + n) % 2][:, 0:TOK]).then_inc(group_done, 1)
            chunks(c_kv + 2, 1)
            done(c_kv + 2)
            dve.tensor_copy(kr_raw, bank[(g_kv + 2) % 2][:, 0:TOK]).then_inc(group_done, 1)
            dve.wait_ge(group_done, g_kv + 3 + 2)
            rotate(0, kr_raw, kr, None)
            take_rstd(n_kv[0])
            dve.wait_ge(ulo_done, 4 * (3 * LAYERS + 4))
            for k in range(2):
                ins = dve.scalar_tensor_tensor(work[:, k, :], ckv[:, k, :], par[:, KVN + k:KVN + k + 1], rstd[:, :],
                                               ALU.mult, ALU.mult)
            ins.then_inc(lat_done, 1)
            dve.wait_ge(lat_hi, 1)
            dve.tensor_tensor(ulo[:, 0:2, :], work[:, 0:2, :], uhi[:, 0:2, :].bitcast(F32), ALU.subtract).then_inc(lat_lo, 1)
            for n in range(4):
                chunks(c_dq + n, 1)
                done(c_dq + n)
                dve.tensor_copy(qlat[:, n, :], bank[(g_dq + n) % 2][:, 0:TOK]).then_inc(group_done, 1)
            take_rstd(n_q[0])
            for k in range(4):
                ins = dve.scalar_tensor_tensor(work[:, 2 + k, :], qlat[:, k, :], par[:, BQ + k:BQ + k + 1], rstd[:, :],
                                               ALU.mult, ALU.mult)
            ins.then_inc(lat_done, 1)
            dve.wait_ge(lat_hi, 2)
            dve.tensor_tensor(ulo[:, 2:6, :], work[:, 2:6, :], uhi[:, 2:6, :].bitcast(F32), ALU.subtract).then_inc(lat_lo, 1)
            for p in range(4):
                chunks(c_uqr + p, 1)
                done(c_uqr + p)
                dve.tensor_scalar(part(p % 2), bank[(g_uqr + p) % 2][:, 0:TOK], MLA_SCALE, None, ALU.mult).then_inc(group_done, 1)
                dve.wait_ge(group_done, g_uqr + p + 3)
                rotate(p + 1, part(p % 2), qr[:, p, :], None)

            def mla_max(h):
                dve.wait_ge(ls_full, h + 1)
                dve.tensor_tensor(ls(h), bank[2 + h % 2][:, 0:CAUSAL], hide, ALU.add).then_inc(ls_add, 1)
                dve.wait_ge(ls_add, h + 1)
                for q, (a, b) in enumerate(((0, P), (P, CAUSAL))):
                    dve.tensor_reduce(lmax(h)[:, q:q + 1], ls(h)[:, a:b], AX_X, ALU.max, negate=True).then_inc(ls_max, 1)

            def mla_norm(h):
                dve.wait_ge(ls_exp, 2 * h + 2)
                dve.reciprocal(lrec(h), lsum(h)).then_inc(ls_rec, 1)
                dve.wait_ge(ls_rec, h + 1)
                for q, (a, b) in enumerate(((0, P), (P, CAUSAL))):
                    ins = dve.tensor_scalar(ls(h)[:, a:b], ls(h)[:, a:b], lrec(h)[:, q:q + 1], None, ALU.mult)
                ins.then_inc(ls_norm, 1)

            def mla_low(h):
                dve.wait_ge(la_hi, h + 1)
                dve.tensor_tensor(hlo[:, h, :], bank[6 + h % 2][:, 0:TOK], hhi[:, h, :].bitcast(F32), ALU.subtract)\
                   .then_inc(la_lo, 1)

            for p in range(5):
                if p < 4:
                    chunks(c_pairs + 2 * p, 1)
                if p > 0:
                    for h in (2 * p - 2, 2 * p - 1):
                        mla_norm(h)
                if p < 4:
                    done(c_pairs + 2 * p)
                    G = g_pairs + 3 * p
                    dve.tensor_copy(kn[:, 2 * p:2 * p + 2, :], pair_bank(G % 2)).then_inc(group_done, 1)
                    dve.tensor_copy(vn[:, :, 2 * p:2 * p + 2, :],
                                    bank[(G + 1) % 2][:, :].rearrange("p (t h d) -> p t h d", t=TT, h=2)).then_inc(group_done, 1)
                    chunks(c_pairs + (2 * p + 1), 1)
                    done(c_pairs + (2 * p + 1))
                    dve.tensor_scalar(qn[:, 2 * p:2 * p + 2, :], pair_bank((G + 2) % 2), MLA_SCALE, None, ALU.mult)\
                       .then_inc(group_done, 1)
                if p > 0:
                    mla_low(2 * p - 2)
                    mla_low(2 * p - 1)
                if p < 4:
                    mla_max(2 * p)
                    mla_max(2 * p + 1)
            chunks(c_o, KT)
            add_result(c_o + (KT - 1))
            take_rstd(n_ffb[0])
            normed(pgain(FFNN + KT))
            conv_ffn(c_ffb, Group(0, g_ffb), 1, 1)
            add_result(c_ffb + (FFN_C - 1))
            take_rstd(n_fin[0])
            normed(pgain(FINAL))
            for t in range(TT):
                for b in range(2):
                    dve.wait_ge(y_tp, 2 * t + b + 1)
                    for e in range(2):
                        dve.tensor_copy(gates[:, 4 * t + 2 * b + e, :], bank[4 + 2 * t + b][:, e * TOK:(e + 1) * TOK])\
                           .then_inc(y_copied, 1)

        @block.tensor
        def _(pe):
            def start_chunk(c):
                pe.wait_ge(lo_ready, c.count(1 + SLOTS))

            def free_bank(g):
                pe.wait_ge(group_done, g.count(1))
                return bank[g.k % 2]

            def mm3(dst, w_hi, w_lo, x_hi, x_lo, start, stop, **kw):
                pe.matmul(dst, w_hi, x_hi, start=start, stop=False, **kw)
                pe.matmul(dst, w_hi, x_lo, start=False, stop=False, **kw)
                return pe.matmul(dst, w_lo, x_hi, start=False, stop=stop, **kw)

            def project(dst, c, kts, xh, xl, width=P, at=0):
                for k in range(kts):
                    s = slice(k * width + at, k * width + at + P)
                    ins = mm3(dst, whi[c.slot][:, s], wlo[c.slot][:, s], xh[:, k, :], xl[:, k, :], k == 0, k == kts - 1)
                return ins

            def project_tokens(dst, c, kts, xh, xl, width=P, at=0):
                for t in range(TT):
                    rows = slice(t * P, (t + 1) * P)
                    for k in range(kts):
                        s = slice(k * width + at, k * width + at + P)
                        pe.matmul(dst(t), xh[:, k, rows], whi[c.slot][:, s], start=(k == 0), stop=False)
                        pe.matmul(dst(t), xl[:, k, rows], whi[c.slot][:, s], start=False, stop=False)
                        ins = pe.matmul(dst(t), xh[:, k, rows], wlo[c.slot][:, s], start=False, stop=(k == kts - 1))
                return ins

            def sum_squares(s_at, tiles):
                for k in range(tiles):
                    if k % 2 == 0:
                        pe.wait_ge(sq_done, s_at + (k // 2 + 1))
                    ins = pe.matmul(bank[2][:, 0:TOK], ones, sq[:, k, :], start=(k == 0), stop=(k == tiles - 1))
                ins.then_inc(ss_full, 1)

            def ffn(c, g, hidden, m):
                with pe.Fori(0, FT // 2) as i:
                    for j in range(2):
                        if j == 0:
                            pe.wait_ge(ulo_done, m * 4 + 4)
                        ci = c.later(i) + 2 * j
                        b = free_bank(g.later(i * 2) + j)
                        start_chunk(ci)
                        project(b[:, 0:TOK], ci, KT, uhi, ulo).then_inc(w_used, 1)
                        start_chunk(ci + 1)
                        project(b[:, TOK:2 * TOK], ci + 1, KT, uhi, ulo).then_inc(w_used, 1)
                d = c + 2 * FT

                def rows(cd, tile, first, last):
                    start_chunk(cd)
                    for n in range(KT):
                        s = slice(n * P, (n + 1) * P)
                        ins = mm3(bank[4 + n // 2][:, (n % 2) * TOK:(n % 2 + 1) * TOK], whi[cd.slot][:, s], wlo[cd.slot][:, s],
                                  tile(hhi), tile(hlo), first and n % 2 == 0, last, skip_group_check=True)
                    ins.then_inc(w_used, 1)

                pe.wait_ge(hlo_done, hidden + FT)
                for k in range(2):
                    rows(d + k, lambda t: t[:, k, :], k == 0, False)
                with pe.Fori(0, (FT - 2) // 4) as i:
                    for j in range(4):
                        rows((d + (2 + j)).later(i),
                             lambda t: t[:, bass.ds(i * 4 + (2 + j), 1), :].rearrange("p a n -> p (a n)"), False, True)

            def turn(src, dst):
                return pe.transpose(dst, src, ident)

            pe.sem_inc(w_used, SLOTS)
            pe.wait_ge(cst_loaded, 16)
            pe.wait_ge(x_loaded, 16)
            xtok = work[:, :, :].rearrange("p (t a) n -> p t (a n)", t=TT)
            for k in range(KT):
                for t in range(TT):
                    ins = turn(xtok[:, t, k * P:(k + 1) * P], bank[4 + k // 2][:, (k % 2) * TOK + t * P:(k % 2) * TOK + (t + 1) * P])
                if k % 2:
                    ins.then_inc(x_tp, 1)
            pe.wait_ge(p_loaded, 16 * PARAM_LOADS)
            for n in range(4):
                ins = turn(param_rows[:, n, :], bank[3][:, n * P:(n + 1) * P])
            ins.then_inc(par_tp, 1)
            pe.wait_ge(m_scaled, TT)
            for k in range(KT):
                if k % 2 == 0:
                    pe.wait_ge(h_ready, k // 2 + 1)
                for t in range(TT):
                    ins = turn(mtok[:, t, k * P:(k + 1) * P], bank[4 + k // 2][:, (k % 2) * TOK + t * P:(k % 2) * TOK + (t + 1) * P])
                if k % 2:
                    ins.then_inc(m_tp, 1)

            with pe.Fori(0, LAYERS) as l:
                c = Chunk(l * (LAYER_C // SLOTS), 0)
                g = Group(l * LAYER_G, 0)
                sum_squares(l * 24, KT)
                ffn(c, g, l * (2 * FT), l * 3)
                c, g = c + FFN_C, g + FFN_G
                pe.wait_ge(m_lo, 4)

                def mem_key(n):
                    b = free_bank(g + n)
                    start_chunk(c + n)
                    project(b[:, 0:TOK], c + n, KT, mhi, mlo).then_inc(w_used, 1)

                mem_key(0)
                sum_squares(l * 24 + 4, KT)
                for n in range(1, 4):
                    mem_key(n)
                sum_squares(l * 24 + 8, KT)
                for n in range(4, 8):
                    b = free_bank(g + n)
                    start_chunk(c + n)
                    project_tokens(lambda t: b[:, t * P:(t + 1) * P], c + n, KT, mhi, mlo).then_inc(w_used, 1)
                pe.wait_ge(ulo_done, l * 12 + 8)

                def mem_query(n):
                    b = free_bank(g + n)
                    start_chunk(c + n)
                    project(b[:, 0:TOK], c + n, KT, uhi, ulo).then_inc(w_used, 1)

                mem_query(8)
                pe.wait_ge(f_split, l * 2 + 4)
                for t in range(TT):
                    rows_t = slice(t * P, (t + 1) * P)
                    for k in range(KT):
                        dst = bank[3][:, t * 8:(t + 1) * 8]
                        pe.matmul(dst, uhi[:, k, rows_t], wfhi[:, k, :], start=(k == 0), stop=False)
                        pe.matmul(dst, ulo[:, k, rows_t], wfhi[:, k, :], start=False, stop=False)
                        ins = pe.matmul(dst, uhi[:, k, rows_t], wflo[:, k, :], start=False, stop=(k == KT - 1))
                ins.then_inc(f_full, 1)
                mem_query(9)
                mem_query(10)
                pe.wait_ge(f_ready, l + 1)
                pe.matmul(bank[3][:, 32:40], up_to, flog[:, 0, :], start=True, stop=True)
                pe.matmul(bank[3][:, 40:48], up_to, flog[:, 1, :], start=True, stop=False)
                pe.matmul(bank[3][:, 40:48], ones, flog[:, 0, :], start=False, stop=True)
                pe.matmul(bank[3][0:8, 64:64 + P], flog[:, 0, :], up_to, start=True, stop=True)
                pe.matmul(bank[3][0:8, 64 + P:64 + TOK], flog[:, 1, :], up_to, start=True, stop=False)
                pe.matmul(bank[3][0:8, 64 + P:64 + TOK], flog[:, 0, :], ones, start=False, stop=True).then_inc(c_full, 1)
                mem_query(11)
                with pe.Fori(0, NPAIR) as p:
                    I = l * NPAIR + p
                    cp = (c + 12).later(p * 3)
                    gp = (g + 12).later(p * 12)

                    def gate(n):
                        b = free_bank(gp + (6 + n))
                        start_chunk(cp + (6 + n))
                        project(b[:, 0:TOK], cp + (6 + n), KT, uhi, ulo).then_inc(w_used, 1)

                    def feature_chunk(n):
                        b = free_bank(gp + n)
                        start_chunk(cp + n)
                        project(b[:, 0:TOK], cp + n, KT, uhi, ulo).then_inc(w_used, 1)

                    def token_chunk(n):
                        b = free_bank(gp + n)
                        start_chunk(cp + n)
                        project_tokens(lambda t: b[:, t * P:(t + 1) * P], cp + n, KT, uhi, ulo).then_inc(w_used, 1)

                    def weighted_values(dst, v, w, h):
                        f = slice(h * HD, (h + 1) * HD)
                        pe.matmul(dst[f, 0:TOK], v[:, h * HD:(h + 1) * HD], w[:, h, 0:TOK], start=True, stop=False)
                        return pe.matmul(dst[f, P:TOK], v[:, P + h * HD:P + (h + 1) * HD], w[:, h, TOK:CAUSAL],
                                         start=False, stop=True)

                    feature_chunk(0)
                    pe.wait_ge(mem_staged, I * 2 + 2)
                    for q in range(TT):
                        ins = pe.matmul(bank[6][:, q * TOK:(q + 1) * TOK], qm1[:, q * P:(q + 1) * P],
                                        kmem[:, bass.ds(p, 1), :].rearrange("p a n -> p (a n)"), start=True, stop=True)
                    ins.then_inc(mem_full, 1)
                    feature_chunk(1)
                    token_chunk(2)
                    pe.wait_ge(mem_norm, I + 1)
                    for q in range(TT):
                        for k in range(TT):
                            ins = turn(mem_p[:, q * TOK + k * P:q * TOK + (k + 1) * P],
                                       bank[7][:, k * TOK + q * P:k * TOK + (q + 1) * P])
                    ins.then_inc(mem_tp, 1)
                    feature_chunk(3)
                    feature_chunk(4)
                    pe.wait_ge(mem_pt, I + 1)
                    for k in range(TT):
                        ins = pe.matmul(bank[6][:, 0:TOK], vm1[:, k, :], mem_pT[:, k * TOK:(k + 1) * TOK],
                                        start=(k == 0), stop=(k == TT - 1))
                    ins.then_inc(o_full, 1)
                    token_chunk(5)
                    pe.wait_ge(group_done, gp.count(2 + 2))
                    for h in range(2):
                        f = slice(h * HD, (h + 1) * HD)
                        pe.matmul(bank[2 + h][:, 0:TOK], ks[f, 0:P], qs[f, 0:TOK], start=True, stop=True)
                        ins = pe.matmul(bank[2 + h][:, TOK:CAUSAL], ks[f, P:TOK], qs[f, P:TOK], start=True, stop=True)
                    ins.then_inc(sbz_full, 1)
                    gate(0)
                    pe.wait_ge(group_done, gp.count(5 + 2))
                    pe.wait_ge(c_pair, I * 2 + 2)
                    pe.wait_ge(olo_done, I * 3 + 1)
                    for h in range(2):
                        f = slice(h * HD, (h + 1) * HD)
                        pe.matmul(bank[4 + h][:, 0:P], qf[f, 0:P], kf[f, 0:P], start=True, stop=False)
                        pe.matmul(bank[4 + h][:, 0:P], ones[0:8, :], cpair[:, h, 0:P], start=False, stop=True)
                        pe.matmul(bank[4 + h][:, P:CAUSAL], qf[f, P:TOK], kf[f, 0:TOK], start=True, stop=False)
                        ins = pe.matmul(bank[4 + h][:, P:CAUSAL], ones[0:8, :], cpair[:, h, :], start=False, stop=True)
                    ins.then_inc(fxz_full, 1)
                    gate(1)
                    pe.wait_ge(sb_masked, I + 1)
                    for h in range(2):
                        pe.matmul(bank[6 + h][:, 0:TOK], later_keys, sb_sp[:, h, 0:TOK], start=True, stop=False)
                        pe.matmul(bank[6 + h][:, P:TOK], ones, sb_sp[:, h, TOK:CAUSAL], start=False, stop=True)
                        ins = pe.matmul(bank[6 + h][:, TOK:CAUSAL], later_keys, sb_sp[:, h, TOK:CAUSAL], start=True, stop=True)
                    ins.then_inc(sb_cum, 1)
                    gate(2)
                    pe.wait_ge(fx_norm, I + 1)
                    for h in range(2):
                        for n in range(3):
                            ins = turn(fx_s[:, h, n * P:(n + 1) * P], bank[2 + h][:, n * P:(n + 1) * P])
                    ins.then_inc(fx_tp, 1)
                    gate(3)
                    pe.wait_ge(sb_ready, I + 1)
                    for h in range(2):
                        ins = weighted_values(bank[4], vs, sb_w, h)
                    ins.then_inc(o_full, 1)
                    gate(4)
                    pe.wait_ge(fx_pt, I * 2 + 2)
                    for h in range(2):
                        ins = weighted_values(bank[5], vf, fx_pT, h)
                    ins.then_inc(o_full, 1)
                    gate(5)
                c, g = c + (12 + 12 * NPAIR), g + (12 + 12 * NPAIR)
                pe.wait_ge(olo_done, l * (3 * NPAIR) + 3 * NPAIR)
                for n in range(4):
                    for br in range(3):
                        m = 3 * n + br
                        b = free_bank(g + m)
                        start_chunk(c + m)
                        heads = slice(4 * br, 4 * br + 4)
                        for t in range(2):
                            ins = project(b[:, t * TOK:(t + 1) * TOK], c + m, 4, hhi[:, heads, :], hlo[:, heads, :], 2 * P, t * P)
                        ins.then_inc(w_used, 1)
                c, g = c + 12, g + 12
                pe.wait_ge(mgl_done, l * 4 + 4)

                def to_stream(c, xh, xl):
                    for n in range(KT):
                        start_chunk(c + n)
                        project(bank[4 + n // 2][:, (n % 2) * TOK:(n % 2 + 1) * TOK], c + n, KT, xh, xl).then_inc(w_used, 1)

                to_stream(c, uhi, ulo)
                c = c + KT
                sum_squares(l * 24 + 12, KT)
                sum_squares(l * 24 + 16, KT)
                ffn(c, g, l * (2 * FT) + FT, l * 3 + 2)
                sum_squares(l * 24 + 20, KT)

            M2 = 3 * LAYERS
            HID = LAYERS * 2 * FT
            sum_squares(n_conv[1], KT)
            pe.wait_ge(ulo_done, M2 * 4 + 4)
            with pe.Fori(0, 2) as i:
                for n in range(12):
                    cn = c_conv.later(i * 3) + n
                    b = free_bank(Group(i * 12 + g_conv, n))
                    start_chunk(cn)
                    project(b[:, 0:TOK], cn, KT, uhi, ulo).then_inc(w_used, 1)
            pe.wait_ge(hlo_done, HID + KT)
            to_stream(c_aout, hhi, hlo)
            sum_squares(n_ffa[1], KT)
            ffn(c_ffa, Group(0, g_ffa), HID + KT, M2 + 1)
            sum_squares(n_h2[1], KT)
            pe.wait_ge(ulo_done, M2 * 4 + 12)
            for n in range(3):
                b = free_bank(Group(0, g_kv + n))
                start_chunk(c_kv + n)
                project(b[:, 0:TOK], c_kv + n, KT, uhi, ulo).then_inc(w_used, 1)

            def swap_halves(n, raw_tile, group):
                pe.wait_ge(group_done, group + 3)
                if n > 0:
                    pe.wait_ge(rp_sin, n)
                pe.matmul(bank[3][:, 0:TOK], swap, raw_tile, start=True, stop=True).then_inc(rp_swap, 1)

            swap_halves(0, kr_raw, g_kv + 2)
            sum_squares(n_kv[1], 2)
            pe.wait_ge(ulo_done, M2 * 4 + 16)
            for n in range(4):
                b = free_bank(Group(0, g_dq + n))
                start_chunk(c_dq + n)
                project(b[:, 0:TOK], c_dq + n, KT, hhi, hlo).then_inc(w_used, 1)
            sum_squares(n_q[1], 4)
            pe.wait_ge(lat_lo, 2)
            qh, qlo_, kvh, kvl = uhi[:, 2:6, :], ulo[:, 2:6, :], uhi[:, 0:2, :], ulo[:, 0:2, :]
            for p in range(4):
                b = free_bank(Group(0, g_uqr + p))
                start_chunk(c_uqr + p)
                project(b[:, 0:TOK], c_uqr + p, 4, qh, qlo_).then_inc(w_used, 1)
                swap_halves(p + 1, part(p % 2), g_uqr + p)

            def mla_scores(h):
                if h >= 2:
                    pe.wait_ge(ls_add, h - 1)
                f = slice((h % 2) * ROPE, (h % 2 + 1) * ROPE)
                for q, (a, n) in enumerate(((0, P), (P, TOK))):
                    dst = bank[2 + h % 2][:, a:a + n]
                    rows = slice(q * P, (q + 1) * P)
                    pe.matmul(dst, qn[:, h, rows], kn[:, h, 0:n], start=True, stop=False)
                    ins = pe.matmul(dst, qr[f, h // 2, rows], kr[f, 0:n], start=False, stop=True)
                ins.then_inc(ls_full, 1)

            def mla_turn(h):
                pe.wait_ge(ls_norm, h + 1)
                for n in range(3):
                    ins = turn(ls(h)[:, n * P:(n + 1) * P], bank[4 + h % 2][:, n * P:(n + 1) * P])
                ins.then_inc(ls_tp, 1)

            def mla_values(h):
                pe.wait_ge(ls_pt, h + 1)
                if h >= 2:
                    pe.wait_ge(la_lo, h - 1)
                b = bank[6 + h % 2]
                pe.matmul(b[:, 0:TOK], vn[:, 0, h, :], lpT(h)[:, 0:TOK], start=True, stop=False)
                pe.matmul(b[:, P:TOK], vn[:, 1, h, :], lpT(h)[:, TOK:CAUSAL], start=False, stop=True).then_inc(la_full, 1)

            for p in range(5):
                G = g_pairs + 3 * p
                if p < 4:
                    cu = c_pairs + 2 * p
                    b = free_bank(Group(0, G))
                    start_chunk(cu)
                    for h in range(2):
                        project(b[:, h * TOK:(h + 1) * TOK], cu, 2, kvh, kvl, 512, h * 2 * P)
                    b2 = free_bank(Group(0, G + 1))
                    for h in range(2):
                        ins = project_tokens(lambda t: b2[:, (2 * t + h) * P:(2 * t + h + 1) * P], cu, 2, kvh, kvl,
                                             512, h * 2 * P + P)
                    ins.then_inc(w_used, 1)
                if p > 0:
                    mla_turn(2 * p - 2)
                    mla_turn(2 * p - 1)
                if p < 4:
                    b = free_bank(Group(0, G + 2))
                    start_chunk(cu + 1)
                    for h in range(2):
                        ins = project(b[:, h * TOK:(h + 1) * TOK], cu + 1, 4, qh, qlo_, 2 * P, h * P)
                    ins.then_inc(w_used, 1)
                if p > 0:
                    mla_values(2 * p - 2)
                    mla_values(2 * p - 1)
                if p < 4:
                    pe.wait_ge(group_done, G + 3 + 2)
                    pe.wait_ge(rp_done, 5)
                    mla_scores(2 * p)
                    mla_scores(2 * p + 1)
            pe.wait_ge(la_lo, NH)
            to_stream(c_o, hhi, hlo)
            sum_squares(n_ffb[1], KT)
            ffn(c_ffb, Group(0, g_ffb), HID + KT + FT, M2 + 4)
            sum_squares(n_fin[1], KT)
            for t in range(TT):
                for b in range(2):
                    if t == 0:
                        pe.wait_ge(un_done, (M2 + 5) * 4 + 2 * b + 2)
                    for k in range(4):
                        ins = turn(work[:, 4 * b + k, t * P:(t + 1) * P], bank[4 + 2 * t + b][:, k * P:(k + 1) * P])
                    ins.then_inc(y_tp, 1)


def kernel(**inputs):
    from concourse import bacc
    from concourse.bass_utils import run_bass_kernel_spmd

    nc = bacc.Bacc("TRN2", target_bir_lowering=False, num_devices=1)
    arrays, given = {}, {}
    for name, value in inputs.items():
        a = np.ascontiguousarray(value)
        arrays[f"in_{name}"] = a
        given[name] = nc.dram_tensor(f"in_{name}", a.shape, mybir.dt.from_np(a.dtype), kind="ExternalInput").ap()
    arrays["constants"] = constants()
    consts = nc.dram_tensor("constants", (P, C_COLS), F32, kind="ExternalInput").ap()
    out = nc.dram_tensor("out", (1, TOK, DM), F32, kind="ExternalOutput").ap()
    program(nc, given, consts, out)
    r = run_bass_kernel_spmd(nc, [arrays], core_ids=[0])
    return r.results[0]["out"]
```

```python
from contextlib import ExitStack

import numpy as np

import concourse.bass as bass
from concourse import mybir

F32 = mybir.dt.float32
F32R = mybir.dt.float32r
ACT = mybir.ActivationFunctionType
ALU = mybir.AluOpType
AX_X = mybir.AxisListType.X

P = 128
DM = 1024
KT = DM // P
TOK = 256
TT = TOK // P
LAYERS = 2
FF = 2816
FT = FF // P
HD = 64
NPAIR = 4
MH = 4
EPS = 1e-6
NOPE, ROPE, VD, NH = 128, 64, 128, 8
QL, KVL = 512, 256
MLA_SCALE = float((NOPE + ROPE) ** -0.5)
MEM_SCALE = float(P ** -0.5)
SB_SCALE = float(HD ** -0.5)

SLOTS = 4
AHEAD = SLOTS
CW = 1024
CAUSAL = 3 * P

FFN_C, FFN_G = 3 * FT, FT
MIX_C = 12 + 12 * NPAIR + 12 + 8
DOWN_PAIRS = 3 * ((FT - 2) // 4)
BRANCHES = (0, 2, 1)
QLAT, KVLAT = slice(8, 12), slice(12, 14)
LAYER_C = 2 * FFN_C + MIX_C
MEM_G, PAIR_G = 10, 10
LAYER_G = 2 * FFN_G + MEM_G + PAIR_G * NPAIR + 12
assert LAYER_C % SLOTS == 0 and LAYER_G % 2 == 0

LP = 72
LP_NAMES = [("ffn1_pre_g", 8), ("ffn1_post_g", 8), ("mix_pre_g", 8), ("mix_post_g", 8),
            ("ffn2_pre_g", 8), ("ffn2_post_g", 8), ("b_gate", 24)]
PRE1, POST1, PREM, POSTM, PRE2, POST2, BGATE = 0, 8, 16, 24, 32, 40, 48
AMIX = LAYERS * LP
ACONV, BMIX, BQ, KVIN, KVN = AMIX + 8, AMIX + 32, AMIX + 40, AMIX + 44, AMIX + 52
FFNN, FINAL, FCONV = AMIX + 54, AMIX + 70, AMIX + 78
PCOLS = FCONV + 2 * 3 * 2 * FT
assert PCOLS <= 512

C_ID, C_ONE, C_GT, C_LE, C_M01, C_MADD, C_PERM, C_COS, C_SIN, C_NEG8 = (
    0, 128, 256, 384, 512, 640, 1024, 1152, 1408, 1664)
C_COLS = C_NEG8 + 8
MASKED = -1e30
PARAM_LOADS = 7 + 9 + PCOLS // P


def constants():
    c = np.zeros((P, C_COLS), np.float32)
    row, col = np.arange(P)[:, None], np.arange(P)[None, :]
    c[:, C_ID:C_ID + P] = row == col
    c[:, C_ONE:C_ONE + P] = 1.0
    c[:, C_GT:C_GT + P] = row > col
    c[:, C_LE:C_LE + P] = row <= col
    c[:, C_M01:C_M01 + P] = row < col
    diagonal = np.where(col <= row, 0.0, MASKED)
    c[:, C_MADD:C_MADD + P] = diagonal
    c[:, C_MADD + 2 * P:C_MADD + 3 * P] = diagonal
    half = ROPE // 2
    c[:, C_PERM:C_PERM + P] = (row // ROPE == col // ROPE) & ((row + half) % ROPE == col % ROPE)
    inv = (1.0 / (10000.0 ** (np.arange(0, ROPE, 2, dtype=np.float32) / ROPE))).astype(np.float32)
    angle = np.arange(TOK, dtype=np.float32)[None, :] * inv[:, None]
    cos, sin = np.cos(angle), np.sin(angle)
    for p in range(0, P, ROPE):
        c[p:p + half, C_COS:C_COS + TOK] = cos
        c[p + half:p + ROPE, C_COS:C_COS + TOK] = cos
        c[p:p + half, C_SIN:C_SIN + TOK] = -sin
        c[p + half:p + ROPE, C_SIN:C_SIN + TOK] = sin
    c[:8, C_NEG8:C_NEG8 + 8] = -np.eye(8)
    return c


class Chunk:

    def __init__(self, rounds, k):
        self.rounds, self.k = rounds, k

    def __add__(self, n):
        return Chunk(self.rounds, self.k + n)

    def later(self, rounds):
        return Chunk(self.rounds + rounds, self.k)

    def count(self, more=0):
        return self.rounds * SLOTS + (self.k + more)

    @property
    def slot(self):
        return self.k % SLOTS

    @property
    def uses(self):
        return self.rounds + (self.k // SLOTS + 1)


class Group:

    def __init__(self, base, k):
        self.base, self.k = base, k

    def __add__(self, n):
        return Group(self.base, self.k + n)

    def later(self, n):
        return Group(self.base + n, self.k)

    def count(self, more=0):
        return self.base + (self.k + more)


def program(nc, A, consts, out):
    ctx = ExitStack()
    with ctx:
        def sb(name, shape, dt=F32):
            return ctx.enter_context(nc.sbuf_tensor(name, shape, dt))

        def sem(name):
            return ctx.enter_context(nc.semaphore(name))

        raw = [sb(f"raw{s}", [P, CW]) for s in range(SLOTS)]
        whi = [sb(f"whi{s}", [P, CW], F32R) for s in range(SLOTS)]
        wlo = [sb(f"wlo{s}", [P, CW], F32R) for s in range(SLOTS)]
        H = sb("H", [P, KT, TOK])
        work = sb("work", [P, KT, TOK])
        sq = sb("sq", [P, KT, TOK])
        uhi, ulo = sb("uhi", [P, KT, TOK], F32R), sb("ulo", [P, KT, TOK], F32R)
        hhi, hlo = sb("hhi", [P, FT, TOK], F32R), sb("hlo", [P, FT, TOK], F32R)
        mhi, mlo = sb("mhi", [P, KT, TOK], F32R), sb("mlo", [P, KT, TOK], F32R)
        gates = sb("gates", [P, 3 * KT, TOK])
        kmem = sb("kmem", [P, MH, TOK])
        vmem = sb("vmem", [P, TT, MH, P])
        qmem = sb("qmem", [P, MH, TOK])
        small = sb("small", [P, 6 * TOK])
        par = sb("par", [P, 512])
        lp = sb("lp", [P, LP])
        mgain, mgain_rows = sb("mgain", [P, KT]), sb("mgain_rows", [KT, P])
        cst = sb("cst", [P, C_COLS])
        bfor = sb("bfor", [P, LAYERS, 8])
        wfor = sb("wfor", [P, KT, 8])
        wfhi, wflo = sb("wfhi", [P, KT, 8], F32R), sb("wflo", [P, KT, 8], F32R)
        flog, fabs = sb("flog", [P, TT, 8]), sb("fabs", [P, TT, 8])
        ctok = sb("ctok", [P, TT, 8])
        crow = sb("crow", [8, TOK])
        cpair = sb("cpair", [8, 2, TOK])
        qm1, vm1 = sb("qm1", [P, TOK]), sb("vm1", [P, TT, P])
        root, rstd = sb("root", [P, TOK]), sb("rstd", [P, TOK])
        fmax, fsum, frec = sb("fmax", [P, 4]), sb("fsum", [P, 4]), sb("frec", [P, 4])
        mmax, msum, mrec = sb("mmax", [P, 2]), sb("msum", [P, 2]), sb("mrec", [P, 2])

        param_rows = gates[:, 0:2, :].rearrange("p a (b n) -> p (a b) n", n=P)
        mtok = gates[:, 8:16, :].rearrange("p (t a) n -> p t (a n)", t=TT)
        flat = lambda t: t[:, :, :].rearrange("p a b -> p (a b)")
        ident, ones = cst[:, C_ID:C_ID + P], cst[:, C_ONE:C_ONE + P]
        later_keys, up_to = cst[:, C_GT:C_GT + P], cst[:, C_LE:C_LE + P]
        before = cst[:, C_M01:C_M01 + P]
        hide = cst[:, C_MADD:C_MADD + CAUSAL]
        swap = cst[:, C_PERM:C_PERM + P]
        cosine, sine = cst[:, C_COS:C_COS + TOK], cst[:, C_SIN:C_SIN + TOK]

        def two(t, a):
            return flat(t)[:, a:a + 2 * CAUSAL].rearrange("p (h c) -> p h c", h=2)

        rstd_pair = rstd[:, :].unsqueeze(1).to_broadcast([P, 2, TOK])
        sb_e, sb_sp = two(sq, 0), two(sq, 2 * CAUSAL)
        fx_pT = sb_e
        mem_p = flat(sq)[:, 4 * CAUSAL:4 * CAUSAL + 512]
        sb_w, fx_s = two(work, 0), two(work, 2 * CAUSAL)
        mem_pT = flat(work)[:, 4 * CAUSAL:4 * CAUSAL + 512]
        part = lambda n: small[:, n * TOK:(n + 1) * TOK]
        qs, ks, qf, kf = (part(n) for n in range(4))
        vpair = small[:, 4 * TOK:6 * TOK].rearrange("p (t n) -> p t n", t=TT)
        sg = [part(0), part(1)]
        hf = [part(2), part(3)]
        zz = [flat(gates)[:, n * 512:(n + 1) * 512].rearrange("p (s n) -> p s n", s=2) for n in range(2)]
        conv_y = [flat(gates)[:, n * 512:(n + 1) * 512] for n in (2, 3)]
        rstd_sq, rstd_q = part(5), part(5)
        kn = gates[:, 0:8, :]
        vn = flat(gates)[:, 2048:4096].rearrange("p (t h d) -> p t h d", t=TT, h=NH)
        qn = gates[:, 16:24, :]
        ckv, kr_raw, kr = kmem[:, 0:2, :], kmem[:, 2, :], kmem[:, 3, :]
        qlat = vmem[:, :, :, :].rearrange("p t h d -> p (t h) d").rearrange("p (k a) d -> p k (a d)", a=2)
        qr = qmem

        def half(t, h, n=CAUSAL, at=0):
            a = at + (h % 2) * n
            return t[:, a:a + n]

        ls = lambda h: half(flat(sq), h)
        lpT = lambda h: half(flat(sq), h, at=2 * CAUSAL)
        lmax, lsum, lrec = (lambda h, t=t: half(t, h, 2) for t in (fmax, fsum, frec))

        bank = [ctx.enter_context(nc.psum_tensor(f"bank{n}", [P, 512], F32)) for n in range(8)]
        pair_bank = lambda n: bank[n][:, :].rearrange("p (t n) -> p t n", t=2)

        w_loaded = [sem(f"w_loaded{s}") for s in range(SLOTS)]
        hi_ready = sem("hi_ready")
        lo_ready = sem("lo_ready")
        w_used = sem("w_used")
        group_done = sem("group_done")
        sq_done = sem("sq_done")
        ss_full = sem("ss_full")
        root_done = sem("root_done")
        rstd_done = sem("rstd_done")
        acc_full = sem("acc_full")
        scaled = sem("scaled")
        h_ready = sem("h_ready")
        un_done = sem("un_done")
        uhi_done = sem("uhi_done")
        ulo_done = sem("ulo_done")
        silu_done, hid_done, hhi_done, hlo_done = sem("silu_done"), sem("hid_done"), sem("hhi_done"), sem("hlo_done")
        tap_done, conv_done, y_done = sem("tap_done"), sem("conv_done"), sem("y_done")
        rstd_squared = sem("rstd_squared")
        mg_loaded, mg_tp, mg_ready = sem("mg_loaded"), sem("mg_tp"), sem("mg_ready")
        zeroed = sem("zeroed")
        f_full, f_biased, f_log, f_ready = sem("f_full"), sem("f_biased"), sem("f_log"), sem("f_ready")
        f_split = sem("f_split")
        wf_loaded = sem("wf_loaded")
        c_full, c_ready = sem("c_full"), sem("c_ready")
        mem_full, mem_max, mem_exp, mem_rec, mem_norm = (sem(n) for n in ("mem_full", "mem_max", "mem_exp", "mem_rec", "mem_norm"))
        mem_staged, mem_tp, mem_pt = sem("mem_staged"), sem("mem_tp"), sem("mem_pt")
        sbz_full, sb_act, sb_dve, sb_masked = sem("sbz_full"), sem("sb_act"), sem("sb_dve"), sem("sb_masked")
        sb_cum, sb_lw, sb_exp, sb_ready = sem("sb_cum"), sem("sb_lw"), sem("sb_exp"), sem("sb_ready")
        fxz_full, fx_add, fx_max, fx_exp, fx_rec, fx_norm = (sem(n) for n in ("fxz_full", "fx_add", "fx_max", "fx_exp", "fx_rec", "fx_norm"))
        fx_tp, fx_pt = sem("fx_tp"), sem("fx_pt")
        c_pair, v_taken = sem("c_pair"), sem("v_taken")
        o_full, ohi_done, olo_done = sem("o_full"), sem("ohi_done"), sem("olo_done")
        sig_done, gated, merged, mgh_done, mgl_done = (sem(n) for n in ("sig_done", "gated", "merged", "mgh_done", "mgl_done"))
        cst_loaded, x_loaded, m_loaded, p_loaded, bf_loaded = (sem(n) for n in ("cst_loaded", "x_loaded", "m_loaded", "p_loaded", "bf_loaded"))
        par_tp, par_ready, x_tp, lp_ready = sem("par_tp"), sem("par_ready"), sem("x_tp"), sem("lp_ready")
        m_sq, m_root, m_rstd, m_scaled, m_tp, m_gain, m_hi, m_lo = (
            sem(n) for n in ("m_sq", "m_root", "m_rstd", "m_scaled", "m_tp", "m_gain", "m_hi", "m_lo"))
        rp_swap, rp_cos, rp_sin, rp_done = (sem(n) for n in ("rp_swap", "rp_cos", "rp_sin", "rp_done"))
        lat_done, lat_hi, lat_lo = sem("lat_done"), sem("lat_hi"), sem("lat_lo")
        ls_full, ls_add, ls_max, ls_exp, ls_rec, ls_norm, ls_tp, ls_pt = (
            sem(n) for n in ("ls_full", "ls_add", "ls_max", "ls_exp", "ls_rec", "ls_norm", "ls_tp", "ls_pt"))
        la_full, la_hi, la_lo = sem("la_full"), sem("la_hi"), sem("la_lo")
        y_tp, y_copied, y_scaled, y_stored = sem("y_tp"), sem("y_copied"), sem("y_scaled"), sem("y_stored")

        C2, G2 = LAYERS * LAYER_C, LAYERS * LAYER_G
        rounds2 = C2 // SLOTS
        c_conv = Chunk(rounds2, 0)
        c_aout = c_conv + 3 * KT
        c_ffa = c_aout + KT
        c_dq = c_ffa + FFN_C
        c_kv = c_dq + 4
        c_uqr = c_kv + 3
        c_pairs = c_uqr + 4
        c_o = c_pairs + 8
        c_ffb = c_o + KT
        CHUNKS = C2 + c_ffb.k + FFN_C
        g_conv = G2
        g_ffa = g_conv + 3 * KT
        g_dq = g_ffa + FFN_G
        g_kv = g_dq + 4
        g_uqr = g_kv + 3
        g_pairs = g_uqr + 4
        g_ffb = g_pairs + 12
        N2, S2 = 6 * LAYERS, 24 * LAYERS
        n_conv, n_ffa, n_h2, n_q, n_kv, n_ffb, n_fin = (
            (N2, S2), (N2 + 1, S2 + 4), (N2 + 2, S2 + 8), (N2 + 3, S2 + 12), (N2 + 4, S2 + 14),
            (N2 + 5, S2 + 15), (N2 + 6, S2 + 19))

        block = ctx.enter_context(nc.Block())

        @block.sync
        def _(sp):
            def load(c, halves):
                pieces = halves(raw[c.slot])
                sp.wait_ge(lo_ready, c.count(1))
                for dst, src in pieces:
                    sp.dma_start(dst, src).then_inc(w_loaded[c.slot], 16)

            def place(at):
                return at if isinstance(at, int) else sp.snap(at)

            def cols(w, kt, at, n, rows=0, into=0, width=None):
                def halves(slot):
                    width_ = width or n
                    d = slot[:, 0:kt * width_].rearrange("p (k n) -> p k n", k=kt)[:, :, into:into + n]
                    s = w.rearrange("(k p) n -> p k n", p=P)[:, rows:rows + kt, bass.ds(place(at), n)]
                    m = kt // 2
                    return [(d[:, m:kt, :], s[:, m:kt, :]), (d[:, 0:m, :], s[:, 0:m, :])]
                return halves

            def sides(w, kt, n, ats, rows=0):
                def halves(slot):
                    d = slot[:, 0:kt * 2 * n].rearrange("p (k s n) -> p k s n", k=kt, s=2)
                    s = w.rearrange("(k p) n -> p k n", p=P)
                    return [(d[:, :, j, :], s[:, rows:rows + kt, bass.ds(place(a), n)]) for j, a in enumerate(ats)]
                return halves

            def rows_of(w, k):
                def halves(slot):
                    s = w[bass.ds(place(k * P), P), :]
                    return [(slot[:, CW // 2:CW], s[:, CW // 2:CW]), (slot[:, 0:CW // 2], s[:, 0:CW // 2])]
                return halves

            def ffn(c, w_gate, g_at, w_up, u_at, w_down):
                with sp.Fori(0, FT // 2) as i:
                    for j in range(2):
                        load(c.later(i) + 2 * j, cols(w_gate, KT, i * (2 * P) + (g_at + j * P), P))
                        load(c.later(i) + (2 * j + 1), cols(w_up, KT, i * (2 * P) + (u_at + j * P), P))
                down = c + 2 * FT
                for k in range(2):
                    load(down + k, rows_of(w_down, k))
                with sp.Fori(0, (FT - 2) // 4) as i:
                    for j in range(4):
                        load((down + (2 + j)).later(i), rows_of(w_down, i * 4 + (2 + j)))

            sp.dma_start(cst[:, :], consts).then_inc(cst_loaded, 16)
            sp.dma_start(work[:, :, :].rearrange("p (t a) n -> p t (a n)", t=TT),
                         A["x"].rearrange("a (t p) d -> p (a t) d", p=P)).then_inc(x_loaded, 16)
            sp.dma_start(mtok, A["mem"].rearrange("a (t p) d -> p (a t) d", p=P)).then_inc(m_loaded, 16)
            sp.dma_start(mgain_rows[:, :], A["mem_norm_g"].rearrange("(k p) -> k p", p=P)).then_inc(mg_loaded, 16)
            with sp.Fori(0, LAYERS) as l:
                of = lambda name: A[name][bass.ds(l, 1), :, :].rearrange("a k n -> (a k) n")
                c = Chunk(l * (LAYER_C // SLOTS), 0)
                ffn(c, of("ffn1_w_gate"), 0, of("ffn1_w_up"), 0, of("ffn1_w_down"))
                c = c + FFN_C
                w_in, w_mem, w_gate = of("w_in"), of("w_mem_kv"), of("w_gate")
                sp.wait_ge(f_split, l * 2 + 2)
                sp.dma_start(wfor[:, :, :], w_in.rearrange("(k p) n -> p k n", p=P)[:, :, 3072:3080])\
                  .then_inc(wf_loaded, 16)
                for n in range(4):
                    load(c + n, cols(w_mem, KT, n * P, P))
                for n in range(4):
                    load(c + (4 + n), cols(w_mem, 4, MH * P + (n // 2) * (2 * P), 2 * P, rows=4 * (n % 2)))
                for h in range(MH):
                    load(c + (8 + h), cols(w_in, KT, 3080 + h * P, P))
                with sp.Fori(0, NPAIR) as p:
                    cp = (c + 12).later(p * 3)
                    for n, part_at in enumerate((0, 1, 3, 4)):
                        load(cp + n, cols(w_in, KT, p * P + part_at * 512, P))
                    for n in range(2):
                        load(cp + (4 + n), sides(w_in, 4, P, (p * P + 2 * 512, p * P + 5 * 512), rows=4 * n))
                    for n in range(6):
                        load(cp + (6 + n), cols(w_gate, KT, p * (6 * P) + n * P, P))
                c = c + (12 + 12 * NPAIR)
                branches = [of(n) for n in ("w_br_sb", "w_br_fox", "w_br_mem")]
                for j in range(4):
                    for n, b in enumerate(BRANCHES):
                        load(c + (3 * j + n), cols(branches[b], 4, j * 2 * P, 2 * P))
                c = c + 12
                w_out = of("w_out")
                for n in range(KT):
                    load(c + n, cols(w_out, KT, n * P, P))
                c = c + KT
                ffn(c, of("ffn2_w_gate"), 0, of("ffn2_w_up"), 0, of("ffn2_w_down"))
            a_in = A["a_w_in_2"][0]
            with sp.Fori(0, 2) as i:
                for f in range(4):
                    for n, part_at in enumerate((DM, 2 * DM, 0)):
                        load(c_conv.later(i * 3) + (3 * f + n), cols(a_in, KT, i * (4 * P) + (part_at + f * P), P))
            for n in range(KT):
                load(c_aout + n, cols(A["a_w_out_2"][0], KT, n * P, P))
            ffn(c_ffa, A["ffn_w_up_2"][0], 0, A["ffn_w_up_2"][0], FF, A["ffn_w_down_2"][0])
            for n in range(4):
                load(c_dq + n, cols(A["b_w_dq_2"][0], KT, n * P, P))
            for n in range(2):
                load(c_kv + n, cols(A["w_dkv_2"], KT, n * P, P))
            load(c_kv + 2, sides(A["w_dkv_2"], KT, ROPE, (KVL, KVL)))
            w_uq, w_ukv = A["b_w_uq_2"][0], A["w_ukv_2"]
            HQ = NOPE + ROPE
            for p in range(4):
                load(c_uqr + p, sides(w_uq, 4, ROPE, (2 * p * HQ + NOPE, (2 * p + 1) * HQ + NOPE)))
            for p in range(4):
                load(c_pairs + 2 * p, sides(w_uq, 4, NOPE, (2 * p * HQ, (2 * p + 1) * HQ)))
                load(c_pairs + (2 * p + 1), cols(w_ukv, 2, p * 512, 512))
            for n in range(KT):
                load(c_o + n, cols(A["b_w_o_2"][0], KT, n * P, P))
            ffn(c_ffb, A["ffn_w_up_2"][1], 0, A["ffn_w_up_2"][1], FF, A["ffn_w_down_2"][1])
            for t in range(TT):
                sp.wait_ge(y_copied, t + 1)
                sp.wait_ge(y_scaled, t + 1)
                sp.dma_start(out[0, t * P:(t + 1) * P, :], gates[:, 4 * t:4 * t + 4, :].rearrange("p a n -> p (a n)"))\
                  .then_inc(y_stored, 16)
            sp.wait_ge(y_stored, 16 * TT)

        @block.gpsimd
        def _(pool):
            pool.memset(param_rows[:, 3, :], 0.0).then_inc(zeroed, 1)

            def add_scaled(first):
                for b in range(4):
                    pool.wait_ge(scaled, first + (b + 1))
                    s = slice(2 * b, 2 * b + 2)
                    pool.tensor_tensor(H[:, s, :], H[:, s, :], work[:, s, :], ALU.add).then_inc(h_ready, 1)

            def low(m):
                for b in range(4):
                    pool.wait_ge(uhi_done, m * 4 + (b + 1))
                    s = slice(2 * b, 2 * b + 2)
                    pool.tensor_tensor(ulo[:, s, :], work[:, s, :], uhi[:, s, :].bitcast(F32), ALU.subtract)\
                        .then_inc(ulo_done, 1)

            def conv_ffn(use):
                before_it = LAYERS * 2 * FT + KT
                with pool.Fori(0, FT // 2) as i:
                    for j in range(2):
                        f = i * 2 + (j + use * FT)
                        pool.wait_ge(hhi_done, f + (before_it + 1))
                        at = lambda t: t[:, bass.ds(i * 2 + j, 1), :].rearrange("p a n -> p (a n)")
                        pool.tensor_tensor(at(hlo), hf[j], at(hhi).bitcast(F32), ALU.subtract).then_inc(hlo_done, 1)

            for b in range(4):
                pool.wait_ge(m_hi, b + 1)
                s = slice(2 * b, 2 * b + 2)
                pool.tensor_tensor(mlo[:, s, :], gates[:, 16 + 2 * b:18 + 2 * b, :], mhi[:, s, :].bitcast(F32), ALU.subtract)\
                    .then_inc(m_lo, 1)

            diag = lambda t: t.rearrange("p h (a n) -> p h a n", n=P)[:, :, 0:3:2, :]
            mask = before.unsqueeze(1).unsqueeze(1).to_broadcast([P, 2, 2, P])
            with pool.Fori(0, LAYERS) as l:
                add_scaled(l * 12)
                low(l * 3 + 1)
                with pool.Fori(0, NPAIR) as p:
                    I = l * NPAIR + p
                    pool.wait_ge(sb_dve, I * 2 + 2)
                    pool.tensor_tensor(diag(sb_sp), diag(sb_sp), mask, ALU.mult).then_inc(sb_masked, 1)
                    pool.wait_ge(sb_exp, I + 1)
                    pool.tensor_tensor(diag(sb_w), diag(sb_w), mask, ALU.mult).then_inc(sb_ready, 1)
                for n in range(4):
                    s = slice(2 * n, 2 * n + 2)
                    pool.wait_ge(mgh_done, l * 4 + (n + 1))
                    pool.tensor_tensor(ulo[:, s, :], work[:, s, :], uhi[:, s, :].bitcast(F32), ALU.subtract).then_inc(mgl_done, 1)
                add_scaled(l * 12 + 4)
                add_scaled(l * 12 + 8)
            conv_ffn(0)
            conv_ffn(1)

        @block.scalar
        def _(act):
            def hi(c):
                if isinstance(c.rounds, int) and c.count() >= CHUNKS:
                    return
                act.wait_ge(w_loaded[c.slot], c.uses * 32)
                act.wait_ge(w_used, c.count(1))
                act.activation(whi[c.slot][:, :], raw[c.slot][:, :], ACT.Copy).then_inc(hi_ready, 1)

            def chunks(c, n):
                for j in range(n):
                    hi(c + (AHEAD + j))

            def take_root(n, width):
                act.wait_ge(ss_full, n + 1)
                act.activation(root[:, :], bank[2][:, 0:TOK], ACT.Sqrt, scale=1.0 / width, bias=EPS)\
                   .then_inc(root_done, 1)

            def squares_of_stream(version):
                for b in range(4):
                    act.wait_ge(h_ready, version * 4 + (b + 1))
                    s = slice(2 * b, 2 * b + 2)
                    act.activation(sq[:, s, :], H[:, s, :], ACT.Square).then_inc(sq_done, 1)

            def result_pair(b, c, use):
                if b < 3:
                    act.wait_ge(acc_full, use * DOWN_PAIRS + (DOWN_PAIRS - 3 + b + 1))
                else:
                    act.wait_ge(w_used, c.count(FT + SLOTS))

            def square_pair(b):
                act.activation(sq[:, 2 * b:2 * b + 2, :], pair_bank(4 + b), ACT.Square).then_inc(sq_done, 1)

            def scaled_high(version, gain, dst=uhi):
                for b in range(4):
                    act.wait_ge(h_ready, version * 4 + (b + 1))
                    for k in (2 * b, 2 * b + 1):
                        ins = act.activation(dst[:, k, :], H[:, k, :], ACT.Copy, scale=gain[:, k:k + 1])
                    ins.then_inc(uhi_done, 1)

            def tile(t, n):
                return t[:, bass.ds(n, 1), :].rearrange("p a n -> p (a n)")

            def ffn(c, g, use, n):
                def tiles(i, first=False):
                    ci = c.later(i)

                    def silu(j):
                        act.wait_ge(group_done, g.base + i * 2 + (g.k + j + 3))
                        act.activation(sg[j], zz[j][:, 0, :], ACT.Silu).then_inc(silu_done, 1)

                    def high(j):
                        act.wait_ge(hid_done, use * FT + (i * 2 + (j + 1)))
                        act.activation(tile(hhi, i * 2 + j), hf[j], ACT.Copy).then_inc(hhi_done, 1)

                    chunks(ci, 2)
                    if first:
                        take_root(n, DM)
                        act.preload_act_table(ACT.Silu)
                    silu(0)
                    chunks(ci + 2, 1)
                    high(0)
                    chunks(ci + 3, 1)
                    silu(1)
                    high(1)

                tiles(0, first=True)
                with act.Fori(1, FT // 2) as i:
                    tiles(i)
                down(c + 2 * FT)

            def down(c):
                turns = (FT - 2) // 4
                last = isinstance(c.rounds, int) and c.count(FT) > CHUNKS
                with act.Fori(0, turns - last) as i:
                    chunks(c.later(i), 4)
                if last:
                    chunks(c + 4 * (turns - 1), 4)
                act.preload_act_table(ACT.Sqrt)

            def conv_ffn(c, g, use, layer, n):
                taps = FCONV + layer * 6 * FT
                before_it = LAYERS * 2 * FT

                def tiles(i, first=False):
                    ci = c.later(i)
                    f0 = i * 2 + use * FT

                    def newest_tap(j):
                        act.wait_ge(group_done, i * 2 + (g + j + 3))
                        for s in range(2):
                            act.activation(conv_y[j][:, s * TOK:(s + 1) * TOK], zz[j][:, s, :], ACT.Copy,
                                           scale=par[:, bass.ds(i * 2 + (taps + 4 * FT + s * FT + j), 1)]).then_inc(tap_done, 1)

                    def silu(j):
                        act.wait_ge(conv_done, (f0 + j) * 4 + 3)
                        act.activation(sg[j], conv_y[j][:, 0:TOK], ACT.Silu).then_inc(silu_done, 1)

                    def high(j):
                        act.wait_ge(hid_done, f0 + (j + before_it + 1))
                        act.activation(tile(hhi, i * 2 + j), hf[j % 2], ACT.Copy).then_inc(hhi_done, 1)

                    chunks(ci + 1, 1)
                    if first:
                        take_root(n, DM)
                        act.preload_act_table(ACT.Silu)
                    else:
                        high(-1)
                    newest_tap(0)
                    chunks(ci + 2, 1)
                    silu(0)
                    chunks(ci + 3, 1)
                    high(0)
                    newest_tap(1)
                    chunks(ci + 4, 1)
                    silu(1)

                chunks(c, 1)
                tiles(0, first=True)
                with act.Fori(1, FT // 2) as i:
                    tiles(i)
                act.wait_ge(hid_done, (use + 1) * FT + before_it)
                act.activation(hhi[:, FT - 1, :], hf[1], ACT.Copy).then_inc(hhi_done, 1)
                down(c + (2 * FT + 1))

            def head_high(count, src, dst):
                act.wait_ge(o_full, count)
                act.activation(dst, src, ACT.Copy).then_inc(ohi_done, 1)

            at = 0
            pieces = [(A[n], LAYERS * k) for n, k in LP_NAMES]
            pieces += [(A["a_mix_norm_2"][0], 8), (A["a_conv_2"][0], 24),
                       (A["b_mix_norm_2"][0], 8), (A["b_q_norm_2"][0], 4), (A["kv_in_norm_2"], 8),
                       (A["kv_norm_2"], 2), (A["ffn_norm_2"], 16), (A["final_norm_2"], 8),
                       (A["ffn_conv_2"], 264)]
            loads = 0
            act.wait_ge(zeroed, 1)
            for src, k in pieces:
                if len(src.shape) == 3:
                    src = src.rearrange("a b (k p) -> (a b k) p", p=P)
                elif len(src.shape) == 2:
                    src = src.rearrange("a (k p) -> (a k) p", p=P)
                else:
                    src = src.rearrange("(k p) -> k p", p=P)
                done = 0
                while done < k:
                    r, row_group = at % P, at // P
                    m = min(k - done, P - r)
                    act.dma_start(param_rows[r:r + m, row_group, :], src[done:done + m, :]).then_inc(p_loaded, 16)
                    loads += 1
                    at += m
                    done += m
            assert at == PCOLS
            assert loads == PARAM_LOADS
            act.dma_start(bfor[:, :, :].rearrange("p l h -> p (l h)"),
                           A["b_forget"].rearrange("l h -> (l h)").partition_broadcast(P)).then_inc(bf_loaded, 16)

            for n in range(2):
                hi(Chunk(0, n))
            act.wait_ge(m_loaded, 16)
            for t in range(TT):
                act.activation(flat(sq)[:, t * DM:(t + 1) * DM], mtok[:, t, :], ACT.Square,
                               accum_out=msum[:, t:t + 1]).then_inc(m_sq, 1)
            act.wait_ge(m_sq, TT)
            act.activation(mmax[:, :], msum[:, :], ACT.Sqrt, scale=1.0 / DM, bias=EPS).then_inc(m_root, 1)
            for n in range(2, SLOTS):
                hi(Chunk(0, n))
            for b in range(4):
                act.wait_ge(m_gain, 2 * b + 2)
                act.activation(mhi[:, 2 * b:2 * b + 2, :], gates[:, 16 + 2 * b:18 + 2 * b, :], ACT.Copy).then_inc(m_hi, 1)

            with act.Fori(0, LAYERS) as l:
                c = Chunk(l * (LAYER_C // SLOTS), 0)
                g = Group(l * LAYER_G, 0)
                gain = lambda at: lp[:, at:at + KT]
                act.wait_ge(lp_ready, l * 2 + 2)
                scaled_high(l * 3, gain(PRE1))
                squares_of_stream(l * 3)
                ffn(c, g, l * 2, l * 6)
                for b in range(4):
                    result_pair(b, c + 2 * FT, l * 2)
                    square_pair(b)
                c, g = c + FFN_C, g + FFN_G
                chunks(c + (-2), 2)
                take_root(l * 6 + 1, DM)
                chunks(c, 1)
                squares_of_stream(l * 3 + 1)
                chunks(c + 1, 2)
                take_root(l * 6 + 2, DM)
                act.preload_act_table_set("natural_log_exp_and_others")
                chunks(c + 3, 1)
                for b in range(4):
                    act.wait_ge(un_done, l * 4 + (b + 1))
                    s = slice(2 * b, 2 * b + 2)
                    act.activation(uhi[:, s, :], work[:, s, :], ACT.Copy).then_inc(uhi_done, 1)
                chunks(c + 4, 4)
                act.wait_ge(wf_loaded, l * 16 + 16)
                act.activation(wfhi[:, :, :], wfor[:, :, :], ACT.Copy).then_inc(f_split, 1)
                chunks(c + 8, 1)
                act.wait_ge(f_biased, l + 1)
                act.activation(fabs[:, :, :], flog[:, :, :], ACT.Abs).then_inc(f_log, 1)
                act.wait_ge(f_log, l * 3 + 1)
                act.activation(fabs[:, :, :], fabs[:, :, :], ACT.Exp, scale=-1.0).then_inc(f_log, 1)
                act.wait_ge(f_log, l * 3 + 2)
                act.activation(fabs[:, :, :], fabs[:, :, :], ACT.Ln, bias=1.0).then_inc(f_log, 1)
                chunks(c + 9, 3)
                with act.Fori(0, NPAIR) as p:
                    I = l * NPAIR + p
                    cp = (c + 12).later(p * 3)
                    o = lambda branch: tile(hhi, p + 4 * branch)
                    chunks(cp, 1)
                    act.wait_ge(mem_max, I + 1)
                    for q in range(TT):
                        act.activation(mem_p[:, q * TOK:(q + 1) * TOK], bank[6][:, q * TOK:(q + 1) * TOK], ACT.Exp,
                                       bias=mmax[:, q:q + 1], accum_out=msum[:, q:q + 1]).then_inc(mem_exp, 1)
                    chunks(cp + 1, 3)
                    act.wait_ge(mem_tp, I + 1)
                    act.activation(mem_pT, bank[7][:, :], ACT.Copy).then_inc(mem_pt, 1)
                    act.wait_ge(sbz_full, I + 1)
                    act.activation(sb_e[:, 0, :], bank[2][:, 0:CAUSAL], ACT.Abs).then_inc(sb_act, 1)
                    act.activation(sb_e[:, 1, :], bank[3][:, 0:CAUSAL], ACT.Abs).then_inc(sb_act, 1)
                    act.wait_ge(sb_act, I * 4 + 2)
                    act.activation(sb_e, sb_e, ACT.Exp, scale=-1.0).then_inc(sb_act, 1)
                    chunks(cp + 4, 1)
                    act.wait_ge(sb_act, I * 4 + 3)
                    act.activation(sb_e, sb_e, ACT.Ln, bias=1.0).then_inc(sb_act, 1)
                    head_high(I * 3 + 1, bank[6][:, 0:TOK], o(2))
                    chunks(cp + 5, 3)
                    act.wait_ge(fx_max, I * 2 + 2)
                    for h in range(2):
                        for q, (a, b) in enumerate(((0, P), (P, CAUSAL))):
                            n = 2 * q + h
                            act.activation(fx_s[:, h, a:b], fx_s[:, h, a:b], ACT.Exp, bias=fmax[:, n:n + 1],
                                           accum_out=fsum[:, n:n + 1]).then_inc(fx_exp, 1)
                    chunks(cp + 8, 1)
                    act.wait_ge(sb_lw, I * 2 + 2)
                    act.activation(sb_w, sb_w, ACT.Exp).then_inc(sb_exp, 1)
                    chunks(cp + 9, 1)
                    act.wait_ge(fx_tp, I + 1)
                    for h in range(2):
                        act.activation(fx_pT[:, h, :], bank[2 + h][:, 0:CAUSAL], ACT.Copy).then_inc(fx_pt, 1)
                    chunks(cp + 10, 1)
                    head_high(I * 3 + 2, bank[4][:, 0:TOK], o(0))
                    chunks(cp + 11, 1)
                    head_high(I * 3 + 3, bank[5][:, 0:TOK], o(1))
                c, g = c + (12 + 12 * NPAIR), g + (MEM_G + PAIR_G * NPAIR)
                act.wait_ge(group_done, g.count(2))
                def sigmoids(n):
                    for b in BRANCHES:
                        s = slice(8 * b + 2 * n, 8 * b + 2 * n + 2)
                        act.activation(gates[:, s, :], gates[:, s, :], ACT.Sigmoid).then_inc(sig_done, 1)

                def merged_high(n):
                    act.wait_ge(merged, l * 8 + (2 * n + 2))
                    s = slice(2 * n, 2 * n + 2)
                    act.activation(uhi[:, s, :], work[:, s, :], ACT.Copy).then_inc(mgh_done, 1)

                sigmoids(0)
                for n in range(4):
                    chunks(c + 3 * n, 1)
                    if n > 0:
                        merged_high(n - 1)
                    chunks(c + (3 * n + 1), 1)
                    if n < 3:
                        sigmoids(n + 1)
                    else:
                        act.preload_act_table(ACT.Sqrt)
                    chunks(c + (3 * n + 2), 1)
                merged_high(3)
                c, g = c + 12, g + 12
                chunks(c, KT - 2)
                for b in range(4):
                    act.wait_ge(w_used, (c + (2 * b + 1)).count(1 + SLOTS))
                    square_pair(b)
                c = c + KT
                chunks(c + (-2), 2)
                take_root(l * 6 + 3, DM)
                scaled_high(l * 3 + 2, gain(PRE2))
                squares_of_stream(l * 3 + 2)
                ffn(c, g, l * 2 + 1, l * 6 + 4)
                for b in range(4):
                    result_pair(b, c + 2 * FT, l * 2 + 1)
                    square_pair(b)
                chunks(c + (FFN_C - 2), 2)
                take_root(l * 6 + 5, DM)

            V2, M2 = 3 * LAYERS, 3 * LAYERS
            pgain = lambda at: par[:, at:at + KT]
            scaled_high(V2, pgain(AMIX))
            squares_of_stream(V2)
            for t in range(KT):
                ci = c_conv + 3 * t
                chunks(ci, 1)
                if t == 0:
                    take_root(n_conv[0], DM)
                chunks(ci + 1, 1)
                act.wait_ge(group_done, g_conv + 3 * t + 2 + 2)
                act.activation(sg[t % 2], hf[t % 2], ACT.Copy, scale=par[:, ACONV + 2 * KT + t:ACONV + 2 * KT + t + 1])\
                   .then_inc(tap_done, 1)
                chunks(ci + 2, 1)
                act.wait_ge(y_done, t * 3 + 3)
                act.activation(hhi[:, t, :], hf[t % 2], ACT.Copy).then_inc(hhi_done, 1)
            chunks(c_aout, KT - 2)
            scaled_high(V2 + 1, pgain(FFNN))
            squares_of_stream(V2 + 1)
            chunks(c_aout + (KT - 2), 2)
            conv_ffn(c_ffa, g_ffa, 0, 0, n_ffa[0])
            scaled_high(V2 + 2, pgain(BMIX), hhi)
            squares_of_stream(V2 + 2)
            scaled_high(V2 + 2, pgain(KVIN))
            chunks(c_ffa + (FFN_C - 1), 1)
            chunks(c_dq, 1)
            take_root(n_h2[0], DM)
            chunks(c_dq + 1, 3)
            act.wait_ge(group_done, g_dq + 4 + 2)
            for b in range(2):
                act.activation(sq[:, 2 * b:2 * b + 2, :], qlat[:, 2 * b:2 * b + 2, :], ACT.Square).then_inc(sq_done, 1)
            chunks(c_kv, 1)
            take_root(n_q[0], QL)
            chunks(c_kv + 1, 1)
            act.wait_ge(group_done, g_kv + 2 + 2)
            act.activation(sq[:, 4:6, :], ckv, ACT.Square).then_inc(sq_done, 1)
            act.wait_ge(lat_done, 1)
            act.activation(hhi[:, QLAT, :], work[:, 2:6, :], ACT.Copy).then_inc(lat_hi, 1)
            chunks(c_kv + 2, 1)
            take_root(n_kv[0], KVL)
            act.wait_ge(lat_done, 2)
            act.activation(hhi[:, KVLAT, :], work[:, 0:2, :], ACT.Copy).then_inc(lat_hi, 1)
            act.preload_act_table(ACT.Exp)
            chunks(c_uqr, 4)

            def mla_exp(h):
                act.wait_ge(ls_max, 2 * h + 2)
                for q, (a, b) in enumerate(((0, P), (P, CAUSAL))):
                    act.activation(ls(h)[:, a:b], ls(h)[:, a:b], ACT.Exp, bias=lmax(h)[:, q:q + 1],
                                   accum_out=lsum(h)[:, q:q + 1]).then_inc(ls_exp, 1)

            def mla_pT(h):
                act.wait_ge(ls_tp, h + 1)
                act.activation(lpT(h), bank[4 + h % 2][:, 0:CAUSAL], ACT.Copy).then_inc(ls_pt, 1)

            def mla_high(h):
                act.wait_ge(la_full, h + 1)
                act.activation(hhi[:, h, :], bank[6 + h % 2][:, 0:TOK], ACT.Copy).then_inc(la_hi, 1)

            for p in range(5):
                if p < 4:
                    chunks(c_pairs + 2 * p, 1)
                if p > 0:
                    mla_exp(2 * p - 2)
                    mla_exp(2 * p - 1)
                    mla_pT(2 * p - 2)
                    mla_pT(2 * p - 1)
                if p < 4:
                    chunks(c_pairs + (2 * p + 1), 1)
                if p > 0:
                    mla_high(2 * p - 2)
                    mla_high(2 * p - 1)
            act.preload_act_table(ACT.Sqrt)
            chunks(c_o, KT - 2)
            scaled_high(V2 + 3, pgain(FFNN + KT))
            squares_of_stream(V2 + 3)
            chunks(c_o + (KT - 2), 2)
            conv_ffn(c_ffb, g_ffb, 1, 1, n_ffb[0])
            for b in range(4):
                act.wait_ge(h_ready, (V2 + 4) * 4 + (b + 1))
                for k in (2 * b, 2 * b + 1):
                    ins = act.activation(work[:, k, :], H[:, k, :], ACT.Copy, scale=par[:, FINAL + k:FINAL + k + 1])
                ins.then_inc(un_done, 1)
                act.activation(sq[:, 2 * b:2 * b + 2, :], H[:, 2 * b:2 * b + 2, :], ACT.Square).then_inc(sq_done, 1)
            act.wait_ge(ss_full, n_fin[0] + 1)
            act.activation(mmax[:, :], bank[2][:, 0:2 * TT:2], ACT.Sqrt, scale=1.0 / DM, bias=EPS).then_inc(root_done, 1)
            for t in range(TT):
                act.wait_ge(rstd_done, n_fin[0] + 1)
                act.wait_ge(y_tp, 2 * t + 1)
                act.activation(gates[:, 4 * t:4 * t + 2, :], pair_bank(4 + 2 * t), ACT.Copy, scale=mrec[:, t:t + 1])\
                   .then_inc(y_copied, 1)

        @block.vector
        def _(dve):
            def lo(c):
                if isinstance(c.rounds, int) and c.count() >= CHUNKS:
                    return
                dve.wait_ge(hi_ready, c.count(1))
                dve.tensor_tensor(wlo[c.slot][:, :], raw[c.slot][:, :], whi[c.slot][:, :].bitcast(F32), ALU.subtract)\
                   .then_inc(lo_ready, 1)

            def chunks(c, n):
                for j in range(n):
                    lo(c + (AHEAD + j))

            def done(c):
                dve.wait_ge(w_used, c.count(1 + SLOTS))

            def take_rstd(n, dst=None):
                dst = rstd[:, :] if dst is None else dst
                dve.wait_ge(root_done, n + 1)
                dve.reciprocal(dst, root[:, :]).then_inc(rstd_done, 1)
                dve.wait_ge(rstd_done, n + 1)

            def scale_result(gain, pairs):
                for b in pairs:
                    for k in (2 * b, 2 * b + 1):
                        ins = dve.scalar_tensor_tensor(work[:, k, :], bank[4 + b][:, (k % 2) * TOK:(k % 2 + 1) * TOK],
                                                       gain[:, k:k + 1], rstd[:, :], ALU.mult, ALU.mult)
                    ins.then_inc(scaled, 1)

            def scaled_low(m, gain, dst=ulo, src=uhi):
                for b in range(4):
                    dve.wait_ge(uhi_done, m * 4 + (b + 1))
                    for k in (2 * b, 2 * b + 1):
                        ins = dve.scalar_tensor_tensor(dst[:, k, :], H[:, k, :], gain[:, k:k + 1],
                                                       src[:, k, :].bitcast(F32), ALU.mult, ALU.subtract)
                    ins.then_inc(ulo_done, 1)

            def add_result(complete):
                for b in range(4):
                    complete(b)
                    s = slice(2 * b, 2 * b + 2)
                    dve.tensor_tensor(H[:, s, :], pair_bank(4 + b), H[:, s, :], ALU.add).then_inc(h_ready, 1)

            def of_down(c, use):
                def complete(b):
                    if b < 3:
                        dve.wait_ge(acc_full, use * DOWN_PAIRS + (DOWN_PAIRS - 3 + b + 1))
                    else:
                        done(c + (FT - 1))
                return complete

            def tile(t, n):
                return t[:, bass.ds(n, 1), :].rearrange("p a n -> p (a n)")

            def down(c):
                turns = (FT - 2) // 4
                last = isinstance(c.rounds, int) and c.count(FT) > CHUNKS
                with dve.Fori(0, turns - last) as i:
                    chunks(c.later(i), 4)
                if last:
                    chunks(c + 4 * (turns - 1), 4)

            def ffn(c, g, use, n):
                def tiles(i, first=False):
                    ci = c.later(i)
                    f0 = i * 2 + use * FT

                    def scale(j):
                        done(ci + (2 * j + 1))
                        dve.tensor_tensor(zz[j], pair_bank((g.k + j) % 2), rstd_pair, ALU.mult).then_inc(group_done, 1)

                    def hidden(j):
                        dve.wait_ge(silu_done, f0 + (j + 1))
                        dve.tensor_tensor(hf[j], zz[j][:, 1, :], sg[j], ALU.mult).then_inc(hid_done, 1)

                    def low(j):
                        dve.wait_ge(hhi_done, f0 + (j + 1))
                        dve.tensor_tensor(tile(hlo, i * 2 + j), hf[j], tile(hhi, i * 2 + j).bitcast(F32), ALU.subtract)\
                           .then_inc(hlo_done, 1)

                    chunks(ci, 1)
                    if first:
                        take_rstd(n)
                    scale(0)
                    hidden(0)
                    chunks(ci + 1, 1)
                    low(0)
                    chunks(ci + 2, 1)
                    scale(1)
                    hidden(1)
                    chunks(ci + 3, 1)
                    low(1)

                tiles(0, first=True)
                with dve.Fori(1, FT // 2) as i:
                    tiles(i)
                down(c + 2 * FT)

            def conv_ffn(c, g, use, layer, n):
                taps = FCONV + layer * 6 * FT
                before_it = LAYERS * 2 * FT

                def tiles(i, first=False):
                    ci = c.later(i)
                    f0 = i * 2 + use * FT

                    def scale(j):
                        done(ci + (2 * j + 1))
                        dve.tensor_tensor(zz[j], pair_bank((g + j) % 2), rstd_pair, ALU.mult).then_inc(group_done, 1)

                    def older_taps(j):
                        y = conv_y[j]
                        dve.wait_ge(tap_done, (f0 + j) * 2 + (2 + KT))
                        for back in (1, 2):
                            for s in range(2):
                                a = s * TOK
                                if back == 2:
                                    dve.wait_ge(conv_done, (f0 + j) * 4 + (s + 1))
                                dve.scalar_tensor_tensor(
                                    y[:, a + back:a + TOK], zz[j][:, s, 0:TOK - back],
                                    par[:, bass.ds(i * 2 + (taps + (2 - back) * 2 * FT + s * FT + j), 1)],
                                    y[:, a + back:a + TOK], ALU.mult, ALU.add).then_inc(conv_done, 1)

                    def hidden(j):
                        dve.wait_ge(silu_done, f0 + (j + before_it + 1))
                        dve.wait_ge(conv_done, (f0 + j) * 4 + 4)
                        dve.wait_ge(hlo_done, f0 + (j + before_it + KT - 1))
                        dve.tensor_tensor(hf[j], conv_y[j][:, TOK:2 * TOK], sg[j], ALU.mult).then_inc(hid_done, 1)

                    if first:
                        take_rstd(n)
                    for j in range(2):
                        scale(j)
                        chunks(ci + (2 * j + 1), 1)
                        older_taps(j)
                        chunks(ci + (2 * j + 2), 1)
                        hidden(j)

                chunks(c, 1)
                tiles(0, first=True)
                with dve.Fori(1, FT // 2) as i:
                    tiles(i)
                down(c + (2 * FT + 1))

            def head_low(count, src, hi_part, lo_part):
                dve.wait_ge(ohi_done, count)
                dve.tensor_tensor(lo_part, src, hi_part.bitcast(F32), ALU.subtract).then_inc(olo_done, 1)

            dve.sem_inc(lo_ready, SLOTS)
            dve.sem_inc(group_done, 2)
            dve.sem_inc(f_split, 2)
            dve.sem_inc(olo_done, 1)
            for b in range(4):
                dve.wait_ge(x_tp, b + 1)
                dve.tensor_copy(H[:, 2 * b:2 * b + 2, :], pair_bank(4 + b)).then_inc(h_ready, 1)
            for n in range(2):
                lo(Chunk(0, n))
            dve.wait_ge(m_root, 1)
            dve.reciprocal(mrec[:, :], mmax[:, :]).then_inc(m_rstd, 1)
            dve.wait_ge(m_rstd, 1)
            for t in range(TT):
                dve.tensor_scalar(mtok[:, t, :], mtok[:, t, :], mrec[:, t:t + 1], None, ALU.mult).then_inc(m_scaled, 1)
            dve.wait_ge(mg_tp, 1)
            dve.tensor_copy(mgain[:, :], bank[2][:, 0:KT]).then_inc(mg_ready, 1)
            dve.wait_ge(mg_ready, 1)
            for k in range(KT):
                dve.wait_ge(m_tp, k // 2 + 1)
                dve.tensor_scalar(gates[:, 16 + k, :], bank[4 + k // 2][:, (k % 2) * TOK:(k % 2 + 1) * TOK],
                                  mgain[:, k:k + 1], None, ALU.mult).then_inc(m_gain, 1)
            for n in range(2, SLOTS):
                lo(Chunk(0, n))
            dve.wait_ge(par_tp, 1)
            dve.tensor_copy(par[:, :], bank[3][:, :]).then_inc(par_ready, 1)
            dve.wait_ge(par_ready, 1)
            for at in (POST1, POST2):
                v = par[:, at * LAYERS:(at + KT) * LAYERS]
                dve.tensor_scalar(v, v, 0.5, None, ALU.mult).then_inc(par_ready, 1)

            with dve.Fori(0, LAYERS) as l:
                c = Chunk(l * (LAYER_C // SLOTS), 0)
                g = Group(l * LAYER_G, 0)
                dve.wait_ge(par_ready, 3)
                by_layer = par[:, 0:BGATE * LAYERS].rearrange("p (n l k) -> p n l k", l=LAYERS, k=KT)
                dve.tensor_copy(lp[:, 0:BGATE].rearrange("p (n k) -> p n k", k=KT).unsqueeze(2),
                                by_layer[:, :, bass.ds(l, 1), :]).then_inc(lp_ready, 1)
                dve.tensor_copy(lp[:, BGATE:LP], par[:, bass.ds(l * (3 * KT) + BGATE * LAYERS, 3 * KT)]).then_inc(lp_ready, 1)
                dve.wait_ge(lp_ready, l * 2 + 2)
                gain = lambda at: lp[:, at:at + KT]
                scaled_low(l * 3, gain(PRE1))
                ffn(c, g, l * 2, l * 6)
                c, g = c + FFN_C, g + FFN_G
                chunks(c + (-2), 2)

                def take_mem(n):
                    done(c + (n if n < 4 else n + 2))
                    src = bank[n % 2][:, 0:TOK]
                    if n < 4:
                        dve.tensor_copy(kmem[:, n, :], src).then_inc(group_done, 1)
                    else:
                        dve.tensor_scalar(qmem[:, n - 6, :], src, MEM_SCALE, None, ALU.mult).then_inc(group_done, 1)

                take_mem(0)
                take_rstd(l * 6 + 1)
                scale_result(gain(POST1), (0, 1))
                take_mem(1)
                scale_result(gain(POST1), (2, 3))
                chunks(c, 1)
                take_mem(2)
                chunks(c + 1, 1)
                take_mem(3)
                chunks(c + 2, 1)
                take_rstd(l * 6 + 2)
                for b in range(4):
                    dve.wait_ge(h_ready, l * 12 + (b + 5))
                    for k in (2 * b, 2 * b + 1):
                        ins = dve.scalar_tensor_tensor(work[:, k, :], H[:, k, :], lp[:, PREM + k:PREM + k + 1], rstd[:, :],
                                                       ALU.mult, ALU.mult)
                    ins.then_inc(un_done, 1)
                chunks(c + 3, 1)
                for e in range(2):
                    chunks(c + (4 + 2 * e), 1)
                    done(c + (5 + 2 * e))
                    dve.tensor_copy(vmem[:, :, 2 * e:2 * e + 2, :],
                                    bank[e][:, :].rearrange("p (t h d) -> p t h d", t=TT, h=2)).then_inc(group_done, 1)
                    chunks(c + (5 + 2 * e), 1)
                dve.wait_ge(f_split, l * 2 + 3)
                dve.tensor_tensor(wflo[:, :, :], wfor[:, :, :], wfhi[:, :, :].bitcast(F32), ALU.subtract).then_inc(f_split, 1)
                take_mem(6)
                chunks(c + 8, 1)
                dve.wait_ge(f_full, l + 1)
                dve.wait_ge(bf_loaded, 16)
                dve.tensor_tensor(flog[:, :, :], bank[3][:, 0:16].rearrange("p (t h) -> p t h", t=TT),
                                  bfor[:, bass.ds(l, 1), :].to_broadcast([P, TT, 8]), ALU.add).then_inc(f_biased, 1)
                dve.wait_ge(f_log, l * 3 + 3)
                dve.scalar_tensor_tensor(flog[:, :, :], flog[:, :, :], 0.0, fabs[:, :, :], ALU.min, ALU.subtract)\
                   .then_inc(f_ready, 1)
                for n in (7, 8):
                    take_mem(n)
                    chunks(c + (n + 2), 1)
                dve.wait_ge(c_full, l + 1)
                dve.tensor_copy(ctok[:, :, :], bank[3][:, 32:48].rearrange("p (t h) -> p t h", t=TT)).then_inc(c_ready, 1)
                dve.tensor_copy(crow[:, :], bank[3][0:8, 64:64 + TOK]).then_inc(c_ready, 1)
                take_mem(9)
                chunks(c + 11, 1)
                with dve.Fori(0, NPAIR) as p:
                    I = l * NPAIR + p
                    cp = (c + 12).later(p * 3)
                    o = lambda t, branch: tile(t, p + 4 * branch)

                    def gate(n):
                        done(cp + (6 + n))
                        dve.tensor_scalar(tile(gates, p * 6 + n),
                                          bank[n % 2][:, 0:TOK], lp[:, bass.ds(p * 6 + (BGATE + n), 1)], None, ALU.add)\
                           .then_inc(group_done, 1)

                    dve.tensor_copy(qm1[:, :], tile(qmem, p)).then_inc(mem_staged, 1)
                    dve.tensor_copy(vm1[:, :, :], vmem[:, :, bass.ds(p, 1), :].rearrange("p t a d -> p t (a d)"))\
                       .then_inc(mem_staged, 1)
                    dve.wait_ge(c_ready, l * 2 + 2)
                    for h in range(2):
                        dve.tensor_scalar(cpair[:, h, :], crow[:, :], cst[0:8, bass.ds(p * 2 + (C_NEG8 + h), 1)], None,
                                          ALU.mult).then_inc(c_pair, 1)
                    done(cp)
                    dve.tensor_scalar(qs, bank[0][:, 0:TOK], SB_SCALE, None, ALU.mult).then_inc(group_done, 1)
                    dve.wait_ge(mem_full, I + 1)
                    dve.tensor_reduce(mmax[:, :], pair_bank(6), AX_X, ALU.max, negate=True).then_inc(mem_max, 1)
                    chunks(cp, 1)
                    done(cp + 1)
                    dve.tensor_copy(ks, bank[1][:, 0:TOK]).then_inc(group_done, 1)
                    dve.wait_ge(mem_exp, I * 2 + 2)
                    dve.reciprocal(mrec[:, :], msum[:, :]).then_inc(mem_rec, 1)
                    dve.wait_ge(mem_rec, I + 1)
                    for q in range(TT):
                        ins = dve.tensor_scalar(mem_p[:, q * TOK:(q + 1) * TOK], mem_p[:, q * TOK:(q + 1) * TOK],
                                                mrec[:, q:q + 1], None, ALU.mult)
                    ins.then_inc(mem_norm, 1)
                    chunks(cp + 1, 1)
                    done(cp + 2)
                    dve.tensor_scalar(qf, bank[0][:, 0:TOK], SB_SCALE, None, ALU.mult).then_inc(group_done, 1)
                    chunks(cp + 2, 1)
                    done(cp + 3)
                    dve.tensor_copy(kf, bank[1][:, 0:TOK]).then_inc(group_done, 1)
                    chunks(cp + 3, 2)
                    head_low(I * 3 + 1, bank[6][:, 0:TOK], o(hhi, 2), o(hlo, 2))
                    done(cp + 5)
                    dve.tensor_copy(vpair, pair_bank(5)).then_inc(v_taken, 1)
                    dve.wait_ge(sb_act, I * 4 + 4)
                    for h in range(2):
                        ins = dve.scalar_tensor_tensor(sb_sp[:, h, :], bank[2 + h][:, 0:CAUSAL], 0.0, sb_e[:, h, :],
                                                       ALU.max, ALU.add)
                    ins.then_inc(sb_dve, 1)
                    dve.wait_ge(sb_dve, I * 2 + 1)
                    for h in range(2):
                        ins = dve.tensor_tensor(sb_w[:, h, :], bank[2 + h][:, 0:CAUSAL], sb_sp[:, h, :], ALU.subtract)
                    ins.then_inc(sb_dve, 1)
                    chunks(cp + 5, 1)
                    gate(0)
                    chunks(cp + 6, 1)
                    dve.wait_ge(fxz_full, I + 1)
                    for h in range(2):
                        for q, (a, b) in enumerate(((0, P), (P, CAUSAL))):
                            dve.scalar_tensor_tensor(fx_s[:, h, a:b], bank[4 + h][:, a:b],
                                                     ctok[:, q, bass.ds(p * 2 + h, 1)], hide[:, a:b],
                                                     ALU.add, ALU.add).then_inc(fx_add, 1)
                    dve.wait_ge(fx_add, I * 4 + 4)
                    for q, (a, b) in enumerate(((0, P), (P, CAUSAL))):
                        dve.tensor_reduce(fmax[:, 2 * q:2 * q + 2], fx_s[:, :, a:b], AX_X, ALU.max, negate=True)\
                           .then_inc(fx_max, 1)
                    gate(1)
                    chunks(cp + 7, 1)
                    dve.wait_ge(sb_cum, I + 1)
                    for h in range(2):
                        dve.tensor_tensor(sb_w[:, h, :], sb_w[:, h, :], bank[6 + h][:, 0:CAUSAL], ALU.subtract)\
                           .then_inc(sb_lw, 1)
                    dve.wait_ge(fx_exp, I * 4 + 4)
                    dve.reciprocal(frec[:, :], fsum[:, :]).then_inc(fx_rec, 1)
                    dve.wait_ge(fx_rec, I + 1)
                    for h in range(2):
                        for q, (a, b) in enumerate(((0, P), (P, CAUSAL))):
                            n = 2 * q + h
                            ins = dve.tensor_scalar(fx_s[:, h, a:b], fx_s[:, h, a:b], frec[:, n:n + 1], None, ALU.mult)
                    ins.then_inc(fx_norm, 1)
                    gate(2)
                    chunks(cp + 8, 1)
                    gate(3)
                    chunks(cp + 9, 1)
                    gate(4)
                    chunks(cp + 10, 1)
                    head_low(I * 3 + 2, bank[4][:, 0:TOK], o(hhi, 0), o(hlo, 0))
                    gate(5)
                    chunks(cp + 11, 1)
                    head_low(I * 3 + 3, bank[5][:, 0:TOK], o(hhi, 1), o(hlo, 1))
                c, g = c + (12 + 12 * NPAIR), g + (MEM_G + PAIR_G * NPAIR)
                for n in range(4):
                    s = slice(2 * n, 2 * n + 2)
                    for b, br in enumerate(BRANCHES):
                        dve.wait_ge(sig_done, l * 12 + (3 * n + b + 1))
                        done(c + (3 * n + b))
                        dst = work[:, s, :] if b == 0 else sq[:, 2 * b:2 * b + 2, :]
                        dve.tensor_tensor(dst, pair_bank((3 * n + b) % 2), gates[:, 8 * br + 2 * n:8 * br + 2 * n + 2, :],
                                          ALU.mult).then_inc(group_done, 1)
                        if b == 0:
                            chunks(c + 3 * n, 1)
                        if b > 0:
                            dve.wait_ge(group_done, g.count(3 * n + b + 3))
                            if b == 2:
                                dve.wait_ge(merged, l * 8 + (2 * n + 1))
                            dve.tensor_tensor(work[:, s, :], work[:, s, :], dst, ALU.add).then_inc(merged, 1)
                            chunks(c + (3 * n + b), 1)
                c, g = c + 12, g + 12
                chunks(c, KT)
                c = c + KT
                take_rstd(l * 6 + 3)
                scale_result(gain(POSTM), range(4))
                scaled_low(l * 3 + 2, gain(PRE2))
                ffn(c, g, l * 2 + 1, l * 6 + 4)
                chunks(c + (FFN_C - 2), 2)
                take_rstd(l * 6 + 5)
                scale_result(gain(POST2), range(4))
                dve.wait_ge(scaled, l * 12 + 12)

            HID = LAYERS * 2 * FT
            pgain = lambda at: par[:, at:at + KT]
            M2 = 3 * LAYERS
            scaled_low(M2, pgain(AMIX))
            for t in range(KT):
                ci = c_conv + 3 * t
                G = g_conv + 3 * t + 2
                f, b0 = t % 2, 3 * t
                if t == 0:
                    take_rstd(n_conv[0])
                    dve.tensor_tensor(rstd_sq, rstd[:, :], rstd[:, :], ALU.mult).then_inc(rstd_squared, 1)
                    dve.wait_ge(rstd_squared, 1)
                done(ci)
                dve.tensor_tensor(part(4), bank[b0 % 2][:, 0:TOK], rstd_sq, ALU.mult).then_inc(group_done, 1)
                chunks(ci, 1)
                done(ci + 1)
                dve.wait_ge(group_done, G + 1)
                dve.tensor_tensor(hf[f], bank[(b0 + 1) % 2][:, 0:TOK], part(4), ALU.mult).then_inc(group_done, 1)
                chunks(ci + 1, 1)
                dve.wait_ge(tap_done, t + 1)
                for back in (1, 2):
                    if back == 2:
                        dve.wait_ge(y_done, t * 3 + 1)
                    at = ACONV + (2 - back) * KT + t
                    dve.scalar_tensor_tensor(sg[f][:, back:TOK], hf[f][:, 0:TOK - back], par[:, at:at + 1],
                                             sg[f][:, back:TOK], ALU.mult, ALU.add).then_inc(y_done, 1)
                done(ci + 2)
                dve.wait_ge(y_done, t * 3 + 2)
                dve.tensor_tensor(sg[f], bank[(b0 + 2) % 2][:, 0:TOK], sg[f], ALU.mult).then_inc(group_done, 1)
                dve.wait_ge(group_done, G + 3)
                dve.tensor_tensor(hf[f], sg[f], rstd[:, :], ALU.mult).then_inc(y_done, 1)
                chunks(ci + 2, 1)
                dve.wait_ge(hhi_done, t + (HID + 1))
                dve.tensor_tensor(hlo[:, t, :], hf[f], hhi[:, t, :].bitcast(F32), ALU.subtract).then_inc(hlo_done, 1)
            chunks(c_aout, KT - 2)
            add_result(lambda b: done(c_aout + (2 * b + 1)))
            scaled_low(M2 + 1, pgain(FFNN))
            chunks(c_aout + (KT - 2), 2)
            conv_ffn(c_ffa, g_ffa, 0, 0, n_ffa[0])
            add_result(of_down(c_ffa + 2 * FT, 2 * LAYERS))
            scaled_low(M2 + 2, pgain(BMIX), hlo, hhi)
            scaled_low(M2 + 3, pgain(KVIN))
            chunks(c_ffa + (FFN_C - 1), 1)

            for n in range(4):
                if n == 0:
                    take_rstd(n_h2[0])
                done(c_dq + n)
                dve.tensor_tensor(qlat[:, n, :], bank[(g_dq + n) % 2][:, 0:TOK], rstd[:, :], ALU.mult).then_inc(group_done, 1)
                chunks(c_dq + n, 1)

            def take_kv(n, dst):
                done(c_kv + n)
                dve.tensor_tensor(dst, bank[(g_kv + n) % 2][:, 0:TOK], rstd[:, :], ALU.mult).then_inc(group_done, 1)

            def latent(n, first, count, src, at, factor):
                for k in range(count):
                    ins = dve.scalar_tensor_tensor(work[:, first + k, :], src[:, k, :], par[:, at + k:at + k + 1], factor,
                                                   ALU.mult, ALU.mult)
                ins.then_inc(lat_done, 1)

            def latent_low(count, at, first):
                dve.wait_ge(lat_hi, count)
                n = at.stop - at.start
                dve.tensor_tensor(hlo[:, at, :], work[:, first:first + n, :], hhi[:, at, :].bitcast(F32), ALU.subtract)\
                   .then_inc(lat_lo, 1)

            def rotate(n, raw_tile, dst):
                dve.tensor_tensor(dst, raw_tile, cosine, ALU.mult).then_inc(rp_cos, 1)
                dve.wait_ge(rp_swap, n + 1)
                dve.tensor_tensor(part(4), bank[3][:, 0:TOK], sine, ALU.mult).then_inc(rp_sin, 1)
                dve.wait_ge(rp_cos, n + 1)
                dve.wait_ge(rp_sin, n + 1)
                dve.tensor_tensor(dst, dst, part(4), ALU.add).then_inc(rp_done, 1)

            take_kv(0, ckv[:, 0, :])
            chunks(c_kv, 1)
            take_rstd(n_q[0], rstd_q)
            latent(0, 2, 4, qlat, BQ, rstd_q)
            take_kv(1, ckv[:, 1, :])
            chunks(c_kv + 1, 1)
            latent_low(1, QLAT, 2)
            take_kv(2, kr_raw)
            chunks(c_kv + 2, 1)
            dve.wait_ge(group_done, g_kv + 3 + 2)
            take_rstd(n_kv[0])
            latent(1, 0, 2, ckv, KVN, rstd[:, :])
            latent_low(2, KVLAT, 0)
            rotate(0, kr_raw, kr)
            for p in range(4):
                done(c_uqr + p)
                dve.tensor_scalar(part(p % 2), bank[(g_uqr + p) % 2][:, 0:TOK], MLA_SCALE, None, ALU.mult).then_inc(group_done, 1)
                dve.wait_ge(group_done, g_uqr + p + 3)
                chunks(c_uqr + p, 1)
                rotate(p + 1, part(p % 2), qr[:, p, :])

            def mla_max(h):
                dve.wait_ge(ls_full, h + 1)
                dve.tensor_tensor(ls(h), bank[2 + h % 2][:, 0:CAUSAL], hide, ALU.add).then_inc(ls_add, 1)
                dve.wait_ge(ls_add, h + 1)
                for q, (a, b) in enumerate(((0, P), (P, CAUSAL))):
                    dve.tensor_reduce(lmax(h)[:, q:q + 1], ls(h)[:, a:b], AX_X, ALU.max, negate=True).then_inc(ls_max, 1)

            def mla_norm(h):
                dve.wait_ge(ls_exp, 2 * h + 2)
                dve.reciprocal(lrec(h), lsum(h)).then_inc(ls_rec, 1)
                dve.wait_ge(ls_rec, h + 1)
                for q, (a, b) in enumerate(((0, P), (P, CAUSAL))):
                    ins = dve.tensor_scalar(ls(h)[:, a:b], ls(h)[:, a:b], lrec(h)[:, q:q + 1], None, ALU.mult)
                ins.then_inc(ls_norm, 1)

            def mla_low(h):
                dve.wait_ge(la_hi, h + 1)
                dve.tensor_tensor(hlo[:, h, :], bank[6 + h % 2][:, 0:TOK], hhi[:, h, :].bitcast(F32), ALU.subtract)\
                   .then_inc(la_lo, 1)

            for p in range(5):
                if p < 4:
                    chunks(c_pairs + 2 * p, 1)
                if p > 0:
                    for h in (2 * p - 2, 2 * p - 1):
                        mla_norm(h)
                if p < 4:
                    G = g_pairs + 3 * p
                    done(c_pairs + 2 * p)
                    dve.tensor_scalar(qn[:, 2 * p:2 * p + 2, :], pair_bank(G % 2), MLA_SCALE, None, ALU.mult)\
                       .then_inc(group_done, 1)
                    chunks(c_pairs + (2 * p + 1), 1)
                    done(c_pairs + (2 * p + 1))
                    dve.tensor_copy(kn[:, 2 * p:2 * p + 2, :], pair_bank((G + 1) % 2)).then_inc(group_done, 1)
                    dve.tensor_copy(vn[:, :, 2 * p:2 * p + 2, :],
                                    bank[(G + 2) % 2][:, :].rearrange("p (t h d) -> p t h d", t=TT, h=2)).then_inc(group_done, 1)
                if p > 0:
                    mla_low(2 * p - 2)
                    mla_low(2 * p - 1)
                if p < 4:
                    mla_max(2 * p)
                    mla_max(2 * p + 1)
            chunks(c_o, KT - 2)
            add_result(lambda b: done(c_o + (2 * b + 1)))
            scaled_low(M2 + 4, pgain(FFNN + KT))
            chunks(c_o + (KT - 2), 2)
            conv_ffn(c_ffb, g_ffb, 1, 1, n_ffb[0])
            add_result(of_down(c_ffb + 2 * FT, 2 * LAYERS + 1))
            dve.wait_ge(root_done, n_fin[0] + 1)
            dve.reciprocal(mrec[:, :], mmax[:, :]).then_inc(rstd_done, 1)
            dve.wait_ge(rstd_done, n_fin[0] + 1)
            for t in range(TT):
                dve.wait_ge(y_tp, 2 * t + 2)
                dve.tensor_scalar(gates[:, 4 * t + 2:4 * t + 4, :], pair_bank(5 + 2 * t), mrec[:, t:t + 1], None, ALU.mult)\
                   .then_inc(y_scaled, 1)

        @block.tensor
        def _(pe):
            def start_chunk(c):
                pe.wait_ge(lo_ready, c.count(1 + SLOTS))

            def free_bank(g):
                pe.wait_ge(group_done, g.count(1))
                return bank[g.k % 2]

            def mm3(dst, w_hi, w_lo, x_hi, x_lo, start, stop, **kw):
                pe.matmul(dst, w_hi, x_hi, start=start, stop=False, **kw)
                pe.matmul(dst, w_hi, x_lo, start=False, stop=False, **kw)
                return pe.matmul(dst, w_lo, x_hi, start=False, stop=stop, **kw)

            def project(dst, c, kts, xh, xl, width=P, at=0, ready=None):
                for k in range(kts):
                    if ready:
                        ready(k)
                    s = slice(k * width + at, k * width + at + P)
                    ins = mm3(dst, whi[c.slot][:, s], wlo[c.slot][:, s], xh[:, k, :], xl[:, k, :], k == 0, k == kts - 1)
                return ins

            def project_tokens(dst, c, kts, xh, xl, w, first=True, last=True):
                for t in range(TT):
                    rows = slice(t * P, (t + 1) * P)
                    for k in range(kts):
                        start, stop = first and t == 0 and k == 0, last and k == kts - 1
                        pe.matmul(dst(t), xh[:, k, rows], w(whi[c.slot], k), start=start, stop=False, skip_group_check=True)
                        pe.matmul(dst(t), xl[:, k, rows], w(whi[c.slot], k), start=False, stop=False, skip_group_check=True)
                        ins = pe.matmul(dst(t), xh[:, k, rows], w(wlo[c.slot], k), start=False, stop=stop, skip_group_check=True)
                return ins

            half_rows = lambda slot, k: slot[:, k * 2 * P:(k + 1) * 2 * P]

            def sum_squares(s_at, tiles, first=0):
                for k in range(tiles):
                    if k % 2 == 0:
                        pe.wait_ge(sq_done, s_at + (k // 2 + 1))
                    ins = pe.matmul(bank[2][:, 0:TOK], ones, sq[:, first + k, :], start=(k == 0), stop=(k == tiles - 1))
                ins.then_inc(ss_full, 1)

            def stream_pair(m):
                def ready(k):
                    if k % 2 == 0:
                        pe.wait_ge(ulo_done, m * 4 + (k // 2 + 1))
                return ready

            def ffn(c, g, hidden, m, s_at, use):
                def tiles(i, first=False):
                    for j in range(2):
                        ci = c.later(i) + 2 * j
                        b = free_bank(g.later(i * 2) + j)
                        start_chunk(ci)
                        project(b[:, 0:TOK], ci, KT, uhi, ulo, ready=stream_pair(m) if first and j == 0 else None)\
                            .then_inc(w_used, 1)
                        start_chunk(ci + 1)
                        project(b[:, TOK:2 * TOK], ci + 1, KT, uhi, ulo).then_inc(w_used, 1)
                        if first and j == 0:
                            sum_squares(s_at, KT)

                tiles(0, first=True)
                with pe.Fori(1, FT // 2) as i:
                    tiles(i)
                d = c + 2 * FT

                def rows(cd, k, tile, first, last, report):
                    start_chunk(cd)
                    pe.wait_ge(hlo_done, hidden + (k + 1))
                    for n in range(KT):
                        s = slice(n * P, (n + 1) * P)
                        ins = mm3(bank[4 + n // 2][:, (n % 2) * TOK:(n % 2 + 1) * TOK], whi[cd.slot][:, s], wlo[cd.slot][:, s],
                                  tile(hhi), tile(hlo), first and n % 2 == 0, last, skip_group_check=True)
                        if report and n % 2 and n < KT - 1:
                            ins.then_inc(acc_full, 1)
                    ins.then_inc(w_used, 1)

                for k in range(2):
                    rows(d + k, k, lambda t: t[:, k, :], k == 0, False, False)
                with pe.Fori(0, (FT - 2) // 4) as i:
                    for j in range(4):
                        rows((d + (2 + j)).later(i), i * 4 + (2 + j),
                             lambda t: t[:, bass.ds(i * 4 + (2 + j), 1), :].rearrange("p a n -> p (a n)"), False, True, j == 3)

            def turn(src, dst):
                return pe.transpose(dst, src, ident)

            pe.sem_inc(w_used, SLOTS)
            pe.wait_ge(cst_loaded, 16)
            pe.wait_ge(x_loaded, 16)
            xtok = work[:, :, :].rearrange("p (t a) n -> p t (a n)", t=TT)
            for k in range(KT):
                for t in range(TT):
                    ins = turn(xtok[:, t, k * P:(k + 1) * P], bank[4 + k // 2][:, (k % 2) * TOK + t * P:(k % 2) * TOK + (t + 1) * P])
                if k % 2:
                    ins.then_inc(x_tp, 1)
            pe.wait_ge(mg_loaded, 16)
            pe.transpose(bank[2][:, 0:KT], mgain_rows[:, :], ident[0:KT, 0:KT]).then_inc(mg_tp, 1)
            pe.wait_ge(m_scaled, TT)
            for k in range(KT):
                if k % 2 == 0:
                    pe.wait_ge(h_ready, k // 2 + 1)
                for t in range(TT):
                    ins = turn(mtok[:, t, k * P:(k + 1) * P], bank[4 + k // 2][:, (k % 2) * TOK + t * P:(k % 2) * TOK + (t + 1) * P])
                if k % 2:
                    ins.then_inc(m_tp, 1)
            pe.wait_ge(p_loaded, 16 * PARAM_LOADS)
            for n in range(4):
                ins = turn(param_rows[:, n, :], bank[3][:, n * P:(n + 1) * P])
            ins.then_inc(par_tp, 1)

            with pe.Fori(0, LAYERS) as l:
                c = Chunk(l * (LAYER_C // SLOTS), 0)
                g = Group(l * LAYER_G, 0)
                ffn(c, g, l * (2 * FT), l * 3, l * 24, l * 2)
                c, g = c + FFN_C, g + FFN_G
                pe.wait_ge(m_lo, 4)

                def mem_key(n):
                    b = free_bank(g + n)
                    start_chunk(c + n)
                    project(b[:, 0:TOK], c + n, KT, mhi, mlo).then_inc(w_used, 1)

                mem_key(0)
                sum_squares(l * 24 + 4, KT)
                for n in range(1, 4):
                    mem_key(n)
                sum_squares(l * 24 + 8, KT)
                for e in range(2):
                    b = free_bank(g + (4 + e))
                    for n in range(2):
                        cn = c + (4 + 2 * e + n)
                        start_chunk(cn)
                        project_tokens(lambda t: b[:, t * TOK:(t + 1) * TOK], cn, 4, mhi[:, 4 * n:4 * n + 4, :],
                                       mlo[:, 4 * n:4 * n + 4, :], half_rows, n == 0, n == 1).then_inc(w_used, 1)

                def mem_query(n, ready=None):
                    b = free_bank(g + (6 + n))
                    start_chunk(c + (8 + n))
                    project(b[:, 0:TOK], c + (8 + n), KT, uhi, ulo, ready=ready).then_inc(w_used, 1)

                mem_query(0, stream_pair(l * 3 + 1))
                pe.wait_ge(f_split, l * 2 + 4)
                for t in range(TT):
                    rows_t = slice(t * P, (t + 1) * P)
                    for k in range(KT):
                        dst = bank[3][:, t * 8:(t + 1) * 8]
                        pe.matmul(dst, uhi[:, k, rows_t], wfhi[:, k, :], start=(k == 0), stop=False)
                        pe.matmul(dst, ulo[:, k, rows_t], wfhi[:, k, :], start=False, stop=False)
                        ins = pe.matmul(dst, uhi[:, k, rows_t], wflo[:, k, :], start=False, stop=(k == KT - 1))
                ins.then_inc(f_full, 1)
                mem_query(1)
                mem_query(2)
                pe.wait_ge(f_ready, l + 1)
                pe.matmul(bank[3][:, 32:40], up_to, flog[:, 0, :], start=True, stop=True)
                pe.matmul(bank[3][:, 40:48], up_to, flog[:, 1, :], start=True, stop=False)
                pe.matmul(bank[3][:, 40:48], ones, flog[:, 0, :], start=False, stop=True)
                pe.matmul(bank[3][0:8, 64:64 + P], flog[:, 0, :], up_to, start=True, stop=True)
                pe.matmul(bank[3][0:8, 64 + P:64 + TOK], flog[:, 1, :], up_to, start=True, stop=False)
                pe.matmul(bank[3][0:8, 64 + P:64 + TOK], flog[:, 0, :], ones, start=False, stop=True).then_inc(c_full, 1)
                mem_query(3)
                with pe.Fori(0, NPAIR) as p:
                    I = l * NPAIR + p
                    cp = (c + 12).later(p * 3)
                    gp = (g + MEM_G).later(p * PAIR_G)

                    def gate(n):
                        b = free_bank(gp + (4 + n))
                        start_chunk(cp + (6 + n))
                        project(b[:, 0:TOK], cp + (6 + n), KT, uhi, ulo).then_inc(w_used, 1)

                    def feature_chunk(n):
                        b = free_bank(gp + n)
                        start_chunk(cp + n)
                        project(b[:, 0:TOK], cp + n, KT, uhi, ulo).then_inc(w_used, 1)

                    def weighted_values(dst, side, w, h):
                        f = slice(h * HD, (h + 1) * HD)
                        v = slice(side * P + h * HD, side * P + (h + 1) * HD)
                        pe.matmul(dst[f, 0:TOK], vpair[:, 0, v], w[:, h, 0:TOK], start=True, stop=False)
                        return pe.matmul(dst[f, P:TOK], vpair[:, 1, v], w[:, h, TOK:CAUSAL], start=False, stop=True)

                    feature_chunk(0)
                    pe.wait_ge(mem_staged, I * 2 + 2)
                    for q in range(TT):
                        ins = pe.matmul(bank[6][:, q * TOK:(q + 1) * TOK], qm1[:, q * P:(q + 1) * P],
                                        kmem[:, bass.ds(p, 1), :].rearrange("p a n -> p (a n)"), start=True, stop=True)
                    ins.then_inc(mem_full, 1)
                    feature_chunk(1)
                    feature_chunk(2)
                    pe.wait_ge(mem_norm, I + 1)
                    for q in range(TT):
                        for k in range(TT):
                            ins = turn(mem_p[:, q * TOK + k * P:q * TOK + (k + 1) * P],
                                       bank[7][:, k * TOK + q * P:k * TOK + (q + 1) * P])
                    ins.then_inc(mem_tp, 1)
                    feature_chunk(3)
                    pe.wait_ge(group_done, gp.count(2 + 2))
                    for h in range(2):
                        f = slice(h * HD, (h + 1) * HD)
                        pe.matmul(bank[2 + h][:, 0:TOK], ks[f, 0:P], qs[f, 0:TOK], start=True, stop=True)
                        ins = pe.matmul(bank[2 + h][:, TOK:CAUSAL], ks[f, P:TOK], qs[f, P:TOK], start=True, stop=True)
                    ins.then_inc(sbz_full, 1)
                    pe.wait_ge(olo_done, I * 3 + 1)
                    for n in range(2):
                        start_chunk(cp + (4 + n))
                        project_tokens(lambda t: bank[5][:, t * TOK:(t + 1) * TOK], cp + (4 + n), 4, uhi[:, 4 * n:4 * n + 4, :],
                                       ulo[:, 4 * n:4 * n + 4, :], half_rows, n == 0, n == 1).then_inc(w_used, 1)
                        if n == 0:
                            pe.wait_ge(mem_pt, I + 1)
                            for k in range(TT):
                                ins = pe.matmul(bank[6][:, 0:TOK], vm1[:, k, :], mem_pT[:, k * TOK:(k + 1) * TOK],
                                                start=(k == 0), stop=(k == TT - 1))
                            ins.then_inc(o_full, 1)
                    gate(0)
                    pe.wait_ge(group_done, gp.count(4 + 2))
                    pe.wait_ge(c_pair, I * 2 + 2)
                    pe.wait_ge(v_taken, I + 1)
                    for h in range(2):
                        f = slice(h * HD, (h + 1) * HD)
                        pe.matmul(bank[4 + h][:, 0:P], qf[f, 0:P], kf[f, 0:P], start=True, stop=False)
                        pe.matmul(bank[4 + h][:, 0:P], ones[0:8, :], cpair[:, h, 0:P], start=False, stop=True)
                        pe.matmul(bank[4 + h][:, P:CAUSAL], qf[f, P:TOK], kf[f, 0:TOK], start=True, stop=False)
                        ins = pe.matmul(bank[4 + h][:, P:CAUSAL], ones[0:8, :], cpair[:, h, :], start=False, stop=True)
                    ins.then_inc(fxz_full, 1)
                    gate(1)
                    pe.wait_ge(sb_masked, I + 1)
                    pe.wait_ge(olo_done, I * 3 + 2)
                    for h in range(2):
                        pe.matmul(bank[6 + h][:, 0:TOK], later_keys, sb_sp[:, h, 0:TOK], start=True, stop=False)
                        pe.matmul(bank[6 + h][:, P:TOK], ones, sb_sp[:, h, TOK:CAUSAL], start=False, stop=True)
                        ins = pe.matmul(bank[6 + h][:, TOK:CAUSAL], later_keys, sb_sp[:, h, TOK:CAUSAL], start=True, stop=True)
                    ins.then_inc(sb_cum, 1)
                    gate(2)
                    gate(3)
                    pe.wait_ge(fx_norm, I + 1)
                    for h in range(2):
                        for n in range(3):
                            ins = turn(fx_s[:, h, n * P:(n + 1) * P], bank[2 + h][:, n * P:(n + 1) * P])
                    ins.then_inc(fx_tp, 1)
                    gate(4)
                    pe.wait_ge(sb_ready, I + 1)
                    for h in range(2):
                        ins = weighted_values(bank[4], 0, sb_w, h)
                    ins.then_inc(o_full, 1)
                    gate(5)
                    pe.wait_ge(fx_pt, I * 2 + 2)
                    for h in range(2):
                        ins = weighted_values(bank[5], 1, fx_pT, h)
                    ins.then_inc(o_full, 1)
                c, g = c + (12 + 12 * NPAIR), g + (MEM_G + PAIR_G * NPAIR)
                for n in range(4):
                    for at, br in enumerate(BRANCHES):
                        m = 3 * n + at
                        b = free_bank(g + m)
                        start_chunk(c + m)
                        if n == 0:
                            pe.wait_ge(olo_done, l * (3 * NPAIR) + (3 * NPAIR + (at == 2)))
                        heads = slice(4 * br, 4 * br + 4)
                        for t in range(2):
                            ins = project(b[:, t * TOK:(t + 1) * TOK], c + m, 4, hhi[:, heads, :], hlo[:, heads, :], 2 * P, t * P)
                        ins.then_inc(w_used, 1)
                c, g = c + 12, g + 12

                def to_stream(c, xh, xl, ready):
                    for n in range(KT):
                        start_chunk(c + n)
                        project(bank[4 + n // 2][:, (n % 2) * TOK:(n % 2 + 1) * TOK], c + n, KT, xh, xl,
                                ready=ready if n == 0 else None).then_inc(w_used, 1)

                def merged_pair(k):
                    if k % 2 == 0:
                        pe.wait_ge(mgl_done, l * 4 + (k // 2 + 1))

                to_stream(c, uhi, ulo, merged_pair)
                c = c + KT
                sum_squares(l * 24 + 12, KT)
                ffn(c, g, l * (2 * FT) + FT, l * 3 + 2, l * 24 + 16, l * 2 + 1)
                sum_squares(l * 24 + 20, KT)

            M2 = 3 * LAYERS
            HID = LAYERS * 2 * FT
            for n in range(3 * KT):
                b = free_bank(Group(g_conv, n))
                start_chunk(c_conv + n)
                project(b[:, 0:TOK], c_conv + n, KT, uhi, ulo, ready=stream_pair(M2) if n == 0 else None).then_inc(w_used, 1)
                if n == 0:
                    sum_squares(n_conv[1], KT)
            to_stream(c_aout, hhi, hlo, lambda k: pe.wait_ge(hlo_done, HID + k + 1))
            ffn(c_ffa, Group(0, g_ffa), HID + KT, M2 + 1, n_ffa[1], 2 * LAYERS)
            for n in range(4):
                b = free_bank(Group(0, g_dq + n))
                start_chunk(c_dq + n)
                project(b[:, 0:TOK], c_dq + n, KT, hhi, hlo, ready=stream_pair(M2 + 2) if n == 0 else None).then_inc(w_used, 1)
                if n == 0:
                    sum_squares(n_h2[1], KT)

            def kv(n):
                b = free_bank(Group(0, g_kv + n))
                start_chunk(c_kv + n)
                project(b[:, 0:TOK], c_kv + n, KT, uhi, ulo, ready=stream_pair(M2 + 3) if n == 0 else None).then_inc(w_used, 1)

            kv(0)
            sum_squares(n_q[1], 4)
            kv(1)
            kv(2)
            sum_squares(n_kv[1], 2, 4)

            def swap_halves(n, raw_tile, group):
                pe.wait_ge(group_done, group + 3)
                if n > 0:
                    pe.wait_ge(rp_sin, n)
                pe.matmul(bank[3][:, 0:TOK], swap, raw_tile, start=True, stop=True).then_inc(rp_swap, 1)

            qh, qlo_, kvh, kvl = hhi[:, QLAT, :], hlo[:, QLAT, :], hhi[:, KVLAT, :], hlo[:, KVLAT, :]
            swap_halves(0, kr_raw, g_kv + 2)
            pe.wait_ge(lat_lo, 1)
            for p in range(4):
                b = free_bank(Group(0, g_uqr + p))
                start_chunk(c_uqr + p)
                project(b[:, 0:TOK], c_uqr + p, 4, qh, qlo_).then_inc(w_used, 1)
                if p > 0:
                    swap_halves(p, part((p - 1) % 2), g_uqr + p - 1)

            def mla_scores(h):
                if h >= 2:
                    pe.wait_ge(ls_add, h - 1)
                f = slice((h % 2) * ROPE, (h % 2 + 1) * ROPE)
                for q, (a, n) in enumerate(((0, P), (P, TOK))):
                    dst = bank[2 + h % 2][:, a:a + n]
                    rows = slice(q * P, (q + 1) * P)
                    pe.matmul(dst, qn[:, h, rows], kn[:, h, 0:n], start=True, stop=False)
                    ins = pe.matmul(dst, qr[f, h // 2, rows], kr[f, 0:n], start=False, stop=True)
                ins.then_inc(ls_full, 1)

            def mla_turn(h):
                pe.wait_ge(ls_norm, h + 1)
                for n in range(3):
                    ins = turn(ls(h)[:, n * P:(n + 1) * P], bank[4 + h % 2][:, n * P:(n + 1) * P])
                ins.then_inc(ls_tp, 1)

            def mla_values(h):
                pe.wait_ge(ls_pt, h + 1)
                if h >= 2:
                    pe.wait_ge(la_lo, h - 1)
                b = bank[6 + h % 2]
                pe.matmul(b[:, 0:TOK], vn[:, 0, h, :], lpT(h)[:, 0:TOK], start=True, stop=False)
                pe.matmul(b[:, P:TOK], vn[:, 1, h, :], lpT(h)[:, TOK:CAUSAL], start=False, stop=True).then_inc(la_full, 1)

            for p in range(5):
                G = g_pairs + 3 * p
                if p < 4:
                    cu = c_pairs + 2 * p
                    b = free_bank(Group(0, G))
                    start_chunk(cu)
                    for h in range(2):
                        ins = project(b[:, h * TOK:(h + 1) * TOK], cu, 4, qh, qlo_, 2 * P, h * P)
                    ins.then_inc(w_used, 1)
                if p == 0:
                    swap_halves(4, part(1), g_uqr + 3)
                    pe.wait_ge(lat_lo, 2)
                if p > 0:
                    mla_turn(2 * p - 2)
                    mla_turn(2 * p - 1)
                if p < 4:
                    b = free_bank(Group(0, G + 1))
                    start_chunk(cu + 1)
                    for h in range(2):
                        project(b[:, h * TOK:(h + 1) * TOK], cu + 1, 2, kvh, kvl, 512, h * 2 * P)
                    b2 = free_bank(Group(0, G + 2))
                    both_values = lambda slot, k: slot[:, k * 512:(k + 1) * 512].rearrange("p (h s d) -> p h s d", h=2, s=2)[:, :, 1, :]
                    project_tokens(lambda t: b2[:, t * TOK:(t + 1) * TOK].rearrange("p (h d) -> p h d", h=2), cu + 1, 2, kvh, kvl,
                                   both_values).then_inc(w_used, 1)
                if p > 0:
                    mla_values(2 * p - 2)
                    mla_values(2 * p - 1)
                if p < 4:
                    pe.wait_ge(group_done, G + 3 + 2)
                    pe.wait_ge(rp_done, 5)
                    mla_scores(2 * p)
                    mla_scores(2 * p + 1)
            to_stream(c_o, hhi, hlo, lambda k: pe.wait_ge(la_lo, k + 1))
            ffn(c_ffb, Group(0, g_ffb), HID + KT + FT, M2 + 4, n_ffb[1], 2 * LAYERS + 1)
            for t in range(TT):
                for b in range(2):
                    if t == 0:
                        pe.wait_ge(un_done, LAYERS * 4 + 2 * b + 2)
                    for k in range(4):
                        ins = turn(work[:, 4 * b + k, t * P:(t + 1) * P], bank[4 + 2 * t + b][:, k * P:(k + 1) * P])
                    ins.then_inc(y_tp, 1)
                if t == 0:
                    pe.wait_ge(sq_done, n_fin[1] + 4)
                    for tt in range(TT):
                        for k in range(KT):
                            ins = pe.matmul(bank[2][:, 2 * tt:2 * tt + 2], sq[:, k, tt * P:(tt + 1) * P], ones[:, 0:2],
                                            start=(k == 0), stop=(k == KT - 1))
                    ins.then_inc(ss_full, 1)


def kernel(**inputs):
    from concourse import bacc
    from concourse.bass_utils import run_bass_kernel_spmd

    nc = bacc.Bacc("TRN2", target_bir_lowering=False, num_devices=1)
    arrays, given = {}, {}
    for name, value in inputs.items():
        a = np.ascontiguousarray(value)
        arrays[f"in_{name}"] = a
        given[name] = nc.dram_tensor(f"in_{name}", a.shape, mybir.dt.from_np(a.dtype), kind="ExternalInput").ap()
    arrays["constants"] = constants()
    consts = nc.dram_tensor("constants", (P, C_COLS), F32, kind="ExternalInput").ap()
    out = nc.dram_tensor("out", (1, TOK, DM), F32, kind="ExternalOutput").ap()
    program(nc, given, consts, out)
    r = run_bass_kernel_spmd(nc, [arrays], core_ids=[0])
    return r.results[0]["out"]
```

```python
from contextlib import ExitStack

import numpy as np

import concourse.bass as bass
from concourse import mybir

F32 = mybir.dt.float32
F32R = mybir.dt.float32r
ACT = mybir.ActivationFunctionType
ALU = mybir.AluOpType
AX_X = mybir.AxisListType.X

P = 128
DM = 1024
KT = DM // P
TOK = 256
TT = TOK // P
LAYERS = 2
FF = 2816
FT = FF // P
HD = 64
NPAIR = 4
MH = 4
EPS = 1e-6
NOPE, ROPE, VD, NH = 128, 64, 128, 8
QL, KVL = 512, 256
MLA_SCALE = float((NOPE + ROPE) ** -0.5)
MEM_SCALE = float(P ** -0.5)
SB_SCALE = float(HD ** -0.5)

SLOTS = 4
AHEAD = SLOTS
CW = 1024
CAUSAL = 3 * P

FFN_C, FFN_G = 3 * FT, FT
MIX_C = 12 + 12 * NPAIR + 12 + 8
DOWN_PAIRS = 3 * ((FT - 2) // 4)
BRANCHES = (0, 2, 1)
QLAT, KVLAT = slice(8, 12), slice(12, 14)
LAYER_C = 2 * FFN_C + MIX_C
MEM_G, PAIR_G = 10, 10
LAYER_G = 2 * FFN_G + MEM_G + PAIR_G * NPAIR + 12
assert LAYER_C % SLOTS == 0 and LAYER_G % 2 == 0

LP = 72
LP_NAMES = [("ffn1_pre_g", 8), ("ffn1_post_g", 8), ("mix_pre_g", 8), ("mix_post_g", 8),
            ("ffn2_pre_g", 8), ("ffn2_post_g", 8), ("b_gate", 24)]
PRE1, POST1, PREM, POSTM, PRE2, POST2, BGATE = 0, 8, 16, 24, 32, 40, 48
AMIX = LAYERS * LP
ACONV, BMIX, BQ, KVIN, KVN = AMIX + 8, AMIX + 32, AMIX + 40, AMIX + 44, AMIX + 52
FFNN, FINAL, FCONV = AMIX + 54, AMIX + 70, AMIX + 78
PCOLS = FCONV + 2 * 3 * 2 * FT
assert PCOLS <= 512

C_ID, C_ONE, C_GT, C_LE, C_M01, C_MADD, C_PERM, C_COS, C_SIN, C_NEG8 = (
    0, 128, 256, 384, 512, 640, 1024, 1152, 1408, 1664)
C_COLS = C_NEG8 + 8
MASKED = -1e30
FIRST_PARAMS = 8


def constants():
    c = np.zeros((P, C_COLS), np.float32)
    row, col = np.arange(P)[:, None], np.arange(P)[None, :]
    c[:, C_ID:C_ID + P] = row == col
    c[:, C_ONE:C_ONE + P] = 1.0
    c[:, C_GT:C_GT + P] = row > col
    c[:, C_LE:C_LE + P] = row <= col
    c[:, C_M01:C_M01 + P] = row < col
    diagonal = np.where(col <= row, 0.0, MASKED)
    c[:, C_MADD:C_MADD + P] = diagonal
    c[:, C_MADD + 2 * P:C_MADD + 3 * P] = diagonal
    half = ROPE // 2
    c[:, C_PERM:C_PERM + P] = (row // ROPE == col // ROPE) & ((row + half) % ROPE == col % ROPE)
    inv = (1.0 / (10000.0 ** (np.arange(0, ROPE, 2, dtype=np.float32) / ROPE))).astype(np.float32)
    angle = np.arange(TOK, dtype=np.float32)[None, :] * inv[:, None]
    cos, sin = np.cos(angle), np.sin(angle)
    for p in range(0, P, ROPE):
        c[p:p + half, C_COS:C_COS + TOK] = cos
        c[p + half:p + ROPE, C_COS:C_COS + TOK] = cos
        c[p:p + half, C_SIN:C_SIN + TOK] = -sin
        c[p + half:p + ROPE, C_SIN:C_SIN + TOK] = sin
    for p in (0, HD):
        c[p:p + 8, C_NEG8:C_NEG8 + 8] = -np.eye(8)
    return c


class Chunk:

    def __init__(self, rounds, k):
        self.rounds, self.k = rounds, k

    def __add__(self, n):
        return Chunk(self.rounds, self.k + n)

    def later(self, rounds):
        return Chunk(self.rounds + rounds, self.k)

    def count(self, more=0):
        return self.rounds * SLOTS + (self.k + more)

    @property
    def slot(self):
        return self.k % SLOTS

    @property
    def uses(self):
        return self.rounds + (self.k // SLOTS + 1)


class Group:

    def __init__(self, base, k):
        self.base, self.k = base, k

    def __add__(self, n):
        return Group(self.base, self.k + n)

    def later(self, n):
        return Group(self.base + n, self.k)

    def count(self, more=0):
        return self.base + (self.k + more)


def program(nc, A, consts, out):
    ctx = ExitStack()
    with ctx:
        def sb(name, shape, dt=F32):
            return ctx.enter_context(nc.sbuf_tensor(name, shape, dt))

        def sem(name):
            return ctx.enter_context(nc.semaphore(name))

        raw = [sb(f"raw{s}", [P, CW]) for s in range(SLOTS)]
        whi = [sb(f"whi{s}", [P, CW], F32R) for s in range(SLOTS)]
        wlo = [sb(f"wlo{s}", [P, CW], F32R) for s in range(SLOTS)]
        H = sb("H", [P, KT, TOK])
        work = sb("work", [P, KT, TOK])
        sq = sb("sq", [P, KT, TOK])
        uhi, ulo = sb("uhi", [P, KT, TOK], F32R), sb("ulo", [P, KT, TOK], F32R)
        hhi, hlo = sb("hhi", [P, FT, TOK], F32R), sb("hlo", [P, FT, TOK], F32R)
        mhi, mlo = sb("mhi", [P, KT, TOK], F32R), sb("mlo", [P, KT, TOK], F32R)
        gates = sb("gates", [P, 3 * KT, TOK])
        kmem = sb("kmem", [P, MH, TOK])
        vmem = sb("vmem", [P, TT, MH, P])
        qmem = sb("qmem", [P, MH, TOK])
        small = sb("small", [P, 6 * TOK])
        par = sb("par", [P, 512])
        lp = sb("lp", [P, LP])
        mgain, mgain_rows = sb("mgain", [P, KT]), sb("mgain_rows", [KT, P])
        cst = sb("cst", [P, C_COLS])
        bfor = sb("bfor", [P, LAYERS, 8])
        wfor = sb("wfor", [P, KT, 8])
        wfhi, wflo = sb("wfhi", [P, KT, 8], F32R), sb("wflo", [P, KT, 8], F32R)
        flog, fabs = sb("flog", [P, TT, 8]), sb("fabs", [P, TT, 8])
        ctok = sb("ctok", [P, TT, 8])
        crow = sb("crow", [P, TOK])
        qx, kx1 = [sb(f"qx{h}", [P, TOK]) for h in range(2)], sb("kx1", [P, TOK])
        vm1 = sb("vm1", [P, TT, P])
        root, rstd = sb("root", [P, TOK]), sb("rstd", [P, TOK])
        fmax, fsum, frec = sb("fmax", [P, 8]), sb("fsum", [P, 8]), sb("frec", [P, 8])
        mmax, msum, mrec = sb("mmax", [P, 2]), sb("msum", [P, 2]), sb("mrec", [P, 2])

        param_rows = gates[:, 0:2, :].rearrange("p a (b n) -> p (a b) n", n=P)
        mtok = gates[:, 8:16, :].rearrange("p (t a) n -> p t (a n)", t=TT)
        flat = lambda t: t[:, :, :].rearrange("p a b -> p (a b)")
        ident, ones = cst[:, C_ID:C_ID + P], cst[:, C_ONE:C_ONE + P]
        exact = cst[:, C_ONE:C_GT + P]
        later_keys, up_to = cst[:, C_GT:C_GT + P], cst[:, C_LE:C_LE + P]
        before = cst[:, C_M01:C_M01 + P]
        hide = cst[:, C_MADD:C_MADD + CAUSAL]
        swap = cst[:, C_PERM:C_PERM + P]
        cosine, sine = cst[:, C_COS:C_COS + TOK], cst[:, C_SIN:C_SIN + TOK]

        def two(t, a):
            return flat(t)[:, a:a + 2 * CAUSAL].rearrange("p (h c) -> p h c", h=2)

        rstd_pair = rstd[:, :].unsqueeze(1).to_broadcast([P, 2, TOK])
        sb_e, sb_sp = two(sq, 0), two(sq, 2 * CAUSAL)
        HEADS = 3 * NPAIR
        sb_hi, sb_lo = two(hhi, HEADS * TOK), two(hlo, HEADS * TOK)
        exact_r = hhi[:, HEADS + 2 * CAUSAL // TOK, :]
        fx_pT = sb_e
        mem_p = flat(sq)[:, 4 * CAUSAL:4 * CAUSAL + 512]
        sb_w, fx_s = two(work, 0), two(work, 2 * CAUSAL)
        mem_pT = flat(work)[:, 4 * CAUSAL:4 * CAUSAL + 512]
        part = lambda n: small[:, n * TOK:(n + 1) * TOK]
        qs, ks = part(0), part(1)
        kx = [part(2), kx1[:, :]]
        qm1 = part(3)
        features = [slice(0, HD), slice(HD, P)]
        c_rows = [slice(HD, HD + 8), slice(0, 8)]
        contracted = [slice(0, HD + 8), slice(0, P)]
        vpair = small[:, 4 * TOK:6 * TOK].rearrange("p (t n) -> p t n", t=TT)
        sg = [part(0), part(1)]
        hf = [part(2), part(3)]
        zz = [flat(gates)[:, n * 512:(n + 1) * 512].rearrange("p (s n) -> p s n", s=2) for n in range(2)]
        conv_y = [flat(gates)[:, n * 512:(n + 1) * 512] for n in (2, 3)]
        rstd_sq, rstd_q = part(5), part(5)
        kn = gates[:, 0:8, :]
        vn = flat(gates)[:, 2048:4096].rearrange("p (t h d) -> p t h d", t=TT, h=NH)
        qn = gates[:, 16:24, :]
        ckv, kr_raw, kr = kmem[:, 0:2, :], kmem[:, 2, :], kmem[:, 3, :]
        qlat = vmem[:, :, :, :].rearrange("p t h d -> p (t h) d").rearrange("p (k a) d -> p k (a d)", a=2)
        qr = qmem

        fourth = lambda t, h, n: t[:, (h % 4) * n:(h % 4 + 1) * n]
        ls = lambda h: fourth(flat(sq), h, CAUSAL)
        lpT = lambda h: fourth(flat(work), h, CAUSAL)
        lmax, lsum, lrec = (lambda h, t=t: fourth(t, h, 2) for t in (fmax, fsum, frec))

        bank = [ctx.enter_context(nc.psum_tensor(f"bank{n}", [P, 512], F32)) for n in range(8)]
        pair_bank = lambda n: bank[n][:, :].rearrange("p (t n) -> p t n", t=2)
        last_block = bank[7][:, 0:2 * P].rearrange("p (h n) -> p h n", h=2)

        w_loaded = [sem(f"w_loaded{s}") for s in range(SLOTS)]
        hi_ready = sem("hi_ready")
        lo_ready = sem("lo_ready")
        w_used = sem("w_used")
        group_done = sem("group_done")
        sq_done = sem("sq_done")
        sq_summed = sem("sq_summed")
        ss_full = sem("ss_full")
        root_done = sem("root_done")
        rstd_done = sem("rstd_done")
        acc_full = sem("acc_full")
        scaled = sem("scaled")
        h_ready = sem("h_ready")
        un_done = sem("un_done")
        uhi_done = sem("uhi_done")
        ulo_done = sem("ulo_done")
        silu_done, hid_done, hhi_done, hlo_done = sem("silu_done"), sem("hid_done"), sem("hhi_done"), sem("hlo_done")
        tap_done, conv_done, y_done = sem("tap_done"), sem("conv_done"), sem("y_done")
        rstd_squared = sem("rstd_squared")
        mg_loaded, mg_tp, mg_ready = sem("mg_loaded"), sem("mg_tp"), sem("mg_ready")
        zeroed = sem("zeroed")
        f_full, f_biased, f_log, f_ready = sem("f_full"), sem("f_biased"), sem("f_log"), sem("f_ready")
        f_split = sem("f_split")
        wf_loaded = sem("wf_loaded")
        c_full, c_ready = sem("c_full"), sem("c_ready")
        mem_full, mem_max, mem_exp, mem_rec, mem_norm = (sem(n) for n in ("mem_full", "mem_max", "mem_exp", "mem_rec", "mem_norm"))
        mem_staged, mem_tp, mem_pt = sem("mem_staged"), sem("mem_tp"), sem("mem_pt")
        sbz_full, sb_act, sb_dve, sb_masked = sem("sbz_full"), sem("sb_act"), sem("sb_dve"), sem("sb_masked")
        sb_high, sb_split, cst_rounded = sem("sb_high"), sem("sb_split"), sem("cst_rounded")
        sb_cum, sb_lw, sb_exp, sb_ready = sem("sb_cum"), sem("sb_lw"), sem("sb_exp"), sem("sb_ready")
        fxz_full, fx_add, fx_max, fx_exp, fx_rec, fx_norm = (sem(n) for n in ("fxz_full", "fx_add", "fx_max", "fx_exp", "fx_rec", "fx_norm"))
        fx_rows = sem("fx_rows")
        fx_tp, fx_pt = sem("fx_tp"), sem("fx_pt")
        c_pair, v_taken = sem("c_pair"), sem("v_taken")
        o_full, ohi_done, olo_done = sem("o_full"), sem("ohi_done"), sem("olo_done")
        sig_done, gated, merged, mgh_done, mgl_done = (sem(n) for n in ("sig_done", "gated", "merged", "mgh_done", "mgl_done"))
        cst_loaded, x_loaded, m_loaded, p_loaded, bf_loaded = (sem(n) for n in ("cst_loaded", "x_loaded", "m_loaded", "p_loaded", "bf_loaded"))
        par_tp, par_ready, x_tp, lp_ready = sem("par_tp"), sem("par_ready"), sem("x_tp"), sem("lp_ready")
        m_sq, m_root, m_rstd, m_scaled, m_tp, m_gain, m_hi, m_lo = (
            sem(n) for n in ("m_sq", "m_root", "m_rstd", "m_scaled", "m_tp", "m_gain", "m_hi", "m_lo"))
        rp_swap, rp_cos, rp_sin, rp_done = (sem(n) for n in ("rp_swap", "rp_cos", "rp_sin", "rp_done"))
        lat_done, lat_hi, lat_lo = sem("lat_done"), sem("lat_hi"), sem("lat_lo")
        ls_full, ls_add, ls_max, ls_exp, ls_rec, ls_norm, ls_tp, ls_pt = (
            sem(n) for n in ("ls_full", "ls_add", "ls_max", "ls_exp", "ls_rec", "ls_norm", "ls_tp", "ls_pt"))
        la_full, la_hi, la_lo = sem("la_full"), sem("la_hi"), sem("la_lo")
        y_tp, y_copied, y_scaled, y_stored = sem("y_tp"), sem("y_copied"), sem("y_scaled"), sem("y_stored")

        param_pieces = []
        at = 0
        for src, k in [(A[n], LAYERS * k) for n, k in LP_NAMES] + [
                (A["a_mix_norm_2"][0], 8), (A["a_conv_2"][0], 24), (A["b_mix_norm_2"][0], 8), (A["b_q_norm_2"][0], 4),
                (A["kv_in_norm_2"], 8), (A["kv_norm_2"], 2), (A["ffn_norm_2"], 16), (A["final_norm_2"], 8),
                (A["ffn_conv_2"], 264)]:
            if len(src.shape) == 3:
                src = src.rearrange("a b (k p) -> (a b k) p", p=P)
            elif len(src.shape) == 2:
                src = src.rearrange("a (k p) -> (a k) p", p=P)
            else:
                src = src.rearrange("(k p) -> k p", p=P)
            done = 0
            while done < k:
                r = at % P
                m = min(k - done, P - r)
                param_pieces.append((param_rows[r:r + m, at // P, :], src[done:done + m, :]))
                at += m
                done += m
        assert at == PCOLS

        C2, G2 = LAYERS * LAYER_C, LAYERS * LAYER_G
        rounds2 = C2 // SLOTS
        c_conv = Chunk(rounds2, 0)
        c_aout = c_conv + 3 * KT
        c_ffa = c_aout + KT
        c_dq = c_ffa + FFN_C
        c_kv = c_dq + 4
        c_uqr = c_kv + 3
        c_pairs = c_uqr + 4
        c_o = c_pairs + 8
        c_ffb = c_o + KT
        CHUNKS = C2 + c_ffb.k + FFN_C
        g_conv = G2
        g_ffa = g_conv + 3 * KT
        g_dq = g_ffa + FFN_G
        g_kv = g_dq + 4
        g_uqr = g_kv + 3
        g_pairs = g_uqr + 4
        g_ffb = g_pairs + 12
        N2, S2 = 6 * LAYERS, 24 * LAYERS
        n_conv, n_ffa, n_h2, n_q, n_kv, n_ffb, n_fin = (
            (N2, S2), (N2 + 1, S2 + 4), (N2 + 2, S2 + 8), (N2 + 3, S2 + 12), (N2 + 4, S2 + 14),
            (N2 + 5, S2 + 15), (N2 + 6, S2 + 19))

        block = ctx.enter_context(nc.Block())

        @block.sync
        def _(sp):
            def load(c, halves):
                pieces = halves(raw[c.slot])
                sp.wait_ge(lo_ready, c.count(1))
                for dst, src in pieces:
                    sp.dma_start(dst, src).then_inc(w_loaded[c.slot], 16)

            def place(at):
                return at if isinstance(at, int) else sp.snap(at)

            def cols(w, kt, at, n, rows=0, into=0, width=None):
                def halves(slot):
                    width_ = width or n
                    d = slot[:, 0:kt * width_].rearrange("p (k n) -> p k n", k=kt)[:, :, into:into + n]
                    s = w.rearrange("(k p) n -> p k n", p=P)[:, rows:rows + kt, bass.ds(place(at), n)]
                    m = kt // 2
                    return [(d[:, m:kt, :], s[:, m:kt, :]), (d[:, 0:m, :], s[:, 0:m, :])]
                return halves

            def sides(w, kt, n, ats, rows=0):
                def halves(slot):
                    d = slot[:, 0:kt * 2 * n].rearrange("p (k s n) -> p k s n", k=kt, s=2)
                    s = w.rearrange("(k p) n -> p k n", p=P)
                    return [(d[:, :, j, :], s[:, rows:rows + kt, bass.ds(place(a), n)]) for j, a in enumerate(ats)]
                return halves

            def rows_of(w, k):
                def halves(slot):
                    s = w[bass.ds(place(k * P), P), :]
                    return [(slot[:, CW // 2:CW], s[:, CW // 2:CW]), (slot[:, 0:CW // 2], s[:, 0:CW // 2])]
                return halves

            def ffn(c, w_gate, g_at, w_up, u_at, w_down):
                with sp.Fori(0, FT // 2) as i:
                    for j in range(2):
                        load(c.later(i) + 2 * j, cols(w_gate, KT, i * (2 * P) + (g_at + j * P), P))
                        load(c.later(i) + (2 * j + 1), cols(w_up, KT, i * (2 * P) + (u_at + j * P), P))
                down = c + 2 * FT
                for k in range(2):
                    load(down + k, rows_of(w_down, k))
                with sp.Fori(0, (FT - 2) // 4) as i:
                    for j in range(4):
                        load((down + (2 + j)).later(i), rows_of(w_down, i * 4 + (2 + j)))

            sp.dma_start(ident, consts[:, C_ID:C_ID + P]).then_inc(cst_loaded, 16)
            sp.dma_start(work[:, :, :].rearrange("p (t a) n -> p t (a n)", t=TT),
                         A["x"].rearrange("a (t p) d -> p (a t) d", p=P)).then_inc(x_loaded, 16)
            sp.dma_start(mtok, A["mem"].rearrange("a (t p) d -> p (a t) d", p=P)).then_inc(m_loaded, 16)
            sp.dma_start(mgain_rows[:, :], A["mem_norm_g"].rearrange("(k p) -> k p", p=P)).then_inc(mg_loaded, 16)
            for dst, src in param_pieces[:FIRST_PARAMS]:
                sp.dma_start(dst, src).then_inc(p_loaded, 16)
            with sp.Fori(0, LAYERS) as l:
                of = lambda name: A[name][bass.ds(l, 1), :, :].rearrange("a k n -> (a k) n")
                c = Chunk(l * (LAYER_C // SLOTS), 0)
                ffn(c, of("ffn1_w_gate"), 0, of("ffn1_w_up"), 0, of("ffn1_w_down"))
                c = c + FFN_C
                w_in, w_mem, w_gate = of("w_in"), of("w_mem_kv"), of("w_gate")
                sp.wait_ge(f_split, l * 2 + 2)
                sp.dma_start(wfor[:, :, :], w_in.rearrange("(k p) n -> p k n", p=P)[:, :, 3072:3080])\
                  .then_inc(wf_loaded, 16)
                for n in range(4):
                    load(c + n, cols(w_mem, KT, n * P, P))
                for n in range(4):
                    load(c + (4 + n), cols(w_mem, 4, MH * P + (n // 2) * (2 * P), 2 * P, rows=4 * (n % 2)))
                for h in range(MH):
                    load(c + (8 + h), cols(w_in, KT, 3080 + h * P, P))
                with sp.Fori(0, NPAIR) as p:
                    cp = (c + 12).later(p * 3)
                    for n, part_at in enumerate((0, 1, 3, 4)):
                        load(cp + n, cols(w_in, KT, p * P + part_at * 512, P))
                    for n in range(2):
                        load(cp + (4 + n), sides(w_in, 4, P, (p * P + 2 * 512, p * P + 5 * 512), rows=4 * n))
                    for n in range(6):
                        load(cp + (6 + n), cols(w_gate, KT, p * (6 * P) + n * P, P))
                c = c + (12 + 12 * NPAIR)
                branches = [of(n) for n in ("w_br_sb", "w_br_fox", "w_br_mem")]
                for j in range(4):
                    for n, b in enumerate(BRANCHES):
                        load(c + (3 * j + n), cols(branches[b], 4, j * 2 * P, 2 * P))
                c = c + 12
                w_out = of("w_out")
                for n in range(KT):
                    load(c + n, cols(w_out, KT, n * P, P))
                c = c + KT
                ffn(c, of("ffn2_w_gate"), 0, of("ffn2_w_up"), 0, of("ffn2_w_down"))
            a_in = A["a_w_in_2"][0]
            with sp.Fori(0, 2) as i:
                for f in range(4):
                    for n, part_at in enumerate((DM, 2 * DM, 0)):
                        load(c_conv.later(i * 3) + (3 * f + n), cols(a_in, KT, i * (4 * P) + (part_at + f * P), P))
            for n in range(KT):
                load(c_aout + n, cols(A["a_w_out_2"][0], KT, n * P, P))
            ffn(c_ffa, A["ffn_w_up_2"][0], 0, A["ffn_w_up_2"][0], FF, A["ffn_w_down_2"][0])
            for n in range(4):
                load(c_dq + n, cols(A["b_w_dq_2"][0], KT, n * P, P))
            for n in range(2):
                load(c_kv + n, cols(A["w_dkv_2"], KT, n * P, P))
            load(c_kv + 2, sides(A["w_dkv_2"], KT, ROPE, (KVL, KVL)))
            w_uq, w_ukv = A["b_w_uq_2"][0], A["w_ukv_2"]
            HQ = NOPE + ROPE
            for p in range(4):
                load(c_uqr + p, sides(w_uq, 4, ROPE, (2 * p * HQ + NOPE, (2 * p + 1) * HQ + NOPE)))
            for p in range(4):
                load(c_pairs + 2 * p, cols(w_ukv, 2, p * 512, 512))
                load(c_pairs + (2 * p + 1), sides(w_uq, 4, NOPE, (2 * p * HQ, (2 * p + 1) * HQ)))
            for n in range(KT):
                load(c_o + n, cols(A["b_w_o_2"][0], KT, n * P, P))
            ffn(c_ffb, A["ffn_w_up_2"][1], 0, A["ffn_w_up_2"][1], FF, A["ffn_w_down_2"][1])
            for t in range(TT):
                sp.wait_ge(y_copied, t + 1)
                sp.wait_ge(y_scaled, t + 1)
                sp.dma_start(out[0, t * P:(t + 1) * P, :], gates[:, 4 * t:4 * t + 4, :].rearrange("p a n -> p (a n)"))\
                  .then_inc(y_stored, 16)
            sp.wait_ge(y_stored, 16 * TT)

        @block.gpsimd
        def _(pool):
            pool.memset(param_rows[:, 3, :], 0.0).then_inc(zeroed, 1)
            pool.wait_ge(zeroed, 1)
            pool.memset(qx[0][:, :], 1.0).then_inc(fx_rows, 1)
            pool.wait_ge(fx_rows, 1)
            pool.memset(qx[1][:, :], 1.0).then_inc(fx_rows, 1)
            pool.wait_ge(fx_rows, 2)
            pool.memset(kx[1], 0.0).then_inc(fx_rows, 1)
            pool.wait_ge(fx_rows, 3)

            def add_scaled(first):
                for b in range(4):
                    pool.wait_ge(scaled, first + (b + 1))
                    s = slice(2 * b, 2 * b + 2)
                    pool.tensor_tensor(H[:, s, :], H[:, s, :], work[:, s, :], ALU.add).then_inc(h_ready, 1)

            def sum_squares(s_at, n):
                for b in range(1, 4):
                    pool.wait_ge(sq_done, s_at + (b + 1))
                    if b > 1:
                        pool.wait_ge(sq_summed, n * 3 + (b - 1))
                    pool.tensor_tensor(sq[:, 0:2, :], sq[:, 0:2, :], sq[:, 2 * b:2 * b + 2, :], ALU.add).then_inc(sq_summed, 1)

            def low(m):
                for b in range(4):
                    pool.wait_ge(uhi_done, m * 4 + (b + 1))
                    s = slice(2 * b, 2 * b + 2)
                    pool.tensor_tensor(ulo[:, s, :], work[:, s, :], uhi[:, s, :].bitcast(F32), ALU.subtract)\
                        .then_inc(ulo_done, 1)

            def conv_ffn(use):
                before_it = LAYERS * 2 * FT + KT
                with pool.Fori(0, FT // 2) as i:
                    for j in range(2):
                        f = i * 2 + (j + use * FT)
                        pool.wait_ge(hhi_done, f + (before_it + 1))
                        at = lambda t: t[:, bass.ds(i * 2 + j, 1), :].rearrange("p a n -> p (a n)")
                        pool.tensor_tensor(at(hlo), hf[j], at(hhi).bitcast(F32), ALU.subtract).then_inc(hlo_done, 1)

            for b in range(4):
                pool.wait_ge(m_hi, b + 1)
                s = slice(2 * b, 2 * b + 2)
                pool.tensor_tensor(mlo[:, s, :], gates[:, 16 + 2 * b:18 + 2 * b, :], mhi[:, s, :].bitcast(F32), ALU.subtract)\
                    .then_inc(m_lo, 1)

            diag = lambda t: t.rearrange("p h (a n) -> p h a n", n=P)[:, :, 0:3:2, :]
            mask = before.unsqueeze(1).unsqueeze(1).to_broadcast([P, 2, 2, P])
            with pool.Fori(0, LAYERS) as l:
                add_scaled(l * 12)
                sum_squares(l * 24 + 8, l * 6 + 2)
                low(l * 3 + 1)
                with pool.Fori(0, NPAIR) as p:
                    I = l * NPAIR + p
                    pool.wait_ge(sb_dve, I * 2 + 2)
                    pool.tensor_tensor(diag(sb_sp), diag(sb_sp), mask, ALU.mult).then_inc(sb_masked, 1)
                    pool.wait_ge(sb_high, I + 1)
                    pool.tensor_tensor(sb_lo, sb_sp, sb_hi.bitcast(F32), ALU.subtract).then_inc(sb_split, 1)
                    pool.wait_ge(sb_exp, I + 1)
                    pool.tensor_tensor(diag(sb_w), diag(sb_w), mask, ALU.mult).then_inc(sb_ready, 1)
                for n in range(4):
                    s = slice(2 * n, 2 * n + 2)
                    pool.wait_ge(mgh_done, l * 4 + (n + 1))
                    pool.tensor_tensor(ulo[:, s, :], work[:, s, :], uhi[:, s, :].bitcast(F32), ALU.subtract).then_inc(mgl_done, 1)
                add_scaled(l * 12 + 4)
                add_scaled(l * 12 + 8)
            sum_squares(n_ffa[1], n_ffa[0])
            conv_ffn(0)
            for n in range(5):
                raw_tile, dst = (kr_raw, kr) if n == 0 else (part((n - 1) % 2), qr[:, n - 1, :])
                pool.wait_ge(group_done, g_kv + 2 + 3 if n == 0 else g_uqr + n - 1 + 3)
                pool.tensor_tensor(dst, raw_tile, cosine, ALU.mult).then_inc(rp_cos, 1)
                pool.wait_ge(rp_cos, n + 1)
                pool.wait_ge(rp_sin, n + 1)
                pool.tensor_tensor(dst, dst, part(2 + n % 2), ALU.add).then_inc(rp_done, 1)
            sum_squares(n_ffb[1], n_ffb[0] - 2)
            conv_ffn(1)

        @block.scalar
        def _(act):
            def hi(c):
                if isinstance(c.rounds, int) and c.count() >= CHUNKS:
                    return
                act.wait_ge(w_loaded[c.slot], c.uses * 32)
                act.wait_ge(w_used, c.count(1))
                act.activation(whi[c.slot][:, :], raw[c.slot][:, :], ACT.Copy).then_inc(hi_ready, 1)

            def chunks(c, n):
                for j in range(n):
                    hi(c + (AHEAD + j))

            def take_root(n, width):
                act.wait_ge(ss_full, n + 1)
                act.activation(root[:, :], bank[2][:, 0:TOK], ACT.Sqrt, scale=1.0 / width, bias=EPS)\
                   .then_inc(root_done, 1)

            def squares_of_stream(version, pairs=range(4)):
                for b in pairs:
                    act.wait_ge(h_ready, version * 4 + (b + 1))
                    s = slice(2 * b, 2 * b + 2)
                    act.activation(sq[:, s, :], H[:, s, :], ACT.Square).then_inc(sq_done, 1)

            def result_pair(b, c, use):
                if b < 3:
                    act.wait_ge(acc_full, use * DOWN_PAIRS + (DOWN_PAIRS - 3 + b + 1))
                else:
                    act.wait_ge(w_used, c.count(FT + SLOTS))

            def square_pair(b):
                act.activation(sq[:, 2 * b:2 * b + 2, :], pair_bank(4 + b), ACT.Square).then_inc(sq_done, 1)

            def scaled_high(version, gain, dst=uhi, pairs=range(4)):
                for b in pairs:
                    act.wait_ge(h_ready, version * 4 + (b + 1))
                    for k in (2 * b, 2 * b + 1):
                        ins = act.activation(dst[:, k, :], H[:, k, :], ACT.Copy, scale=gain[:, k:k + 1])
                    ins.then_inc(uhi_done, 1)

            def beside_stream(version, gain, c):
                for b in range(4):
                    if b < 3:
                        chunks(c + 2 * b, 2)
                    scaled_high(version, gain, pairs=[b])
                    squares_of_stream(version, [b])

            def tile(t, n):
                return t[:, bass.ds(n, 1), :].rearrange("p a n -> p (a n)")

            def ffn(c, g, use, n):
                def tiles(i, first=False):
                    ci = c.later(i)

                    def silu(j):
                        act.wait_ge(group_done, g.base + i * 2 + (g.k + j + 3))
                        act.activation(sg[j], zz[j][:, 0, :], ACT.Silu).then_inc(silu_done, 1)

                    def high(j):
                        act.wait_ge(hid_done, use * FT + (i * 2 + (j + 1)))
                        act.activation(tile(hhi, i * 2 + j), hf[j], ACT.Copy).then_inc(hhi_done, 1)

                    chunks(ci, 2)
                    if first:
                        take_root(n, DM)
                        act.preload_act_table(ACT.Silu)
                    silu(0)
                    chunks(ci + 2, 1)
                    high(0)
                    chunks(ci + 3, 1)
                    silu(1)
                    high(1)

                tiles(0, first=True)
                with act.Fori(1, FT // 2) as i:
                    tiles(i)
                down(c + 2 * FT)
                act.preload_act_table(ACT.Sqrt)

            def down(c):
                turns = (FT - 2) // 4
                last = isinstance(c.rounds, int) and c.count(FT) > CHUNKS
                with act.Fori(0, turns - last) as i:
                    chunks(c.later(i), 4)
                if last:
                    chunks(c + 4 * (turns - 1), 4)

            def conv_ffn(c, g, use, layer, n):
                taps = FCONV + layer * 6 * FT
                before_it = LAYERS * 2 * FT

                def tiles(i, first=False):
                    ci = c.later(i)
                    f0 = i * 2 + use * FT

                    def newest_tap(j):
                        act.wait_ge(group_done, i * 2 + (g + j + 3))
                        for s in range(2):
                            act.activation(conv_y[j][:, s * TOK:(s + 1) * TOK], zz[j][:, s, :], ACT.Copy,
                                           scale=par[:, bass.ds(i * 2 + (taps + 4 * FT + s * FT + j), 1)]).then_inc(tap_done, 1)

                    def silu(j):
                        act.wait_ge(conv_done, (f0 + j) * 4 + 3)
                        act.activation(sg[j], conv_y[j][:, 0:TOK], ACT.Silu).then_inc(silu_done, 1)

                    def high(j):
                        act.wait_ge(hid_done, f0 + (j + before_it + 1))
                        act.activation(tile(hhi, i * 2 + j), hf[j % 2], ACT.Copy).then_inc(hhi_done, 1)

                    chunks(ci + 1, 1)
                    if first:
                        take_root(n, DM)
                        act.preload_act_table(ACT.Silu)
                    else:
                        high(-1)
                    newest_tap(0)
                    chunks(ci + 2, 1)
                    silu(0)
                    chunks(ci + 3, 1)
                    high(0)
                    newest_tap(1)
                    chunks(ci + 4, 1)
                    silu(1)

                chunks(c, 1)
                tiles(0, first=True)
                with act.Fori(1, FT // 2) as i:
                    tiles(i)
                act.wait_ge(hid_done, (use + 1) * FT + before_it)
                act.activation(hhi[:, FT - 1, :], hf[1], ACT.Copy).then_inc(hhi_done, 1)
                down(c + (2 * FT + 1))

            def head_high(count, src, dst):
                act.wait_ge(o_full, count)
                act.activation(dst, src, ACT.Copy).then_inc(ohi_done, 1)

            act.wait_ge(zeroed, 1)
            for dst, src in param_pieces[FIRST_PARAMS:]:
                act.dma_start(dst, src).then_inc(p_loaded, 16)
            act.dma_start(bfor[:, :, :].rearrange("p l h -> p (l h)"),
                           A["b_forget"].rearrange("l h -> (l h)").partition_broadcast(P)).then_inc(bf_loaded, 16)
            act.dma_start(cst[:, P:C_COLS], consts[:, P:C_COLS]).then_inc(cst_loaded, 16)

            act.preload_act_table(ACT.Sqrt)
            act.wait_ge(m_loaded, 16)
            for t in range(TT):
                act.activation(flat(sq)[:, t * DM:(t + 1) * DM], mtok[:, t, :], ACT.Square,
                               accum_out=msum[:, t:t + 1]).then_inc(m_sq, 1)
            act.wait_ge(m_sq, TT)
            act.activation(mmax[:, :], msum[:, :], ACT.Sqrt, scale=1.0 / DM, bias=EPS).then_inc(m_root, 1)
            for n in range(SLOTS):
                hi(Chunk(0, n))
            for b in range(4):
                act.wait_ge(m_gain, 2 * b + 2)
                act.activation(mhi[:, 2 * b:2 * b + 2, :], gates[:, 16 + 2 * b:18 + 2 * b, :], ACT.Copy).then_inc(m_hi, 1)

            with act.Fori(0, LAYERS) as l:
                c = Chunk(l * (LAYER_C // SLOTS), 0)
                g = Group(l * LAYER_G, 0)
                gain = lambda at: lp[:, at:at + KT]
                act.wait_ge(par_ready, 3)
                scaled_high(l * 3, par[:, bass.ds(l * KT + PRE1 * LAYERS, KT)])
                squares_of_stream(l * 3)
                ffn(c, g, l * 2, l * 6)
                for b in range(4):
                    result_pair(b, c + 2 * FT, l * 2)
                    square_pair(b)
                c, g = c + FFN_C, g + FFN_G
                chunks(c + (-2), 2)
                take_root(l * 6 + 1, DM)
                chunks(c, 1)
                squares_of_stream(l * 3 + 1)
                chunks(c + 1, 5)
                take_root(l * 6 + 2, DM)
                act.preload_act_table_set("natural_log_exp_and_others")
                for b in range(4):
                    act.wait_ge(un_done, l * 4 + (b + 1))
                    s = slice(2 * b, 2 * b + 2)
                    act.activation(uhi[:, s, :], work[:, s, :], ACT.Copy).then_inc(uhi_done, 1)
                chunks(c + 6, 2)
                act.wait_ge(wf_loaded, l * 16 + 16)
                act.activation(wfhi[:, :, :], wfor[:, :, :], ACT.Copy).then_inc(f_split, 1)
                chunks(c + 8, 1)
                act.wait_ge(f_biased, l + 1)
                act.activation(fabs[:, :, :], flog[:, :, :], ACT.Abs).then_inc(f_log, 1)
                act.wait_ge(f_log, l * 3 + 1)
                act.activation(fabs[:, :, :], fabs[:, :, :], ACT.Exp, scale=-1.0).then_inc(f_log, 1)
                act.wait_ge(f_log, l * 3 + 2)
                act.activation(fabs[:, :, :], fabs[:, :, :], ACT.Ln, bias=1.0).then_inc(f_log, 1)
                chunks(c + 9, 3)
                act.wait_ge(cst_loaded, 32)
                act.activation(exact_r, exact, ACT.Copy).then_inc(cst_rounded, 1)
                with act.Fori(0, NPAIR) as p:
                    I = l * NPAIR + p
                    cp = (c + 12).later(p * 3)
                    o = lambda branch: tile(hhi, p + 4 * branch)
                    chunks(cp, 1)
                    act.wait_ge(mem_max, I + 1)
                    for q in range(TT):
                        act.activation(mem_p[:, q * TOK:(q + 1) * TOK], bank[6][:, q * TOK:(q + 1) * TOK], ACT.Exp,
                                       bias=mmax[:, q:q + 1], accum_out=msum[:, q:q + 1]).then_inc(mem_exp, 1)
                    chunks(cp + 1, 3)
                    act.wait_ge(mem_tp, I + 1)
                    act.activation(mem_pT, bank[7][:, :], ACT.Copy).then_inc(mem_pt, 1)
                    act.wait_ge(sbz_full, I + 1)
                    act.activation(sb_e[:, 0, :], bank[2][:, 0:CAUSAL], ACT.Abs).then_inc(sb_act, 1)
                    act.activation(sb_e[:, 1, :], bank[3][:, 0:CAUSAL], ACT.Abs).then_inc(sb_act, 1)
                    act.wait_ge(sb_act, I * 4 + 2)
                    act.activation(sb_e, sb_e, ACT.Exp, scale=-1.0).then_inc(sb_act, 1)
                    chunks(cp + 4, 1)
                    act.wait_ge(sb_act, I * 4 + 3)
                    act.activation(sb_e, sb_e, ACT.Ln, bias=1.0).then_inc(sb_act, 1)
                    head_high(I * 3 + 1, bank[6][:, 0:TOK], o(2))
                    chunks(cp + 5, 2)
                    act.wait_ge(sb_masked, I + 1)
                    act.activation(sb_hi, sb_sp, ACT.Copy).then_inc(sb_high, 1)
                    chunks(cp + 7, 1)
                    act.wait_ge(fx_max, I * 2 + 2)
                    for h in range(2):
                        for q, (a, b) in enumerate(((0, P), (P, CAUSAL))):
                            n = 2 * q + h
                            act.activation(fx_s[:, h, a:b], fx_s[:, h, a:b], ACT.Exp, bias=fmax[:, n:n + 1],
                                           accum_out=fsum[:, n:n + 1]).then_inc(fx_exp, 1)
                    chunks(cp + 8, 1)
                    act.wait_ge(sb_lw, I * 2 + 2)
                    act.activation(sb_w, sb_w, ACT.Exp).then_inc(sb_exp, 1)
                    chunks(cp + 9, 1)
                    act.wait_ge(fx_tp, I + 1)
                    for h in range(2):
                        act.activation(fx_pT[:, h, :], bank[2 + h][:, 0:CAUSAL], ACT.Copy).then_inc(fx_pt, 1)
                    chunks(cp + 10, 1)
                    head_high(I * 3 + 2, bank[4][:, 0:TOK], o(0))
                    chunks(cp + 11, 1)
                    head_high(I * 3 + 3, bank[5][:, 0:TOK], o(1))
                c, g = c + (12 + 12 * NPAIR), g + (MEM_G + PAIR_G * NPAIR)
                act.wait_ge(group_done, g.count(2))
                def sigmoids(n):
                    for b in BRANCHES:
                        s = slice(8 * b + 2 * n, 8 * b + 2 * n + 2)
                        act.activation(gates[:, s, :], gates[:, s, :], ACT.Sigmoid).then_inc(sig_done, 1)

                def merged_high(n):
                    act.wait_ge(merged, l * 8 + (2 * n + 2))
                    s = slice(2 * n, 2 * n + 2)
                    act.activation(uhi[:, s, :], work[:, s, :], ACT.Copy).then_inc(mgh_done, 1)

                sigmoids(0)
                for n in range(4):
                    chunks(c + 3 * n, 1)
                    if n > 0:
                        merged_high(n - 1)
                    chunks(c + (3 * n + 1), 1)
                    if n < 3:
                        sigmoids(n + 1)
                    else:
                        act.preload_act_table(ACT.Sqrt)
                    chunks(c + (3 * n + 2), 1)
                merged_high(3)
                c, g = c + 12, g + 12
                chunks(c, KT - 2)
                for b in range(4):
                    act.wait_ge(w_used, (c + (2 * b + 1)).count(1 + SLOTS))
                    square_pair(b)
                c = c + KT
                chunks(c + (-2), 2)
                take_root(l * 6 + 3, DM)
                act.wait_ge(lp_ready, l * 2 + 2)
                scaled_high(l * 3 + 2, gain(PRE2))
                squares_of_stream(l * 3 + 2)
                ffn(c, g, l * 2 + 1, l * 6 + 4)
                for b in range(4):
                    result_pair(b, c + 2 * FT, l * 2 + 1)
                    square_pair(b)
                chunks(c + (FFN_C - 2), 2)
                take_root(l * 6 + 5, DM)

            V2, M2 = 3 * LAYERS, 3 * LAYERS
            pgain = lambda at: par[:, at:at + KT]
            scaled_high(V2, pgain(AMIX))
            squares_of_stream(V2)
            for t in range(KT):
                ci = c_conv + 3 * t
                chunks(ci, 1)
                if t == 0:
                    take_root(n_conv[0], DM)
                chunks(ci + 1, 1)
                act.wait_ge(group_done, g_conv + 3 * t + 2 + 2)
                act.activation(sg[t % 2], hf[t % 2], ACT.Copy, scale=par[:, ACONV + 2 * KT + t:ACONV + 2 * KT + t + 1])\
                   .then_inc(tap_done, 1)
                chunks(ci + 2, 1)
                act.wait_ge(y_done, t * 3 + 3)
                act.activation(hhi[:, t, :], hf[t % 2], ACT.Copy).then_inc(hhi_done, 1)
            beside_stream(V2 + 1, pgain(FFNN), c_aout)
            chunks(c_aout + (KT - 2), 2)
            conv_ffn(c_ffa, g_ffa, 0, 0, n_ffa[0])
            scaled_high(V2 + 2, pgain(BMIX), hhi)
            squares_of_stream(V2 + 2)
            act.preload_act_table(ACT.Sqrt)
            scaled_high(V2 + 2, pgain(KVIN), pairs=(0, 1))
            take_root(n_h2[0], DM)
            scaled_high(V2 + 2, pgain(KVIN), pairs=(2, 3))
            chunks(c_ffa + (FFN_C - 1), 1)
            chunks(c_dq, 4)
            act.wait_ge(group_done, g_dq + 4 + 2)
            for b in range(2):
                act.activation(sq[:, 2 * b:2 * b + 2, :], qlat[:, 2 * b:2 * b + 2, :], ACT.Square).then_inc(sq_done, 1)
            chunks(c_kv, 1)
            take_root(n_q[0], QL)
            chunks(c_kv + 1, 1)
            act.wait_ge(group_done, g_kv + 2 + 2)
            act.activation(sq[:, 4:6, :], ckv, ACT.Square).then_inc(sq_done, 1)
            act.wait_ge(lat_done, 1)
            act.activation(hhi[:, QLAT, :], work[:, 2:6, :], ACT.Copy).then_inc(lat_hi, 1)
            chunks(c_kv + 2, 1)
            take_root(n_kv[0], KVL)
            chunks(c_uqr, 1)
            act.wait_ge(lat_done, 2)
            act.activation(hhi[:, KVLAT, :], work[:, 0:2, :], ACT.Copy).then_inc(lat_hi, 1)
            chunks(c_uqr + 1, 3)
            act.preload_act_table(ACT.Exp)

            def mla_exp(h):
                act.wait_ge(ls_max, 2 * h + 2)
                for q, (a, b) in enumerate(((0, P), (P, CAUSAL))):
                    act.activation(ls(h)[:, a:b], ls(h)[:, a:b], ACT.Exp, bias=lmax(h)[:, q:q + 1],
                                   accum_out=lsum(h)[:, q:q + 1]).then_inc(ls_exp, 1)

            def mla_pT(h):
                act.wait_ge(ls_tp, h + 1)
                act.activation(lpT(h), bank[4 + h % 2][:, 0:CAUSAL], ACT.Copy).then_inc(ls_pt, 1)

            def mla_high(h):
                act.wait_ge(la_full, h + 1)
                act.activation(hhi[:, h, :], bank[6 + h % 2][:, 0:TOK], ACT.Copy).then_inc(la_hi, 1)

            def heads(step, of):
                for h in (2 * step, 2 * step + 1):
                    of(h)

            for p in range(7):
                if p < 4:
                    chunks(c_pairs + 2 * p, 1)
                if p >= 3:
                    heads(p - 3, mla_high)
                if 1 <= p <= 4:
                    heads(p - 1, mla_exp)
                if p < 4:
                    chunks(c_pairs + (2 * p + 1), 1)
                if 2 <= p <= 5:
                    heads(p - 2, mla_pT)
            act.preload_act_table(ACT.Sqrt)
            beside_stream(V2 + 3, pgain(FFNN + KT), c_o)
            chunks(c_o + (KT - 2), 2)
            conv_ffn(c_ffb, g_ffb, 1, 1, n_ffb[0])
            for b in range(4):
                act.wait_ge(h_ready, (V2 + 4) * 4 + (b + 1))
                for k in (2 * b, 2 * b + 1):
                    ins = act.activation(work[:, k, :], H[:, k, :], ACT.Copy, scale=par[:, FINAL + k:FINAL + k + 1])
                ins.then_inc(un_done, 1)
            act.preload_act_table(ACT.Sqrt)
            act.wait_ge(ss_full, n_fin[0] + 1)
            act.activation(mmax[:, :], bank[2][:, 0:2 * TT:2], ACT.Sqrt, scale=1.0 / DM, bias=EPS).then_inc(root_done, 1)
            for t in range(TT):
                act.wait_ge(rstd_done, n_fin[0] + 1)
                act.wait_ge(y_tp, 2 * t + 1)
                act.activation(gates[:, 4 * t:4 * t + 2, :], pair_bank(4 + 2 * t), ACT.Copy, scale=mrec[:, t:t + 1])\
                   .then_inc(y_copied, 1)

        @block.vector
        def _(dve):
            def lo(c):
                if isinstance(c.rounds, int) and c.count() >= CHUNKS:
                    return
                dve.wait_ge(hi_ready, c.count(1))
                dve.tensor_tensor(wlo[c.slot][:, :], raw[c.slot][:, :], whi[c.slot][:, :].bitcast(F32), ALU.subtract)\
                   .then_inc(lo_ready, 1)

            def chunks(c, n):
                for j in range(n):
                    lo(c + (AHEAD + j))

            def done(c):
                dve.wait_ge(w_used, c.count(1 + SLOTS))

            def take_rstd(n, dst=None):
                dst = rstd[:, :] if dst is None else dst
                dve.wait_ge(root_done, n + 1)
                dve.reciprocal(dst, root[:, :]).then_inc(rstd_done, 1)
                dve.wait_ge(rstd_done, n + 1)

            def sum_squares(s_at, n):
                for b in range(1, 4):
                    dve.wait_ge(sq_done, s_at + (b + 1))
                    if b > 1:
                        dve.wait_ge(sq_summed, n * 3 + (b - 1))
                    dve.tensor_tensor(sq[:, 0:2, :], sq[:, 0:2, :], sq[:, 2 * b:2 * b + 2, :], ALU.add).then_inc(sq_summed, 1)

            def scale_result(gain, pairs):
                for b in pairs:
                    for k in (2 * b, 2 * b + 1):
                        ins = dve.scalar_tensor_tensor(work[:, k, :], bank[4 + b][:, (k % 2) * TOK:(k % 2 + 1) * TOK],
                                                       gain[:, k:k + 1], rstd[:, :], ALU.mult, ALU.mult)
                    ins.then_inc(scaled, 1)

            def scaled_low(m, gain, dst=ulo, src=uhi):
                for b in range(4):
                    low_pair(b, m, gain, dst, src)

            def low_pair(b, m, gain, dst, src):
                dve.wait_ge(uhi_done, m * 4 + (b + 1))
                for k in (2 * b, 2 * b + 1):
                    ins = dve.scalar_tensor_tensor(dst[:, k, :], H[:, k, :], gain[:, k:k + 1],
                                                   src[:, k, :].bitcast(F32), ALU.mult, ALU.subtract)
                ins.then_inc(ulo_done, 1)

            def add_result(complete, low=None):
                for b in range(4):
                    complete(b)
                    s = slice(2 * b, 2 * b + 2)
                    dve.tensor_tensor(H[:, s, :], pair_bank(4 + b), H[:, s, :], ALU.add).then_inc(h_ready, 1)
                    if low and b > 0:
                        low(b - 1)
                if low:
                    low(3)

            def beside_projection(c):
                def complete(b):
                    if b < 3:
                        chunks(c + 2 * b, 2)
                    done(c + (2 * b + 1))
                return complete

            def of_down(c, use):
                def complete(b):
                    if b < 3:
                        dve.wait_ge(acc_full, use * DOWN_PAIRS + (DOWN_PAIRS - 3 + b + 1))
                    else:
                        done(c + (FT - 1))
                return complete

            def tile(t, n):
                return t[:, bass.ds(n, 1), :].rearrange("p a n -> p (a n)")

            def down(c, leave=0):
                turns = (FT - 2) // 4
                last = leave or isinstance(c.rounds, int) and c.count(FT) > CHUNKS
                with dve.Fori(0, turns - bool(last)) as i:
                    chunks(c.later(i), 4)
                if last:
                    chunks(c + 4 * (turns - 1), 4 - leave)

            def ffn(c, g, use, n):
                def tiles(i, first=False):
                    ci = c.later(i)
                    f0 = i * 2 + use * FT

                    def scale(j):
                        done(ci + (2 * j + 1))
                        dve.tensor_tensor(zz[j], pair_bank((g.k + j) % 2), rstd_pair, ALU.mult).then_inc(group_done, 1)

                    def hidden(j):
                        dve.wait_ge(silu_done, f0 + (j + 1))
                        dve.tensor_tensor(hf[j], zz[j][:, 1, :], sg[j], ALU.mult).then_inc(hid_done, 1)

                    def low(j):
                        dve.wait_ge(hhi_done, f0 + (j + 1))
                        dve.tensor_tensor(tile(hlo, i * 2 + j), hf[j], tile(hhi, i * 2 + j).bitcast(F32), ALU.subtract)\
                           .then_inc(hlo_done, 1)

                    chunks(ci, 1)
                    if first:
                        take_rstd(n)
                    scale(0)
                    hidden(0)
                    chunks(ci + 1, 1)
                    low(0)
                    chunks(ci + 2, 1)
                    scale(1)
                    hidden(1)
                    chunks(ci + 3, 1)
                    low(1)

                tiles(0, first=True)
                with dve.Fori(1, FT // 2) as i:
                    tiles(i)
                down(c + 2 * FT)

            def conv_ffn(c, g, use, layer, n):
                taps = FCONV + layer * 6 * FT
                before_it = LAYERS * 2 * FT

                def tiles(i, first=False):
                    ci = c.later(i)
                    f0 = i * 2 + use * FT

                    def scale(j):
                        done(ci + (2 * j + 1))
                        dve.tensor_tensor(zz[j], pair_bank((g + j) % 2), rstd_pair, ALU.mult).then_inc(group_done, 1)

                    def older_taps(j):
                        y = conv_y[j]
                        dve.wait_ge(tap_done, (f0 + j) * 2 + (2 + KT))
                        for back in (1, 2):
                            for s in range(2):
                                a = s * TOK
                                if back == 2:
                                    dve.wait_ge(conv_done, (f0 + j) * 4 + (s + 1))
                                dve.scalar_tensor_tensor(
                                    y[:, a + back:a + TOK], zz[j][:, s, 0:TOK - back],
                                    par[:, bass.ds(i * 2 + (taps + (2 - back) * 2 * FT + s * FT + j), 1)],
                                    y[:, a + back:a + TOK], ALU.mult, ALU.add).then_inc(conv_done, 1)

                    def hidden(j):
                        dve.wait_ge(silu_done, f0 + (j + before_it + 1))
                        dve.wait_ge(conv_done, (f0 + j) * 4 + 4)
                        dve.wait_ge(hlo_done, f0 + (j + before_it + KT - 1))
                        dve.tensor_tensor(hf[j], conv_y[j][:, TOK:2 * TOK], sg[j], ALU.mult).then_inc(hid_done, 1)

                    if first:
                        take_rstd(n)
                    for j in range(2):
                        scale(j)
                        chunks(ci + (2 * j + 1), 1)
                        older_taps(j)
                        chunks(ci + (2 * j + 2), 1)
                        hidden(j)

                chunks(c, 1)
                tiles(0, first=True)
                with dve.Fori(1, FT // 2) as i:
                    tiles(i)
                down(c + (2 * FT + 1), leave=1 if use == 0 else 0)

            def head_low(count, src, hi_part, lo_part):
                dve.wait_ge(ohi_done, count)
                dve.tensor_tensor(lo_part, src, hi_part.bitcast(F32), ALU.subtract).then_inc(olo_done, 1)

            dve.sem_inc(lo_ready, SLOTS)
            dve.sem_inc(group_done, 2)
            dve.sem_inc(f_split, 2)
            dve.sem_inc(olo_done, 1)
            for b in range(4):
                dve.wait_ge(x_tp, b + 1)
                dve.tensor_copy(H[:, 2 * b:2 * b + 2, :], pair_bank(4 + b)).then_inc(h_ready, 1)
            dve.wait_ge(par_tp, 1)
            dve.tensor_copy(par[:, :], bank[3][:, :]).then_inc(par_ready, 1)
            dve.wait_ge(par_ready, 1)
            for at in (POST1, POST2):
                v = par[:, at * LAYERS:(at + KT) * LAYERS]
                dve.tensor_scalar(v, v, 0.5, None, ALU.mult).then_inc(par_ready, 1)
            dve.wait_ge(m_root, 1)
            dve.reciprocal(mrec[:, :], mmax[:, :]).then_inc(m_rstd, 1)
            dve.wait_ge(m_rstd, 1)
            for t in range(TT):
                dve.tensor_scalar(mtok[:, t, :], mtok[:, t, :], mrec[:, t:t + 1], None, ALU.mult).then_inc(m_scaled, 1)
            lo(Chunk(0, 0))
            dve.wait_ge(mg_tp, 1)
            dve.tensor_copy(mgain[:, :], bank[2][:, 0:KT]).then_inc(mg_ready, 1)
            dve.wait_ge(mg_ready, 1)
            for k in range(KT):
                dve.wait_ge(m_tp, k // 2 + 1)
                dve.tensor_scalar(gates[:, 16 + k, :], bank[4 + k // 2][:, (k % 2) * TOK:(k % 2 + 1) * TOK],
                                  mgain[:, k:k + 1], None, ALU.mult).then_inc(m_gain, 1)
            for n in range(1, SLOTS - 1):
                lo(Chunk(0, n))

            with dve.Fori(0, LAYERS) as l:
                c = Chunk(l * (LAYER_C // SLOTS), 0)
                g = Group(l * LAYER_G, 0)
                gain = lambda at: lp[:, at:at + KT]
                dve.wait_ge(par_ready, 3)
                scaled_low(l * 3, par[:, bass.ds(l * KT + PRE1 * LAYERS, KT)])
                by_layer = par[:, 0:BGATE * LAYERS].rearrange("p (n l k) -> p n l k", l=LAYERS, k=KT)
                dve.tensor_copy(lp[:, 0:BGATE].rearrange("p (n k) -> p n k", k=KT).unsqueeze(2),
                                by_layer[:, :, bass.ds(l, 1), :]).then_inc(lp_ready, 1)
                dve.tensor_copy(lp[:, BGATE:LP], par[:, bass.ds(l * (3 * KT) + BGATE * LAYERS, 3 * KT)]).then_inc(lp_ready, 1)
                dve.wait_ge(lp_ready, l * 2 + 2)
                sum_squares(l * 24, l * 6)
                chunks(c + (-1), 1)
                ffn(c, g, l * 2, l * 6)
                c, g = c + FFN_C, g + FFN_G
                sum_squares(l * 24 + 4, l * 6 + 1)
                chunks(c + (-2), 2)

                def take_mem(n):
                    done(c + (n if n < 4 else n + 2))
                    src = bank[n % 2][:, 0:TOK]
                    if n < 4:
                        dve.tensor_copy(kmem[:, n, :], src).then_inc(group_done, 1)
                    else:
                        dve.tensor_scalar(qmem[:, n - 6, :], src, MEM_SCALE, None, ALU.mult).then_inc(group_done, 1)

                take_mem(0)
                take_rstd(l * 6 + 1)
                scale_result(gain(POST1), (0, 1))
                take_mem(1)
                scale_result(gain(POST1), (2, 3))
                chunks(c, 1)
                take_mem(2)
                chunks(c + 1, 1)
                take_mem(3)
                chunks(c + 2, 2)

                def take_values(e):
                    done(c + (5 + 2 * e))
                    dve.tensor_copy(vmem[:, :, 2 * e:2 * e + 2, :],
                                    bank[e][:, :].rearrange("p (t h d) -> p t h d", t=TT, h=2)).then_inc(group_done, 1)

                take_values(0)
                chunks(c + 4, 2)
                take_rstd(l * 6 + 2)
                for b in range(4):
                    dve.wait_ge(h_ready, l * 12 + (b + 5))
                    for k in (2 * b, 2 * b + 1):
                        ins = dve.scalar_tensor_tensor(work[:, k, :], H[:, k, :], lp[:, PREM + k:PREM + k + 1], rstd[:, :],
                                                       ALU.mult, ALU.mult)
                    ins.then_inc(un_done, 1)
                take_values(1)
                chunks(c + 6, 2)
                dve.wait_ge(f_split, l * 2 + 3)
                dve.tensor_tensor(wflo[:, :, :], wfor[:, :, :], wfhi[:, :, :].bitcast(F32), ALU.subtract).then_inc(f_split, 1)
                take_mem(6)
                chunks(c + 8, 1)
                dve.wait_ge(f_full, l + 1)
                dve.wait_ge(bf_loaded, 16)
                dve.tensor_tensor(flog[:, :, :], bank[3][:, 0:16].rearrange("p (t h) -> p t h", t=TT),
                                  bfor[:, bass.ds(l, 1), :].to_broadcast([P, TT, 8]), ALU.add).then_inc(f_biased, 1)
                dve.wait_ge(f_log, l * 3 + 3)
                dve.scalar_tensor_tensor(flog[:, :, :], flog[:, :, :], 0.0, fabs[:, :, :], ALU.min, ALU.subtract)\
                   .then_inc(f_ready, 1)
                for n in (7, 8):
                    take_mem(n)
                    chunks(c + (n + 2), 1)
                dve.wait_ge(c_full, l + 1)
                dve.tensor_copy(ctok[:, :, :], bank[3][:, 32:48].rearrange("p (t h) -> p t h", t=TT)).then_inc(c_ready, 1)
                for h in range(2):
                    dve.tensor_copy(crow[c_rows[h], :], bank[3][0:8, 64:64 + TOK]).then_inc(c_ready, 1)
                take_mem(9)
                chunks(c + 11, 1)
                with dve.Fori(0, NPAIR) as p:
                    I = l * NPAIR + p
                    cp = (c + 12).later(p * 3)
                    o = lambda t, branch: tile(t, p + 4 * branch)

                    def gate(n):
                        done(cp + (6 + n))
                        dve.tensor_scalar(tile(gates, p * 6 + n),
                                          bank[n % 2][:, 0:TOK], lp[:, bass.ds(p * 6 + (BGATE + n), 1)], None, ALU.add)\
                           .then_inc(group_done, 1)

                    dve.tensor_copy(qm1, tile(qmem, p)).then_inc(mem_staged, 1)
                    dve.tensor_copy(vm1[:, :, :], vmem[:, :, bass.ds(p, 1), :].rearrange("p t a d -> p t (a d)"))\
                       .then_inc(mem_staged, 1)
                    dve.wait_ge(c_ready, l * 3 + 3)
                    dve.wait_ge(fx_rows, 3)
                    for h in range(2):
                        r = c_rows[h]
                        dve.tensor_scalar(kx[h][r, :], crow[r, :], cst[r, bass.ds(p * 2 + (C_NEG8 + h), 1)], None,
                                          ALU.mult).then_inc(c_pair, 1)
                    done(cp)
                    dve.tensor_scalar(qs, bank[0][:, 0:TOK], SB_SCALE, None, ALU.mult).then_inc(group_done, 1)
                    dve.wait_ge(mem_full, I + 1)
                    dve.tensor_reduce(mmax[:, :], pair_bank(6), AX_X, ALU.max, negate=True).then_inc(mem_max, 1)
                    chunks(cp, 1)
                    done(cp + 1)
                    dve.tensor_copy(ks, bank[1][:, 0:TOK]).then_inc(group_done, 1)
                    dve.wait_ge(mem_exp, I * 2 + 2)
                    dve.reciprocal(mrec[:, :], msum[:, :]).then_inc(mem_rec, 1)
                    dve.wait_ge(mem_rec, I + 1)
                    for q in range(TT):
                        ins = dve.tensor_scalar(mem_p[:, q * TOK:(q + 1) * TOK], mem_p[:, q * TOK:(q + 1) * TOK],
                                                mrec[:, q:q + 1], None, ALU.mult)
                    ins.then_inc(mem_norm, 1)
                    chunks(cp + 1, 1)
                    done(cp + 2)
                    for h, f in enumerate(features):
                        ins = dve.tensor_scalar(qx[h][f, :], bank[0][f, 0:TOK], SB_SCALE, None, ALU.mult)
                    ins.then_inc(group_done, 1)
                    chunks(cp + 2, 1)
                    done(cp + 3)
                    for h, f in enumerate(features):
                        ins = dve.tensor_copy(kx[h][f, :], bank[1][f, 0:TOK])
                    ins.then_inc(group_done, 1)
                    chunks(cp + 3, 2)
                    head_low(I * 3 + 1, bank[6][:, 0:TOK], o(hhi, 2), o(hlo, 2))
                    done(cp + 5)
                    dve.tensor_copy(vpair, pair_bank(5)).then_inc(v_taken, 1)
                    dve.wait_ge(sb_act, I * 4 + 4)
                    for h in range(2):
                        ins = dve.scalar_tensor_tensor(sb_sp[:, h, :], bank[2 + h][:, 0:CAUSAL], 0.0, sb_e[:, h, :],
                                                       ALU.max, ALU.add)
                    ins.then_inc(sb_dve, 1)
                    dve.wait_ge(sb_dve, I * 2 + 1)
                    for h in range(2):
                        ins = dve.tensor_tensor(sb_w[:, h, :], bank[2 + h][:, 0:CAUSAL], sb_sp[:, h, :], ALU.subtract)
                    ins.then_inc(sb_dve, 1)
                    chunks(cp + 5, 1)
                    gate(0)
                    chunks(cp + 6, 1)
                    dve.wait_ge(fxz_full, I + 1)
                    for h in range(2):
                        for q, (a, b) in enumerate(((0, P), (P, CAUSAL))):
                            dve.scalar_tensor_tensor(fx_s[:, h, a:b], bank[4 + h][:, a:b],
                                                     ctok[:, q, bass.ds(p * 2 + h, 1)], hide[:, a:b],
                                                     ALU.add, ALU.add).then_inc(fx_add, 1)
                    dve.wait_ge(fx_add, I * 4 + 4)
                    for q, (a, b) in enumerate(((0, P), (P, CAUSAL))):
                        dve.tensor_reduce(fmax[:, 2 * q:2 * q + 2], fx_s[:, :, a:b], AX_X, ALU.max, negate=True)\
                           .then_inc(fx_max, 1)
                    gate(1)
                    chunks(cp + 7, 1)
                    dve.wait_ge(sb_cum, I + 1)
                    for cols, sums in ((slice(0, TOK), pair_bank(6)), (slice(TOK, CAUSAL), last_block)):
                        dve.tensor_tensor(sb_w[:, :, cols], sb_w[:, :, cols], sums, ALU.subtract).then_inc(sb_lw, 1)
                    dve.wait_ge(fx_exp, I * 4 + 4)
                    dve.reciprocal(frec[:, 0:4], fsum[:, 0:4]).then_inc(fx_rec, 1)
                    dve.wait_ge(fx_rec, I + 1)
                    for h in range(2):
                        for q, (a, b) in enumerate(((0, P), (P, CAUSAL))):
                            n = 2 * q + h
                            ins = dve.tensor_scalar(fx_s[:, h, a:b], fx_s[:, h, a:b], frec[:, n:n + 1], None, ALU.mult)
                    ins.then_inc(fx_norm, 1)
                    gate(2)
                    chunks(cp + 8, 1)
                    gate(3)
                    chunks(cp + 9, 1)
                    gate(4)
                    chunks(cp + 10, 1)
                    head_low(I * 3 + 2, bank[4][:, 0:TOK], o(hhi, 0), o(hlo, 0))
                    gate(5)
                    chunks(cp + 11, 1)
                    head_low(I * 3 + 3, bank[5][:, 0:TOK], o(hhi, 1), o(hlo, 1))
                c, g = c + (12 + 12 * NPAIR), g + (MEM_G + PAIR_G * NPAIR)
                for n in range(4):
                    s = slice(2 * n, 2 * n + 2)
                    for b, br in enumerate(BRANCHES):
                        dve.wait_ge(sig_done, l * 12 + (3 * n + b + 1))
                        done(c + (3 * n + b))
                        dst = work[:, s, :] if b == 0 else sq[:, 2 * b:2 * b + 2, :]
                        dve.tensor_tensor(dst, pair_bank((3 * n + b) % 2), gates[:, 8 * br + 2 * n:8 * br + 2 * n + 2, :],
                                          ALU.mult).then_inc(group_done, 1)
                        if b == 0:
                            chunks(c + 3 * n, 1)
                        if b > 0:
                            dve.wait_ge(group_done, g.count(3 * n + b + 3))
                            if b == 2:
                                dve.wait_ge(merged, l * 8 + (2 * n + 1))
                            dve.tensor_tensor(work[:, s, :], work[:, s, :], dst, ALU.add).then_inc(merged, 1)
                            chunks(c + (3 * n + b), 1)
                c, g = c + 12, g + 12
                chunks(c, KT - 2)
                c = c + KT
                sum_squares(l * 24 + 12, l * 6 + 3)
                chunks(c + (-2), 1)
                take_rstd(l * 6 + 3)
                scale_result(gain(POSTM), range(4))
                scaled_low(l * 3 + 2, gain(PRE2))
                sum_squares(l * 24 + 16, l * 6 + 4)
                chunks(c + (-1), 1)
                ffn(c, g, l * 2 + 1, l * 6 + 4)
                sum_squares(l * 24 + 20, l * 6 + 5)
                chunks(c + (FFN_C - 2), 1)
                take_rstd(l * 6 + 5)
                scale_result(gain(POST2), range(4))
                dve.wait_ge(scaled, l * 12 + 12)

            HID = LAYERS * 2 * FT
            pgain = lambda at: par[:, at:at + KT]
            M2 = 3 * LAYERS
            scaled_low(M2, pgain(AMIX))
            sum_squares(n_conv[1], n_conv[0])
            chunks(c_conv + (-1), 1)
            for t in range(KT):
                ci = c_conv + 3 * t
                G = g_conv + 3 * t + 2
                f, b0 = t % 2, 3 * t
                if t == 0:
                    take_rstd(n_conv[0])
                    dve.tensor_tensor(rstd_sq, rstd[:, :], rstd[:, :], ALU.mult).then_inc(rstd_squared, 1)
                    dve.wait_ge(rstd_squared, 1)
                done(ci)
                dve.tensor_tensor(part(4), bank[b0 % 2][:, 0:TOK], rstd_sq, ALU.mult).then_inc(group_done, 1)
                chunks(ci, 1)
                done(ci + 1)
                dve.wait_ge(group_done, G + 1)
                dve.tensor_tensor(hf[f], bank[(b0 + 1) % 2][:, 0:TOK], part(4), ALU.mult).then_inc(group_done, 1)
                chunks(ci + 1, 1)
                dve.wait_ge(tap_done, t + 1)
                for back in (1, 2):
                    if back == 2:
                        dve.wait_ge(y_done, t * 3 + 1)
                    at = ACONV + (2 - back) * KT + t
                    dve.scalar_tensor_tensor(sg[f][:, back:TOK], hf[f][:, 0:TOK - back], par[:, at:at + 1],
                                             sg[f][:, back:TOK], ALU.mult, ALU.add).then_inc(y_done, 1)
                done(ci + 2)
                dve.wait_ge(y_done, t * 3 + 2)
                dve.tensor_tensor(sg[f], bank[(b0 + 2) % 2][:, 0:TOK], sg[f], ALU.mult).then_inc(group_done, 1)
                dve.wait_ge(group_done, G + 3)
                dve.tensor_tensor(hf[f], sg[f], rstd[:, :], ALU.mult).then_inc(y_done, 1)
                chunks(ci + 2, 1)
                dve.wait_ge(hhi_done, t + (HID + 1))
                dve.tensor_tensor(hlo[:, t, :], hf[f], hhi[:, t, :].bitcast(F32), ALU.subtract).then_inc(hlo_done, 1)
            add_result(beside_projection(c_aout), lambda b: low_pair(b, M2 + 1, pgain(FFNN), ulo, uhi))
            chunks(c_aout + (KT - 2), 2)
            conv_ffn(c_ffa, g_ffa, 0, 0, n_ffa[0])
            add_result(of_down(c_ffa + 2 * FT, 2 * LAYERS), lambda b: low_pair(b, M2 + 2, pgain(BMIX), hlo, hhi))
            sum_squares(n_h2[1], n_h2[0])
            chunks(c_ffa + (FFN_C - 2), 1)
            kv_low = lambda b: low_pair(b, M2 + 3, pgain(KVIN), ulo, uhi)
            kv_low(0)
            kv_low(1)
            take_rstd(n_h2[0])

            for n in range(4):
                done(c_dq + n)
                dve.tensor_tensor(qlat[:, n, :], bank[(g_dq + n) % 2][:, 0:TOK], rstd[:, :], ALU.mult).then_inc(group_done, 1)
                if n == 0:
                    kv_low(2)
                    kv_low(3)
                    chunks(c_ffa + (FFN_C - 1), 1)
                chunks(c_dq + n, 1)

            def take_kv(n, dst):
                done(c_kv + n)
                dve.tensor_tensor(dst, bank[(g_kv + n) % 2][:, 0:TOK], rstd[:, :], ALU.mult).then_inc(group_done, 1)

            def latent(n, first, count, src, at, factor):
                for k in range(count):
                    ins = dve.scalar_tensor_tensor(work[:, first + k, :], src[:, k, :], par[:, at + k:at + k + 1], factor,
                                                   ALU.mult, ALU.mult)
                ins.then_inc(lat_done, 1)

            def latent_low(count, at, first):
                dve.wait_ge(lat_hi, count)
                n = at.stop - at.start
                dve.tensor_tensor(hlo[:, at, :], work[:, first:first + n, :], hhi[:, at, :].bitcast(F32), ALU.subtract)\
                   .then_inc(lat_lo, 1)

            def sine_part(n):
                dve.wait_ge(rp_swap, n + 1)
                if n >= 2:
                    dve.wait_ge(rp_done, n - 1)
                dve.tensor_tensor(part(2 + n % 2), bank[3][:, 0:TOK], sine, ALU.mult).then_inc(rp_sin, 1)

            def take_rotary(p):
                done(c_uqr + p)
                if p >= 2:
                    dve.wait_ge(rp_cos, p)
                dve.tensor_scalar(part(p % 2), bank[(g_uqr + p) % 2][:, 0:TOK], MLA_SCALE, None, ALU.mult).then_inc(group_done, 1)

            take_kv(0, ckv[:, 0, :])
            chunks(c_kv, 1)
            take_rstd(n_q[0], rstd_q)
            latent(0, 2, 4, qlat, BQ, rstd_q)
            take_kv(1, ckv[:, 1, :])
            chunks(c_kv + 1, 1)
            latent_low(1, QLAT, 2)
            take_kv(2, kr_raw)
            chunks(c_kv + 2, 1)
            sine_part(0)
            dve.wait_ge(group_done, g_kv + 3 + 2)
            take_rstd(n_kv[0])
            take_rotary(0)
            latent(1, 0, 2, ckv, KVN, rstd[:, :])
            chunks(c_uqr, 1)
            latent_low(2, KVLAT, 0)
            sine_part(1)
            for p in range(1, 4):
                take_rotary(p)
                chunks(c_uqr + p, 1)
                sine_part(p + 1)

            def mla_max(h):
                dve.wait_ge(ls_full, h + 1)
                dve.tensor_tensor(ls(h), bank[2 + h % 2][:, 0:CAUSAL], hide, ALU.add).then_inc(ls_add, 1)
                dve.wait_ge(ls_add, h + 1)
                for q, (a, b) in enumerate(((0, P), (P, CAUSAL))):
                    dve.tensor_reduce(lmax(h)[:, q:q + 1], ls(h)[:, a:b], AX_X, ALU.max, negate=True).then_inc(ls_max, 1)

            def mla_norm(h):
                dve.wait_ge(ls_exp, 2 * h + 2)
                dve.reciprocal(lrec(h), lsum(h)).then_inc(ls_rec, 1)
                dve.wait_ge(ls_rec, h + 1)
                for q, (a, b) in enumerate(((0, P), (P, CAUSAL))):
                    ins = dve.tensor_scalar(ls(h)[:, a:b], ls(h)[:, a:b], lrec(h)[:, q:q + 1], None, ALU.mult)
                ins.then_inc(ls_norm, 1)

            def mla_low(h):
                dve.wait_ge(la_hi, h + 1)
                dve.tensor_tensor(hlo[:, h, :], bank[6 + h % 2][:, 0:TOK], hhi[:, h, :].bitcast(F32), ALU.subtract)\
                   .then_inc(la_lo, 1)

            def heads(step, of):
                for h in (2 * step, 2 * step + 1):
                    of(h)

            for p in range(7):
                G = g_pairs + 3 * p
                if p < 4:
                    done(c_pairs + 2 * p)
                    dve.tensor_copy(kn[:, 2 * p:2 * p + 2, :], pair_bank(G % 2)).then_inc(group_done, 1)
                    dve.tensor_copy(vn[:, :, 2 * p:2 * p + 2, :],
                                    bank[(G + 1) % 2][:, :].rearrange("p (t h d) -> p t h d", t=TT, h=2)).then_inc(group_done, 1)
                    chunks(c_pairs + 2 * p, 1)
                if 1 <= p <= 4:
                    heads(p - 1, mla_max)
                if p >= 3:
                    heads(p - 3, mla_low)
                if p < 4:
                    done(c_pairs + (2 * p + 1))
                    dve.tensor_scalar(qn[:, 2 * p:2 * p + 2, :], pair_bank((G + 2) % 2), MLA_SCALE, None, ALU.mult)\
                       .then_inc(group_done, 1)
                    chunks(c_pairs + (2 * p + 1), 1)
                if 1 <= p <= 4:
                    heads(p - 1, mla_norm)
            add_result(beside_projection(c_o), lambda b: low_pair(b, M2 + 4, pgain(FFNN + KT), ulo, uhi))
            chunks(c_o + (KT - 2), 2)
            conv_ffn(c_ffb, g_ffb, 1, 1, n_ffb[0])
            add_result(of_down(c_ffb + 2 * FT, 2 * LAYERS + 1))
            for b in range(4):
                s = slice(2 * b, 2 * b + 2)
                dve.wait_ge(h_ready, (3 * LAYERS + 4) * 4 + (b + 1))
                dve.tensor_tensor(sq[:, s, :], H[:, s, :], H[:, s, :], ALU.mult).then_inc(sq_done, 1)
            dve.wait_ge(root_done, n_fin[0] + 1)
            dve.reciprocal(mrec[:, :], mmax[:, :]).then_inc(rstd_done, 1)
            dve.wait_ge(rstd_done, n_fin[0] + 1)
            for t in range(TT):
                dve.wait_ge(y_tp, 2 * t + 2)
                dve.tensor_scalar(gates[:, 4 * t + 2:4 * t + 4, :], pair_bank(5 + 2 * t), mrec[:, t:t + 1], None, ALU.mult)\
                   .then_inc(y_scaled, 1)

        @block.tensor
        def _(pe):
            def start_chunk(c):
                pe.wait_ge(lo_ready, c.count(1 + SLOTS))

            def free_bank(g):
                pe.wait_ge(group_done, g.count(1))
                return bank[g.k % 2]

            def mm3(dst, w_hi, w_lo, x_hi, x_lo, start, stop, **kw):
                pe.matmul(dst, w_hi, x_hi, start=start, stop=False, **kw)
                pe.matmul(dst, w_hi, x_lo, start=False, stop=False, **kw)
                return pe.matmul(dst, w_lo, x_hi, start=False, stop=stop, **kw)

            def project(dst, c, kts, xh, xl, width=P, at=0, ready=None):
                for k in range(kts):
                    if ready:
                        ready(k)
                    s = slice(k * width + at, k * width + at + P)
                    ins = mm3(dst, whi[c.slot][:, s], wlo[c.slot][:, s], xh[:, k, :], xl[:, k, :], k == 0, k == kts - 1)
                return ins

            def project_two(dsts, c, xh, xl, ready):
                for j in range(2):
                    start_chunk(c + j)
                for k in range(KT):
                    ready(k)
                    s = slice(k * P, (k + 1) * P)
                    for j in range(2):
                        slot = (c + j).slot
                        ins = mm3(dsts[j], whi[slot][:, s], wlo[slot][:, s], xh[:, k, :], xl[:, k, :],
                                  k == 0 and j == 0, k == KT - 1, skip_group_check=True)
                        if k == KT - 1:
                            ins.then_inc(w_used, 1)

            def project_tokens(dst, c, kts, xh, xl, w, first=True, last=True):
                for t in range(TT):
                    rows = slice(t * P, (t + 1) * P)
                    for k in range(kts):
                        start, stop = first and t == 0 and k == 0, last and k == kts - 1
                        pe.matmul(dst(t), xh[:, k, rows], w(whi[c.slot], k), start=start, stop=False, skip_group_check=True)
                        pe.matmul(dst(t), xl[:, k, rows], w(whi[c.slot], k), start=False, stop=False, skip_group_check=True)
                        ins = pe.matmul(dst(t), xh[:, k, rows], w(wlo[c.slot], k), start=False, stop=stop, skip_group_check=True)
                return ins

            half_rows = lambda slot, k: slot[:, k * 2 * P:(k + 1) * 2 * P]

            def sum_squares(n):
                pe.wait_ge(sq_summed, n * 3 + 3)
                sums(2, 0)

            def sum_latent(s_at, tiles, first=0):
                pe.wait_ge(sq_done, s_at + tiles // 2)
                sums(tiles, first)

            def sums(tiles, first):
                for k in range(tiles):
                    ins = pe.matmul(bank[2][:, 0:TOK], ones, sq[:, first + k, :], start=(k == 0), stop=(k == tiles - 1))
                ins.then_inc(ss_full, 1)

            def stream_pair(m):
                def ready(k):
                    if k % 2 == 0:
                        pe.wait_ge(ulo_done, m * 4 + (k // 2 + 1))
                return ready

            def ffn(c, g, hidden, m, n, use, beside=True):
                def tiles(i, first=False):
                    for j in range(2):
                        ci = c.later(i) + 2 * j
                        b = free_bank(g.later(i * 2) + j)
                        if first and j == 0 and beside:
                            project_two((b[:, 0:TOK], b[:, TOK:2 * TOK]), ci, uhi, ulo, stream_pair(m))
                            sum_squares(n)
                            continue
                        start_chunk(ci)
                        project(b[:, 0:TOK], ci, KT, uhi, ulo, ready=stream_pair(m) if first and j == 0 else None)\
                            .then_inc(w_used, 1)
                        start_chunk(ci + 1)
                        project(b[:, TOK:2 * TOK], ci + 1, KT, uhi, ulo).then_inc(w_used, 1)
                        if first and j == 0:
                            sum_squares(n)

                tiles(0, first=True)
                with pe.Fori(1, FT // 2) as i:
                    tiles(i)
                d = c + 2 * FT

                def rows(cd, k, tile, first, last, report):
                    start_chunk(cd)
                    pe.wait_ge(hlo_done, hidden + (k + 1))
                    for n in range(KT):
                        s = slice(n * P, (n + 1) * P)
                        ins = mm3(bank[4 + n // 2][:, (n % 2) * TOK:(n % 2 + 1) * TOK], whi[cd.slot][:, s], wlo[cd.slot][:, s],
                                  tile(hhi), tile(hlo), first and n % 2 == 0, last, skip_group_check=True)
                        if report and n % 2 and n < KT - 1:
                            ins.then_inc(acc_full, 1)
                    ins.then_inc(w_used, 1)

                for k in range(2):
                    rows(d + k, k, lambda t: t[:, k, :], k == 0, False, False)
                with pe.Fori(0, (FT - 2) // 4) as i:
                    for j in range(4):
                        rows((d + (2 + j)).later(i), i * 4 + (2 + j),
                             lambda t: t[:, bass.ds(i * 4 + (2 + j), 1), :].rearrange("p a n -> p (a n)"), False, True, j == 3)

            def turn(src, dst):
                return pe.transpose(dst, src, ident)

            pe.sem_inc(w_used, SLOTS)
            pe.wait_ge(cst_loaded, 16)
            pe.wait_ge(x_loaded, 16)
            xtok = work[:, :, :].rearrange("p (t a) n -> p t (a n)", t=TT)
            for k in range(KT):
                for t in range(TT):
                    ins = turn(xtok[:, t, k * P:(k + 1) * P], bank[4 + k // 2][:, (k % 2) * TOK + t * P:(k % 2) * TOK + (t + 1) * P])
                if k % 2:
                    ins.then_inc(x_tp, 1)
            pe.wait_ge(p_loaded, 16 * len(param_pieces))
            for n in range(4):
                ins = turn(param_rows[:, n, :], bank[3][:, n * P:(n + 1) * P])
            ins.then_inc(par_tp, 1)
            pe.wait_ge(mg_loaded, 16)
            pe.transpose(bank[2][:, 0:KT], mgain_rows[:, :], ident[0:KT, 0:KT]).then_inc(mg_tp, 1)
            pe.wait_ge(m_scaled, TT)
            for k in range(KT):
                if k % 2 == 0:
                    pe.wait_ge(h_ready, k // 2 + 1)
                for t in range(TT):
                    ins = turn(mtok[:, t, k * P:(k + 1) * P], bank[4 + k // 2][:, (k % 2) * TOK + t * P:(k % 2) * TOK + (t + 1) * P])
                if k % 2:
                    ins.then_inc(m_tp, 1)
            pe.wait_ge(cst_loaded, 32)

            with pe.Fori(0, LAYERS) as l:
                c = Chunk(l * (LAYER_C // SLOTS), 0)
                g = Group(l * LAYER_G, 0)
                ffn(c, g, l * (2 * FT), l * 3, l * 6, l * 2)
                c, g = c + FFN_C, g + FFN_G
                pe.wait_ge(m_lo, 4)

                def mem_key(n):
                    b = free_bank(g + n)
                    start_chunk(c + n)
                    project(b[:, 0:TOK], c + n, KT, mhi, mlo).then_inc(w_used, 1)

                mem_key(0)
                sum_squares(l * 6 + 1)
                for n in range(1, 4):
                    mem_key(n)
                for e in range(2):
                    if e == 1:
                        sum_squares(l * 6 + 2)
                    b = free_bank(g + (4 + e))
                    for n in range(2):
                        cn = c + (4 + 2 * e + n)
                        start_chunk(cn)
                        project_tokens(lambda t: b[:, t * TOK:(t + 1) * TOK], cn, 4, mhi[:, 4 * n:4 * n + 4, :],
                                       mlo[:, 4 * n:4 * n + 4, :], half_rows, n == 0, n == 1).then_inc(w_used, 1)

                def mem_query(n, ready=None):
                    b = free_bank(g + (6 + n))
                    start_chunk(c + (8 + n))
                    project(b[:, 0:TOK], c + (8 + n), KT, uhi, ulo, ready=ready).then_inc(w_used, 1)

                mem_query(0, stream_pair(l * 3 + 1))
                pe.wait_ge(f_split, l * 2 + 4)
                for t in range(TT):
                    rows_t = slice(t * P, (t + 1) * P)
                    for k in range(KT):
                        dst = bank[3][:, t * 8:(t + 1) * 8]
                        pe.matmul(dst, uhi[:, k, rows_t], wfhi[:, k, :], start=(k == 0), stop=False)
                        pe.matmul(dst, ulo[:, k, rows_t], wfhi[:, k, :], start=False, stop=False)
                        ins = pe.matmul(dst, uhi[:, k, rows_t], wflo[:, k, :], start=False, stop=(k == KT - 1))
                ins.then_inc(f_full, 1)
                mem_query(1)
                mem_query(2)
                pe.wait_ge(f_ready, l + 1)
                pe.matmul(bank[3][:, 32:40], up_to, flog[:, 0, :], start=True, stop=True)
                pe.matmul(bank[3][:, 40:48], up_to, flog[:, 1, :], start=True, stop=False)
                pe.matmul(bank[3][:, 40:48], ones, flog[:, 0, :], start=False, stop=True)
                pe.matmul(bank[3][0:8, 64:64 + P], flog[:, 0, :], up_to, start=True, stop=True)
                pe.matmul(bank[3][0:8, 64 + P:64 + TOK], flog[:, 1, :], up_to, start=True, stop=False)
                pe.matmul(bank[3][0:8, 64 + P:64 + TOK], flog[:, 0, :], ones, start=False, stop=True).then_inc(c_full, 1)
                mem_query(3)
                with pe.Fori(0, NPAIR) as p:
                    I = l * NPAIR + p
                    cp = (c + 12).later(p * 3)
                    gp = (g + MEM_G).later(p * PAIR_G)

                    def gate(n):
                        b = free_bank(gp + (4 + n))
                        start_chunk(cp + (6 + n))
                        project(b[:, 0:TOK], cp + (6 + n), KT, uhi, ulo).then_inc(w_used, 1)

                    def feature_chunk(n):
                        b = free_bank(gp + n)
                        start_chunk(cp + n)
                        project(b[:, 0:TOK], cp + n, KT, uhi, ulo).then_inc(w_used, 1)

                    def weighted_values(dst, side, w, h):
                        f = slice(h * HD, (h + 1) * HD)
                        v = slice(side * P + h * HD, side * P + (h + 1) * HD)
                        pe.matmul(dst[f, 0:TOK], vpair[:, 0, v], w[:, h, 0:TOK], start=True, stop=False)
                        return pe.matmul(dst[f, P:TOK], vpair[:, 1, v], w[:, h, TOK:CAUSAL], start=False, stop=True)

                    feature_chunk(0)
                    pe.wait_ge(mem_staged, I * 2 + 2)
                    for q in range(TT):
                        ins = pe.matmul(bank[6][:, q * TOK:(q + 1) * TOK], qm1[:, q * P:(q + 1) * P],
                                        kmem[:, bass.ds(p, 1), :].rearrange("p a n -> p (a n)"), start=True, stop=True)
                    ins.then_inc(mem_full, 1)
                    feature_chunk(1)
                    feature_chunk(2)
                    pe.wait_ge(mem_norm, I + 1)
                    for q in range(TT):
                        for k in range(TT):
                            ins = turn(mem_p[:, q * TOK + k * P:q * TOK + (k + 1) * P],
                                       bank[7][:, k * TOK + q * P:k * TOK + (q + 1) * P])
                    ins.then_inc(mem_tp, 1)
                    feature_chunk(3)
                    pe.wait_ge(group_done, gp.count(2 + 2))
                    for h in range(2):
                        f = slice(h * HD, (h + 1) * HD)
                        pe.matmul(bank[2 + h][:, 0:TOK], ks[f, 0:P], qs[f, 0:TOK], start=True, stop=True)
                        ins = pe.matmul(bank[2 + h][:, TOK:CAUSAL], ks[f, P:TOK], qs[f, P:TOK], start=True, stop=True)
                    ins.then_inc(sbz_full, 1)
                    pe.wait_ge(olo_done, I * 3 + 1)
                    for n in range(2):
                        start_chunk(cp + (4 + n))
                        project_tokens(lambda t: bank[5][:, t * TOK:(t + 1) * TOK], cp + (4 + n), 4, uhi[:, 4 * n:4 * n + 4, :],
                                       ulo[:, 4 * n:4 * n + 4, :], half_rows, n == 0, n == 1).then_inc(w_used, 1)
                        if n == 0:
                            pe.wait_ge(mem_pt, I + 1)
                            for k in range(TT):
                                ins = pe.matmul(bank[6][:, 0:TOK], vm1[:, k, :], mem_pT[:, k * TOK:(k + 1) * TOK],
                                                start=(k == 0), stop=(k == TT - 1))
                            ins.then_inc(o_full, 1)
                    gate(0)
                    pe.wait_ge(group_done, gp.count(4 + 2))
                    pe.wait_ge(c_pair, I * 2 + 2)
                    pe.wait_ge(v_taken, I + 1)
                    for h, r in enumerate(contracted):
                        pe.matmul(bank[4 + h][:, 0:P], qx[h][r, 0:P], kx[h][r, 0:P], start=True, stop=True)
                        ins = pe.matmul(bank[4 + h][:, P:CAUSAL], qx[h][r, P:TOK], kx[h][r, 0:TOK], start=True, stop=True)
                    ins.then_inc(fxz_full, 1)
                    gate(1)
                    pe.wait_ge(cst_rounded, l + 1)
                    pe.wait_ge(olo_done, I * 3 + 2)
                    ones_r, later_r = exact_r[:, 0:P], exact_r[:, P:2 * P]
                    for n, (x, ready) in enumerate(((sb_hi, sb_high), (sb_lo, sb_split))):
                        pe.wait_ge(ready, I + 1)
                        for h in range(2):
                            pe.matmul(pair_bank(6)[:, h, :], later_r, x[:, h, 0:TOK], start=(n == 0 and h == 0), stop=False,
                                      skip_group_check=True)
                        pe.matmul(pair_bank(6)[:, :, P:TOK], ones_r, x[:, :, TOK:CAUSAL], start=False, stop=(n == 1),
                                  skip_group_check=True)
                        ins = pe.matmul(last_block, later_r, x[:, :, TOK:CAUSAL], start=(n == 0), stop=(n == 1))
                    ins.then_inc(sb_cum, 1)
                    gate(2)
                    gate(3)
                    pe.wait_ge(fx_norm, I + 1)
                    for h in range(2):
                        for n in range(3):
                            ins = turn(fx_s[:, h, n * P:(n + 1) * P], bank[2 + h][:, n * P:(n + 1) * P])
                    ins.then_inc(fx_tp, 1)
                    gate(4)
                    pe.wait_ge(sb_ready, I + 1)
                    for h in range(2):
                        ins = weighted_values(bank[4], 0, sb_w, h)
                    ins.then_inc(o_full, 1)
                    gate(5)
                    pe.wait_ge(fx_pt, I * 2 + 2)
                    for h in range(2):
                        ins = weighted_values(bank[5], 1, fx_pT, h)
                    ins.then_inc(o_full, 1)
                c, g = c + (12 + 12 * NPAIR), g + (MEM_G + PAIR_G * NPAIR)
                for n in range(4):
                    for at, br in enumerate(BRANCHES):
                        m = 3 * n + at
                        b = free_bank(g + m)
                        start_chunk(c + m)
                        if n == 0:
                            pe.wait_ge(olo_done, l * (3 * NPAIR) + (3 * NPAIR + (at == 2)))
                        heads = slice(4 * br, 4 * br + 4)
                        for t in range(2):
                            ins = project(b[:, t * TOK:(t + 1) * TOK], c + m, 4, hhi[:, heads, :], hlo[:, heads, :], 2 * P, t * P)
                        ins.then_inc(w_used, 1)
                c, g = c + 12, g + 12

                def to_stream(c, xh, xl, ready):
                    place = lambda n: bank[4 + n // 2][:, (n % 2) * TOK:(n % 2 + 1) * TOK]
                    project_two((place(0), place(1)), c, xh, xl, ready)
                    for n in range(2, KT):
                        start_chunk(c + n)
                        project(place(n), c + n, KT, xh, xl).then_inc(w_used, 1)

                def merged_pair(k):
                    if k % 2 == 0:
                        pe.wait_ge(mgl_done, l * 4 + (k // 2 + 1))

                to_stream(c, uhi, ulo, merged_pair)
                c = c + KT
                sum_squares(l * 6 + 3)
                ffn(c, g, l * (2 * FT) + FT, l * 3 + 2, l * 6 + 4, l * 2 + 1)
                sum_squares(l * 6 + 5)

            M2 = 3 * LAYERS
            HID = LAYERS * 2 * FT
            for n in range(3 * KT):
                b = free_bank(Group(g_conv, n))
                start_chunk(c_conv + n)
                project(b[:, 0:TOK], c_conv + n, KT, uhi, ulo, ready=stream_pair(M2) if n == 0 else None).then_inc(w_used, 1)
                if n == 0:
                    sum_squares(n_conv[0])
            to_stream(c_aout, hhi, hlo, lambda k: pe.wait_ge(hlo_done, HID + k + 1))
            ffn(c_ffa, Group(0, g_ffa), HID + KT, M2 + 1, n_ffa[0], 2 * LAYERS, beside=False)
            for n in range(4):
                b = free_bank(Group(0, g_dq + n))
                start_chunk(c_dq + n)
                project(b[:, 0:TOK], c_dq + n, KT, hhi, hlo, ready=stream_pair(M2 + 2) if n == 0 else None).then_inc(w_used, 1)
                if n == 0:
                    sum_squares(n_h2[0])

            def kv(n):
                b = free_bank(Group(0, g_kv + n))
                start_chunk(c_kv + n)
                project(b[:, 0:TOK], c_kv + n, KT, uhi, ulo, ready=stream_pair(M2 + 3) if n == 0 else None).then_inc(w_used, 1)

            kv(0)
            sum_latent(n_q[1], 4)
            kv(1)
            kv(2)
            sum_latent(n_kv[1], 2, 4)

            def swap_halves(n, raw_tile, group):
                pe.wait_ge(group_done, group + 3)
                if n > 0:
                    pe.wait_ge(rp_sin, n)
                pe.matmul(bank[3][:, 0:TOK], swap, raw_tile, start=True, stop=True).then_inc(rp_swap, 1)

            qh, qlo_, kvh, kvl = hhi[:, QLAT, :], hlo[:, QLAT, :], hhi[:, KVLAT, :], hlo[:, KVLAT, :]
            swap_halves(0, kr_raw, g_kv + 2)
            pe.wait_ge(lat_lo, 1)
            for p in range(4):
                b = free_bank(Group(0, g_uqr + p))
                start_chunk(c_uqr + p)
                project(b[:, 0:TOK], c_uqr + p, 4, qh, qlo_).then_inc(w_used, 1)
                if p > 0:
                    swap_halves(p, part((p - 1) % 2), g_uqr + p - 1)

            def mla_scores(h):
                if h >= 2:
                    pe.wait_ge(ls_add, h - 1)
                f = slice((h % 2) * ROPE, (h % 2 + 1) * ROPE)
                for q, (a, n) in enumerate(((0, P), (P, TOK))):
                    dst = bank[2 + h % 2][:, a:a + n]
                    rows = slice(q * P, (q + 1) * P)
                    pe.matmul(dst, qn[:, h, rows], kn[:, h, 0:n], start=True, stop=False)
                    ins = pe.matmul(dst, qr[f, h // 2, rows], kr[f, 0:n], start=False, stop=True)
                ins.then_inc(ls_full, 1)

            def mla_turn(h):
                pe.wait_ge(ls_norm, h + 1)
                for n in range(3):
                    ins = turn(ls(h)[:, n * P:(n + 1) * P], bank[4 + h % 2][:, n * P:(n + 1) * P])
                ins.then_inc(ls_tp, 1)

            def mla_values(h):
                pe.wait_ge(ls_pt, h + 1)
                if h >= 2:
                    pe.wait_ge(la_lo, h - 1)
                b = bank[6 + h % 2]
                pe.matmul(b[:, 0:TOK], vn[:, 0, h, :], lpT(h)[:, 0:TOK], start=True, stop=False)
                pe.matmul(b[:, P:TOK], vn[:, 1, h, :], lpT(h)[:, TOK:CAUSAL], start=False, stop=True).then_inc(la_full, 1)

            both_values = lambda slot, k: slot[:, k * 512:(k + 1) * 512].rearrange("p (h s d) -> p h s d", h=2, s=2)[:, :, 1, :]
            for p in range(7):
                G = g_pairs + 3 * p
                cu = c_pairs + 2 * p
                if p == 0:
                    pe.wait_ge(lat_lo, 2)
                if p < 4:
                    b = free_bank(Group(0, G))
                    start_chunk(cu)
                    for h in range(2):
                        project(b[:, h * TOK:(h + 1) * TOK], cu, 2, kvh, kvl, 512, h * 2 * P)
                    b2 = free_bank(Group(0, G + 1))
                    project_tokens(lambda t: b2[:, t * TOK:(t + 1) * TOK].rearrange("p (h d) -> p h d", h=2), cu, 2, kvh, kvl,
                                   both_values).then_inc(w_used, 1)
                if p == 0:
                    swap_halves(4, part(1), g_uqr + 3)
                if p >= 3:
                    mla_values(2 * p - 6)
                    mla_values(2 * p - 5)
                if 1 <= p <= 4:
                    pe.wait_ge(group_done, G + 2)
                    pe.wait_ge(rp_done, 5)
                    mla_scores(2 * p - 2)
                    mla_scores(2 * p - 1)
                if p < 4:
                    b = free_bank(Group(0, G + 2))
                    start_chunk(cu + 1)
                    for h in range(2):
                        ins = project(b[:, h * TOK:(h + 1) * TOK], cu + 1, 4, qh, qlo_, 2 * P, h * P)
                    ins.then_inc(w_used, 1)
                if 2 <= p <= 5:
                    mla_turn(2 * p - 4)
                    mla_turn(2 * p - 3)
            to_stream(c_o, hhi, hlo, lambda k: pe.wait_ge(la_lo, k + 1))
            ffn(c_ffb, Group(0, g_ffb), HID + KT + FT, M2 + 4, n_ffb[0] - 2, 2 * LAYERS + 1, beside=False)
            for t in range(TT):
                for b in range(2):
                    if t == 0:
                        pe.wait_ge(un_done, LAYERS * 4 + 2 * b + 2)
                    for k in range(4):
                        ins = turn(work[:, 4 * b + k, t * P:(t + 1) * P], bank[4 + 2 * t + b][:, k * P:(k + 1) * P])
                    ins.then_inc(y_tp, 1)
                if t == 0:
                    pe.wait_ge(sq_done, n_fin[1] + 4)
                    for tt in range(TT):
                        for k in range(KT):
                            ins = pe.matmul(bank[2][:, 2 * tt:2 * tt + 2], sq[:, k, tt * P:(tt + 1) * P], ones[:, 0:2],
                                            start=(k == 0), stop=(k == KT - 1))
                    ins.then_inc(ss_full, 1)


def kernel(**inputs):
    from concourse import bacc
    from concourse.bass_utils import run_bass_kernel_spmd

    nc = bacc.Bacc("TRN2", target_bir_lowering=False, num_devices=1)
    arrays, given = {}, {}
    for name, value in inputs.items():
        a = np.ascontiguousarray(value)
        arrays[f"in_{name}"] = a
        given[name] = nc.dram_tensor(f"in_{name}", a.shape, mybir.dt.from_np(a.dtype), kind="ExternalInput").ap()
    arrays["constants"] = constants()
    consts = nc.dram_tensor("constants", (P, C_COLS), F32, kind="ExternalInput").ap()
    out = nc.dram_tensor("out", (1, TOK, DM), F32, kind="ExternalOutput").ap()
    program(nc, given, consts, out)
    r = run_bass_kernel_spmd(nc, [arrays], core_ids=[0])
    return r.results[0]["out"]
```
